# Optimizing a Trainium2 kernel written in Bass

```python
import math
import jax, jax.numpy as jnp
from jax import lax
import numpy as np

D_MODEL = 2048
BATCH = 1
SEQ = 256
DEPTH = 1

CHUNK = 64

MIX_WIDTH = D_MODEL
CONV_CH = MIX_WIDTH // 2
SSM_CH = MIX_WIDTH - CONV_CH
CONV_WIDTH = 31
SSM_GROUP_WIDTH = 16
SSM_GROUPS = SSM_CH // SSM_GROUP_WIDTH
SSM_STATE = 64
IN_COLS = 2 * CONV_CH + 2 * SSM_CH

N_GROUPS = 4
EXPERTS_PER_GROUP = 8
TOP_K = 2
D_EXPERT = 512

EPS = 1e-6

kernel_name = 'hymba_conformer_s5_hmoe_trunk'

def rms_norm(x, g):
    xf = x.astype(jnp.float32)
    y = xf * lax.rsqrt(jnp.mean(xf * xf, axis=-1, keepdims=True) + EPS)
    return (y * g.astype(jnp.float32)).astype(x.dtype)

def layer_norm(x, g, b):
    xf = x.astype(jnp.float32)
    mu = jnp.mean(xf, axis=-1, keepdims=True)
    var = jnp.mean(jnp.square(xf - mu), axis=-1, keepdims=True)
    y = (xf - mu) * lax.rsqrt(var + EPS)
    return (y * g.astype(jnp.float32) + b.astype(jnp.float32)).astype(x.dtype)

def modulate(h, shift, scale):
    return h * (1.0 + scale[:, None, :]) + shift[:, None, :]

def conformer_conv(val, gate, dw_w, dw_b, ln_g, ln_b):
    z = val * jax.nn.sigmoid(gate)
    z = lax.conv_general_dilated(
        z, dw_w[:, None, :].astype(z.dtype), window_strides=(1,),
        padding=[(CONV_WIDTH - 1, 0)],
        dimension_numbers=('NWC', 'WIO', 'NWC'),
        feature_group_count=CONV_CH) + dw_b
    z = layer_norm(z, ln_g, ln_b)
    return jax.nn.silu(z)

def s5_ssm(u, gate, a_re, a_im, b_re, b_im, c_re, c_im, d_skip, log_dt):
    dtype = u.dtype
    bsz, seq, _ = u.shape
    f32 = jnp.float32
    uf = u.astype(f32).reshape(bsz, seq, SSM_GROUPS, SSM_GROUP_WIDTH)
    dt = jnp.exp(log_dt.astype(f32))[:, None]
    lr, li = a_re.astype(f32), a_im.astype(f32)
    mag = jnp.exp(lr * dt)
    ang = li * dt
    abar_re, abar_im = mag * jnp.cos(ang), mag * jnp.sin(ang)
    den = lr * lr + li * li
    nr, ni = abar_re - 1.0, abar_im
    f_re = (nr * lr + ni * li) / den
    f_im = (ni * lr - nr * li) / den
    br, bi = b_re.astype(f32), b_im.astype(f32)
    bb_re = f_re[..., None] * br - f_im[..., None] * bi
    bb_im = f_re[..., None] * bi + f_im[..., None] * br
    bu_re = jnp.einsum('blgh,gph->blgp', uf, bb_re)
    bu_im = jnp.einsum('blgh,gph->blgp', uf, bb_im)
    a_seq_re = jnp.broadcast_to(abar_re, (1, seq, SSM_GROUPS, SSM_STATE))
    a_seq_im = jnp.broadcast_to(abar_im, (1, seq, SSM_GROUPS, SSM_STATE))

    def combine(e1, e2):
        a1r, a1i, b1r, b1i = e1
        a2r, a2i, b2r, b2i = e2
        ar = a1r * a2r - a1i * a2i
        ai = a1r * a2i + a1i * a2r
        brr = a2r * b1r - a2i * b1i + b2r
        bii = a2r * b1i + a2i * b1r + b2i
        return (ar, ai, brr, bii)

    _, _, s_re, s_im = lax.associative_scan(combine, (a_seq_re, a_seq_im, bu_re, bu_im), axis=1)
    y = (jnp.einsum('blgp,ghp->blgh', s_re, c_re.astype(f32))
         - jnp.einsum('blgp,ghp->blgh', s_im, c_im.astype(f32)))
    y = y + uf * d_skip.astype(f32).reshape(SSM_GROUPS, SSM_GROUP_WIDTH)
    y = y.reshape(bsz, seq, SSM_CH)
    return (jax.nn.gelu(y) * jax.nn.sigmoid(gate.astype(f32))).astype(dtype)

def hier_moe(h, rg_w, rg_b, re_w, re_b, w_gate, w_up, w_down):
    bsz, seq, d = h.shape
    f32 = jnp.float32
    t = h.reshape(bsz * seq, d)
    g_logits = (t @ rg_w + rg_b).astype(f32)
    g_prob = jax.nn.softmax(g_logits, axis=-1)
    g_idx = jnp.argmax(g_logits, axis=-1)
    g_w = jnp.take_along_axis(g_prob, g_idx[:, None], axis=-1)
    e_logits = (jnp.einsum('td,gde->tge', t, re_w) + re_b).astype(f32)
    e_sel = jnp.take_along_axis(e_logits, g_idx[:, None, None], axis=1)[:, 0]
    top_v, top_i = lax.top_k(e_sel, TOP_K)
    top_w = jax.nn.softmax(top_v, axis=-1) * g_w
    e_w = jnp.sum(jax.nn.one_hot(top_i, EXPERTS_PER_GROUP, dtype=f32) * top_w[..., None], axis=1)
    comb = (jax.nn.one_hot(g_idx, N_GROUPS, dtype=f32)[:, :, None] * e_w[:, None, :]).astype(t.dtype)
    y = jnp.zeros_like(t)
    for g in range(N_GROUPS):
        a = jnp.einsum('td,edf->tef', t, w_gate[g])
        u = jnp.einsum('td,edf->tef', t, w_up[g])
        hm = jax.nn.silu(a) * u * comb[:, g, :, None]
        y = y + jnp.einsum('tef,efd->td', hm, w_down[g])
    return y.reshape(bsz, seq, d)

def setup_inputs(seed: int = 0) -> dict:
    key = jax.random.key(seed)
    ks = jax.random.split(key, 32)
    f32 = jnp.float32
    L, D = DEPTH, D_MODEL
    nrm = lambda k, shape, s: jax.random.normal(k, shape, f32) * s
    gain = lambda k, shape: 1.0 + 0.02 * jax.random.normal(k, shape, f32)
    n_idx = jnp.arange(SSM_STATE, dtype=f32)
    a_re = -0.5 + 0.01 * jax.random.normal(ks[10], (L, SSM_GROUPS, SSM_STATE), f32)
    a_im = math.pi * n_idx + 0.01 * jax.random.normal(ks[11], (L, SSM_GROUPS, SSM_STATE), f32)
    log_dt = jax.random.uniform(ks[18], (L, SSM_GROUPS), f32, math.log(1e-3), math.log(1e-1))
    return {
        'x': jax.random.normal(ks[0], (BATCH, SEQ, D), f32),
        'c': jax.random.normal(ks[1], (BATCH, D), f32),
        'w_ada': nrm(ks[2], (L, D, 6 * D), 0.5 * D ** -0.5),
        'b_ada': nrm(ks[3], (L, 6 * D), 0.02),
        'norm1_g': gain(ks[4], (L, D)),
        'w_in': nrm(ks[5], (L, D, IN_COLS), D ** -0.5),
        'conv_w': nrm(ks[6], (L, CONV_WIDTH, CONV_CH), CONV_WIDTH ** -0.5),
        'conv_b': nrm(ks[7], (L, CONV_CH), 0.02),
        'conv_ln_g': gain(ks[8], (L, CONV_CH)),
        'conv_ln_b': nrm(ks[9], (L, CONV_CH), 0.02),
        'ssm_a_re': a_re,
        'ssm_a_im': a_im,
        'ssm_b_re': nrm(ks[12], (L, SSM_GROUPS, SSM_STATE, SSM_GROUP_WIDTH), (2 * SSM_GROUP_WIDTH) ** -0.5),
        'ssm_b_im': nrm(ks[13], (L, SSM_GROUPS, SSM_STATE, SSM_GROUP_WIDTH), (2 * SSM_GROUP_WIDTH) ** -0.5),
        'ssm_c_re': nrm(ks[14], (L, SSM_GROUPS, SSM_GROUP_WIDTH, SSM_STATE), (2 * SSM_STATE) ** -0.5),
        'ssm_c_im': nrm(ks[15], (L, SSM_GROUPS, SSM_GROUP_WIDTH, SSM_STATE), (2 * SSM_STATE) ** -0.5),
        'ssm_d': nrm(ks[16], (L, SSM_CH), 1.0),
        'ssm_log_dt': log_dt,
        'out_norm_conv_g': gain(ks[17], (L, CONV_CH)),
        'out_norm_ssm_g': gain(ks[19], (L, SSM_CH)),
        'w_out': nrm(ks[20], (L, MIX_WIDTH, D), MIX_WIDTH ** -0.5),
        'norm2_g': gain(ks[21], (L, D)),
        'router_group_w': nrm(ks[22], (L, D, N_GROUPS), D ** -0.5),
        'router_group_b': nrm(ks[23], (L, N_GROUPS), 0.01),
        'router_expert_w': nrm(ks[24], (L, N_GROUPS, D, EXPERTS_PER_GROUP), D ** -0.5),
        'router_expert_b': nrm(ks[25], (L, N_GROUPS, EXPERTS_PER_GROUP), 0.01),
        'exp_w_gate': nrm(ks[26], (L, N_GROUPS, EXPERTS_PER_GROUP, D, D_EXPERT), D ** -0.5),
        'exp_w_up': nrm(ks[27], (L, N_GROUPS, EXPERTS_PER_GROUP, D, D_EXPERT), D ** -0.5),
        'exp_w_down': nrm(ks[28], (L, N_GROUPS, EXPERTS_PER_GROUP, D_EXPERT, D), D_EXPERT ** -0.5),
        'final_norm_g': gain(ks[29], (D,)),
    }

def reference(x, c, w_ada, b_ada, norm1_g, w_in, conv_w, conv_b, conv_ln_g, conv_ln_b,
              ssm_a_re, ssm_a_im, ssm_b_re, ssm_b_im, ssm_c_re, ssm_c_im, ssm_d, ssm_log_dt,
              out_norm_conv_g, out_norm_ssm_g, w_out, norm2_g,
              router_group_w, router_group_b, router_expert_w, router_expert_b,
              exp_w_gate, exp_w_up, exp_w_down, final_norm_g):
    c_act = jax.nn.silu(c)
    for l in range(DEPTH):
        mod = c_act @ w_ada[l] + b_ada[l]
        shift1, scale1, gate1, shift2, scale2, gate2 = jnp.split(mod, 6, axis=-1)

        h = modulate(rms_norm(x, norm1_g[l]), shift1, scale1)
        p = h @ w_in[l]
        o = 0
        conv_val = p[..., o:o + CONV_CH]; o += CONV_CH
        conv_gate = p[..., o:o + CONV_CH]; o += CONV_CH
        ssm_in = p[..., o:o + SSM_CH]; o += SSM_CH
        ssm_gate = p[..., o:o + SSM_CH]
        y_conv = conformer_conv(conv_val, conv_gate, conv_w[l], conv_b[l], conv_ln_g[l], conv_ln_b[l])
        y_ssm = s5_ssm(ssm_in, ssm_gate, ssm_a_re[l], ssm_a_im[l], ssm_b_re[l], ssm_b_im[l],
                       ssm_c_re[l], ssm_c_im[l], ssm_d[l], ssm_log_dt[l])
        y = jnp.concatenate([rms_norm(y_conv, out_norm_conv_g[l]),
                             rms_norm(y_ssm, out_norm_ssm_g[l])], axis=-1) @ w_out[l]
        x = x + gate1[:, None, :] * y

        h = modulate(rms_norm(x, norm2_g[l]), shift2, scale2)
        y = hier_moe(h, router_group_w[l], router_group_b[l], router_expert_w[l], router_expert_b[l],
                     exp_w_gate[l], exp_w_up[l], exp_w_down[l])
        x = x + gate2[:, None, :] * y
    return rms_norm(x, final_norm_g)


_drawn_inputs = setup_inputs


def setup_inputs(seed=0):
    import zlib

    import numpy as np

    out = dict(_drawn_inputs(seed))
    spreads = {}
    factors = {'norm1_g': 4.998,
     'conv_b': 4.071,
     'conv_ln_g': 5.516,
     'conv_ln_b': 8.0,
     'ssm_a_re': 64.0,
     'ssm_a_im': 3.22,
     'ssm_b_re': 16.407,
     'ssm_b_im': 24.891,
     'ssm_c_re': 4.102,
     'ssm_c_im': 3.747,
     'ssm_log_dt': 3.367,
     'out_norm_conv_g': 6.849,
     'out_norm_ssm_g': 5.464,
     'norm2_g': 3.822,
     'router_group_b': 7.467,
     'router_expert_b': 6.633,
     'final_norm_g': 8.095}
    for name, (base, spread) in spreads.items():
        noise = np.random.default_rng([zlib.crc32(name.encode()), seed]).standard_normal(out[name].shape)
        drawn = base * np.exp(spread * noise) if base else spread * noise
        out[name] = __import__('jax').numpy.asarray(drawn.astype(out[name].dtype))
    for name, factor in factors.items():
        out[name] = (out[name] * factor).astype(out[name].dtype)
    return out
```

```python
import math
from contextlib import ExitStack

import concourse.bass as bass
from concourse import mybir

ALU = mybir.AluOpType
ACT = mybir.ActivationFunctionType
AX = mybir.AxisListType
F32 = mybir.dt.float32
I32 = mybir.dt.int32
U32 = mybir.dt.uint32

P = 128
D = 2048
T = 256
TT = T // P
KD = D // P
CH = 1024
CT_ = CH // P
TAPS = 31
PAD = TAPS - 1
G, HG, S = 64, 16, 64
PAIRS = G // 2
QUADS = PAIRS // 4
HALF = T // 2
NG, NE, F = 4, 8, 512
EXP = NG * NE
SLOTS = 64
BE = 4
NB = EXP // BE
JOBS = (T // SLOTS) * NB
N = 512
EPS = 1e-6
MAGIC = 1.5 * 2.0 ** 23
TWO_PI_DOWN = 6.283185
PI_DOWN = 3.1415925
C1 = 6.28125
C2 = 0.0019350051879882812
C3 = 2 * math.pi - C1 - C2

RING = 12
UNIT = 2048
A_UNITS, B_UNITS, C_UNITS, D_UNITS = 32, 96, 16, 48
B_ORDER = [8, 9, 10, 11, 0, 1, 2, 3, 4, 5, 6, 7]


def ring_use(n):
    if n < A_UNITS:
        return n % 8, n // 8
    r, s = divmod(n - A_UNITS, RING)
    s = B_ORDER[s]
    return s, r + (4 if s < 8 else 0)


D_BASE = A_UNITS + B_UNITS + C_UNITS
D_USES = [13 if s < 8 else 10 for s in range(RING)]

CHUNKS = [(2048, "u"), (2560, "u"), (1024, "gate"), (0, "value"), (1536, "gate"), (512, "value"),
          (3072, "out_gate"), (3584, "out_gate")]
TURNED = {0: 0, 1: 4, 3: 0, 5: 4, 6: 0, 7: 4}
ADA_PARTS = [2, 3, 4, 5]


def side_jobs(g):
    jobs = []
    chunk, j = g // 4 - 1, g % 4
    if chunk in TURNED:
        jobs.append(("turn", chunk, j))
    if g >= 5 and (g - 5) % 2 == 0 and (g - 5) // 2 < QUADS:
        jobs.append(("drive", (g - 5) // 2))
    if g >= 8 and (g - 8) % 2 == 0 and (g - 8) // 2 < QUADS:
        jobs.append(("read", (g - 8) // 2))
    return jobs


SIDE = [j for g in range(36) for j in side_jobs(g) if j[0] != "drive"]


def side_number(job):
    return SIDE.index(job)


def trunk(nc, a, out):
    ctx = ExitStack()
    with ctx:
        def sb(name, shape, dt=F32):
            return ctx.enter_context(nc.sbuf_tensor(name, shape, dt))

        def sem(name):
            return ctx.enter_context(nc.semaphore(name))

        ring = sb("ring", [P, RING, UNIT])
        KB = 256
        arena = sb("arena", [P, 122 * KB])

        def at(kb, words, parts=P):
            o = int(kb * KB)
            return arena[0:parts, o:o + words]

        hT = at(0, 16 * KB).rearrange("p (k t) -> p k t", k=KD)
        cosT = at(16, 16 * KB).rearrange("p (q t) -> p q t", q=PAIRS)
        sinT = at(32, 16 * KB).rearrange("p (q t) -> p q t", q=PAIRS)
        uT = at(48, 8 * KB).rearrange("p (c t) -> p c t", c=CT_)
        zT = at(56, CT_ * (PAD + T)).rearrange("p (c t) -> p c t", c=CT_)
        rot = at(66, 32 * KB).rearrange("p (b w r t) -> p b w r t", b=2, w=2, r=4)
        driveT = at(98, 8 * KB).rearrange("p (c q s) -> p c q s", c=2, q=QUADS)
        readT = at(106, 8 * KB).rearrange("p (c q s) -> p c q s", c=2, q=QUADS)
        rows = at(114, 8 * KB).rearrange("p (b t n) -> p b t n", b=2, t=TT)
        sgT = at(98, 8 * KB).rearrange("p (c t) -> p c t", c=CT_)
        xr = at(66, 16 * KB).rearrange("p (t d) -> p t d", t=TT)
        bst = at(82, 16 * KB, 32).rearrange("p (c s) -> p c s", c=2)
        cst = at(48, 4 * KB).rearrange("p (c q s) -> p c q s", c=2, q=QUADS)
        cexp = at(52, 8 * KB).rearrange("p (c q g s) -> p c q g s", c=2, q=QUADS, g=2)
        cwst = at(60, 4 * KB, TAPS + 1)
        vst = at(64, P, 40)
        prm = at(98, 20 * P, 32).rearrange("p (n s) -> p n s", n=20)
        btmp = at(108, 4 * KB).rearrange("p (n f) -> p n f", n=2)
        bdiag = at(114, 8 * KB).rearrange("p (c r g h) -> p c r g h", c=2, r=PAIRS, g=2)
        conv = at(16, 8 * KB).rearrange("p (c t) -> p c t", c=CT_)
        sq = at(24, 8 * KB).rearrange("p (c t) -> p c t", c=CT_)
        stat = at(40, 4 * T).rearrange("p (n t) -> p n t", n=4)
        x1 = at(66, 16 * KB).rearrange("p (t d) -> p t d", t=TT)
        gate1 = at(82, 8 * KB)
        gtmp = at(90, 4 * KB).rearrange("p (b n) -> p b n", b=2)
        xn = at(0, 16 * KB).rearrange("p (t d) -> p t d", t=TT)
        xT = at(16, 16 * KB).rearrange("p (k t) -> p k t", k=KD)
        acc = at(32, 16 * KB).rearrange("p (t d) -> p t d", t=TT)
        yexp = at(48, 8 * KB).rearrange("p (n c) -> p n c", n=4)
        silu = at(56, 2 * KB)
        hid = at(58, 2 * KB)
        hidT = at(60, 2 * KB).rearrange("p (j s) -> p j s", j=4)
        pick = at(62, 2 * KB).rearrange("p (t s) -> p t s", t=TT)
        wpick = at(64, 2 * KB).rearrange("p (t s) -> p t s", t=TT)
        wpickT = at(90, 2 * KB).rearrange("p (r t) -> p r t", r=2)
        gate2 = at(98, 8 * KB)
        fgain = at(106, 8 * KB)
        junk = at(16, 8 * KB)

        ident = sb("ident", [P, P])
        iota = sb("iota", [P, SLOTS])
        ccol = sb("ccol", [P, KD])
        g1 = sb("g1", [P, KD])
        g2 = sb("g2", [P, KD])
        mod = sb("mod", [P, 6, KD])
        modrow = sb("modrow", [P, N])
        ss = sb("ss", [P, 8])
        rstd = sb("rstd", [P, 4])
        ldt = sb("ldt", [32, 2])
        dt = sb("dt", [32, 2])
        decay = sb("decay", [P, PAIRS])
        rot128 = sb("rot128", [P, 2, PAIRS])
        carry = sb("carry", [P, 3, 4, 2])
        vT = sb("vT", [P, 5, CT_])
        skip = sb("skip", [P, P])
        rbias = sb("rbias", [NG + EXP, 1])
        halfpi = sb("halfpi", [P, 1])
        eps = sb("eps", [P, 1])
        odd = sb("odd", [P, 2])
        cwT = at(65, 256).rearrange("p (c t) -> p c t", c=CT_)
        bada = at(64.5, 6 * KD).rearrange("p (m k) -> p m k", m=6)
        par = at(112, 4 * PAIRS).rearrange("p (n q) -> p n q", n=4)
        iota_i = at(112.5, P).bitcast(I32)
        steps = at(113, HALF)
        part_i = at(113.5, 1).bitcast(I32)
        place = [int(94 * KB)]

        def small(shape, dt_=F32, parts=P):
            words = math.prod(shape)
            v = arena[0:parts, place[0]:place[0] + words]
            place[0] += words
            if dt_ != F32:
                v = v.bitcast(dt_)
            if len(shape) == 2:
                v = v.rearrange("p (a b) -> p a b", a=shape[0])
            if len(shape) == 3:
                v = v.rearrange("p (a b c) -> p a b c", a=shape[0], b=shape[1])
            return v

        before = small([P])
        ones = small([P])
        mean_w = small([P])
        lgT = small([T], parts=NG + EXP)
        sel = small([TT, 3, EXP])
        comb = small([TT, EXP])
        assert place[0] <= 98 * KB
        place = [int(92 * KB)]
        lg = small([TT, NG + EXP])
        gp = small([TT, 8])
        top = small([TT, 8])
        topi = small([TT, 8], U32)
        etop = small([TT, 8])
        etopi = small([TT, 8], U32)
        rt = small([TT, 16])
        rank = small([TT, EXP])
        rankc = small([TT, BE])
        counts = small([EXP])
        assert place[0] <= 94 * KB
        bada2 = at(45, 6 * KD).rearrange("p (m k) -> p m k", m=6)
        wr = at(114, KD * (NG + EXP)).rearrange("p (k e) -> p k e", k=KD)
        wrg = at(117, KD * NG).rearrange("p (k g) -> p k g", k=KD)
        wre = at(118, NG * KD * NE).rearrange("p (g k e) -> p g k e", g=NG, k=KD)
        jm = at(118, JOBS * JOBS).rearrange("p (j x) -> p j x", j=JOBS)
        jb = at(114, 6 * JOBS).rearrange("p (j x) -> p j x", j=6)
        jobtab = at(116, 2 * JOBS).rearrange("p (j x) -> p j x", j=2)
        jobi = at(116.5, JOBS, 1).bitcast(I32)
        jobn = at(117, 1, 1).bitcast(I32)

        ps = ctx.enter_context(nc.psum_tensor("ps", [P, 8, N], F32))

        mod_dram = nc.dram_tensor("mod_scratch", [6, D], F32, kind="Internal").ap()
        gate_dram = nc.dram_tensor("gate_scratch", [2, D], F32, kind="Internal").ap()

        landed = [sem(f"unit_landed_{s}") for s in range(RING)]
        consumed = sem("units_consumed")
        x_landed = sem("x_landed")
        c_landed = sem("c_landed")
        setup_landed = sem("setup_landed")
        bada_landed = sem("ada_bias_landed")
        wr_landed = sem("router_weights_landed")
        late_landed = sem("late_setup_landed")
        consts_ready = sem("constants_ready")
        blocks_zero = sem("b_blocks_zeroed")
        sum_consts = sem("sum_constants_ready")
        pool_order = sem("pool_order")
        vec_order = sem("vector_order")
        act_order = sem("scalar_order")
        x_squares = sem("x_squares")
        x_var = sem("x_variance")
        x_root = sem("x_root")
        x_rstd = sem("x_rstd")
        x_normed = sem("x_normed")
        x_turned = sem("x_turned")
        x_stored = sem("x_transposes_stored")
        c_silu = sem("c_silu")
        dt_ready = sem("dt_ready")
        decay_in = sem("decay_exponent_ready")
        decay_ready = sem("decay_ready")
        angle_in = sem("angle_reduced")
        angle_ready = sem("angle_sin_cos")
        params_ready = sem("ssm_params_ready")
        b_turned = sem("b_turned")
        cw_turned = sem("conv_weights_turned")
        cw_stored = sem("conv_weights_stored")
        params_turned = sem("ssm_params_turned")
        params_stored = sem("ssm_params_stored")
        bdiag_ready = sem("b_blocks_ready")
        cexp_ready = sem("c_blocks_ready")
        bc_turned = sem("b_c_blocks_turned")
        bc_stored = sem("b_c_blocks_stored")
        phase_ready = sem("table_phase_ready")
        table_sin = sem("table_sin_done")
        table_abs = sem("table_abs_done")
        tables_ready = sem("tables_ready")
        ada_done = sem("ada_part_done")
        ada_copied = sem("ada_part_copied")
        mod_stored = sem("mod_row_in_dram")
        mod_landed = sem("mod_columns_landed")
        h_scaled = sem("h_scaled")
        h_ready = sem("h_ready")
        chunk_done = sem("chunk_done")
        rows_ready = sem("rows_ready")
        z_ready = sem("z_rows_ready")
        side_done = sem("side_bank_done")
        side_stored = sem("side_bank_stored")
        pads_ready = sem("conv_pads_ready")
        drive_done = sem("drive_done")
        drive_read = sem("drive_read")
        states_ready = sem("states_ready")
        skip_ready = sem("skip_diagonal_ready")
        conv_step = sem("conv_step")
        gated = sem("ssm_gated")
        squares = sem("squares_ready")
        sums = sem("sums_done")
        rooted = sem("roots_ready")
        centred = sem("conv_centred")
        scaled = sem("conv_scaled")
        swished = sem("conv_swished")
        ys_ready = sem("ssm_normed")
        yc_ready = sem("conv_normed")
        gate_added = sem("gate_bias_added")
        gate_stored = sem("gate_in_dram")
        gate_landed = sem("gate_landed")
        gain_landed = sem("final_gain_landed")
        x_again = sem("x_landed_again")
        out_done = sem("out_chunk_done")
        x1_ready = sem("x1_chunk_ready")
        x1_squares = sem("x1_squares")
        n2_var = sem("norm2_variance")
        n2_root = sem("norm2_root")
        n2_rstd = sem("norm2_rstd")
        xn_ready = [sem(f"xn_ready_{t}") for t in range(TT)]
        xn_turned = sem("xn_turned")
        h2_even = sem("h2_even_stored")
        h2_odd = sem("h2_odd_stored")
        wr_ready = sem("router_weights_packed")
        logits_done = sem("logits_done")
        logits_biased = sem("logits_biased")
        logits_turned = sem("logits_turned")
        exp_in = sem("router_exp_in")
        exp_done = sem("router_exp_done")
        sel_ready = sem("selection_ready")
        rank_done = sem("rank_done")
        counts_ready = sem("counts_ready")
        jobs_ready = sem("jobs_ready")
        job_order = sem("vector_job_order")
        picks_ready = sem("picks_ready")
        gathered = sem("tokens_gathered")
        tok_even = sem("tokens_even_stored")
        tok_odd = sem("tokens_odd_stored")
        picks_turned = sem("picks_turned")
        scatter_ready = sem("scatter_ready")
        gate_done = sem("expert_gate_done")
        gate_silu = sem("expert_gate_silu")
        up_done = sem("expert_up_done")
        hidden_ready = sem("hidden_ready")
        hidden_turned = sem("hidden_turned")
        hidden_stored = sem("hidden_stored")
        down_done = sem("down_done")
        down_stored = sem("down_stored")
        combined = sem("combined")
        added = sem("added")
        fin_order = sem("final_order")
        fin_sq_in = sem("final_sum_ready")
        fin_sq = sem("final_squares")
        fin_var = sem("final_variance")
        fin_root = sem("final_root")
        fin_out = sem("final_rows_ready")
        out_landed = sem("out_landed")

        w_ada = a["w_ada"][0].rearrange("(p k) n -> k p n", k=KD)
        w_in = a["w_in"][0].rearrange("(p k) n -> p k n", k=KD)
        w_out = a["w_out"][0].rearrange("(k p) n -> p k n", p=P)
        w_gate = a["exp_w_gate"][0].rearrange("g e (p k) f -> (g e) p (k f)", k=KD)
        w_up = a["exp_w_up"][0].rearrange("g e (p k) f -> (g e) p (k f)", k=KD)
        w_down = a["exp_w_down"][0].rearrange("g e (j p) n -> (g e) p j n", p=P)

        def col(v):
            return v.rearrange("(p k) -> p k", k=KD)

        def b_unit(n):
            it, s = divmod(n, RING)
            u, kind = divmod(s, 3)
            if kind == 0:
                return ("in", it, u)
            m = it * 8 + 2 * u + kind - 1
            return ("ada", m // KD, m % KD)

        C_ORDER = [(n, q) for n in range(3) for q in (2, 3)] + [(n, q) for n in range(3) for q in (0, 1)] \
            + [(3, q) for q in (2, 3, 0, 1)]
        OUT_BANKS = [(0, 1), (4, 5), (2, 3), (0, 1)]

        block = ctx.enter_context(nc.Block())

        @block.sync
        def _(sp):
            sp.dma_start(xr[:, 0, :], a["x"][0, 0:P, :]).then_inc(x_landed, 16)
            sp.dma_start(xr[:, 1, :], a["x"][0, P:T, :]).then_inc(x_landed, 16)
            last_user = {}

            def start(n, s, dst, src):
                if s in last_user:
                    sp.wait_ge(consumed, last_user[s] + 1)
                last_user[s] = n
                sp.dma_start(dst, src).then_inc(landed[s], 16)

            for n in range(A_UNITS):
                s, _u = ring_use(n)
                part, k = (1, 0)[n // KD], n % KD
                start(n, s, ring[:, s, :], w_ada[k, :, part * D:(part + 1) * D])
            for m in range(B_UNITS):
                n = A_UNITS + m
                s, _u = ring_use(n)
                kind, i, k = b_unit(m)
                if kind == "in":
                    c0 = CHUNKS[i][0]
                    start(n, s, ring[:, s, :].rearrange("p (k n) -> p k n", k=4),
                          w_in[:, 4 * k:4 * k + 4, c0:c0 + N])
                else:
                    c0 = ADA_PARTS[i] * D
                    start(n, s, ring[:, s, :], w_ada[k, :, c0:c0 + D])
            sp.wait_ge(side_done, side_number(("read", QUADS - 1)) + 1)
            sp.dma_start(x1, a["x"][0].rearrange("(t p) d -> p t d", p=P)).then_inc(x_again, 16)
            for m in range(C_UNITS):
                n = A_UNITS + B_UNITS + m
                s, _u = ring_use(n)
                c, q = C_ORDER[m]
                start(n, s, ring[:, s, :].rearrange("p (k n) -> p k n", k=4),
                      w_out[:, 4 * q:4 * q + 4, c * N:(c + 1) * N])

            def job_units(j, e0):
                m = 0
                for pr in range(2):
                    for stage in range(3):
                        for u in range(4):
                            for x in range(2):
                                s = m % RING
                                e = e0 + (2 * pr + x)
                                sp.wait_ge(consumed, j * D_UNITS + (D_BASE + m - RING + 1))
                                if stage < 2:
                                    w = (w_gate, w_up)[stage]
                                    src = w[bass.ds(e, 1), :, u * UNIT:(u + 1) * UNIT].rearrange("e p n -> (e p) n")
                                    dst = ring[:, s, :]
                                else:
                                    src = w_down[bass.ds(e, 1), :, :, u * N:(u + 1) * N].rearrange("e p j n -> (e p) j n")
                                    dst = ring[:, s, :].rearrange("p (j n) -> p j n", j=4)
                                sp.dma_start(dst, src).then_inc(landed[s], 16)
                                m += 1

            with sp.Fori(0, NB) as j:
                job_units(j, j * BE)
            sp.wait_ge(jobs_ready, 1)
            n_jobs = sp.value_load(jobn[0:1, 0:1], min_val=NB, max_val=JOBS)
            with sp.If(n_jobs > NB):
                with sp.Fori(NB, n_jobs) as j:
                    e0 = sp.value_load(jobi[0:1, bass.ds(j, 1)], min_val=0, max_val=EXP - BE)
                    job_units(j, e0)
            for t in range(TT):
                sp.wait_ge(fin_out, t + 1)
                sp.dma_start(out[0, t * P:(t + 1) * P, :], acc[:, t, :]).then_inc(out_landed, 16)
            sp.wait_ge(out_landed, 16 * TT)

        @block.tensor
        def _(pe):
            mm = nc.tensor.matmul

            def tr(dst, src, k):
                return nc.tensor.transpose(dst, src, ident[0:k, 0:k])

            pe.wait_ge(consts_ready, 1)
            pe.wait_ge(setup_landed, 16 * 14)
            for c in range(CT_):
                tr(ps[:, 2, c * 32:(c + 1) * 32], cwst[:, c * P:(c + 1) * P], 32)
            tr(ps[:, 2, 256:296], vst, 40).then_inc(cw_turned, 1)
            for b in range(8):
                for k in (2 * b, 2 * b + 1):
                    for t in range(TT):
                        pe.wait_ge(x_normed, t + 1)
                        if b >= 4:
                            pe.wait_ge(x_stored, b - 3)
                        o = (k % 2) * T + t * P
                        last = tr(ps[:, 4 + b % 4, o:o + P], xr[:, t, k:D:KD], P)
                last.then_inc(x_turned, 1)

            def ada_unit(n, bank, k):
                s, u = ring_use(n)
                pe.wait_ge(landed[s], 16 * (u + 1))
                for j in range(4):
                    last = mm(ps[32 * j:32 * j + 32, bank, :], ccol[:, k:k + 1].to_broadcast([P, 32]), ring[:, s, j * N:(j + 1) * N],
                              start=(k == 0), stop=(k == KD - 1), skip_group_check=True)
                return last

            pe.wait_ge(c_silu, 1)
            for k in range(KD):
                ada_unit(k, 0, k).then_inc(consumed, 1)
            pe.drain().then_inc(ada_done, 1)
            pe.wait_ge(x_stored, 8)
            for c in range(2):
                for h in range(HG):
                    last = tr(ps[:, 4 + c, h * 32:(h + 1) * 32],
                              bst[:, c, :].rearrange("p (s h) -> p h s", h=HG)[:, h, :], 32)
            last.then_inc(b_turned, 1)
            pe.wait_ge(params_ready, 1)
            for i, slot in enumerate((6, 10, 15, 16)):
                last = tr(ps[:, 3, i * 32:(i + 1) * 32], prm[:, slot, :], 32)
            last.then_inc(params_turned, 1)
            for k in range(KD):
                ada_unit(KD + k, 1, k).then_inc(consumed, 1)
            pe.drain().then_inc(ada_done, 1)
            pe.wait_ge(bdiag_ready, 1)
            pe.wait_ge(cexp_ready, 1)
            for b in range(8):
                for q in range(4):
                    c, qq = (b % 4) // 2, (b % 2) * 4 + q
                    if b < 4:
                        src = bdiag[:, c, :, :, :].rearrange("p r g h -> p (r g h)")[:, qq * P:(qq + 1) * P]
                    else:
                        src = cexp[:, c, qq, :, :].rearrange("p g s -> p (g s)")
                    if b >= 4:
                        pe.wait_ge(bc_stored, b - 3)
                    last = tr(ps[:, 4 + b % 4, q * P:(q + 1) * P], src, P)
                last.then_inc(bc_turned, 1)

            def side(g):
                for job in side_jobs(g):
                    if job[0] == "drive":
                        q = job[1]
                        pe.wait_ge(side_stored, side_number(("turn", q // 4, q % 4)) + 1)
                        pe.wait_ge(bc_stored, 8)
                        if q:
                            pe.wait_ge(drive_read, q)
                        for r in range(4):
                            for c in range(2):
                                last = mm(ps[:, 4 + r, c * T:(c + 1) * T], driveT[32 * r:32 * r + 32, c, q, :],
                                          uT[32 * r:32 * r + 32, q, :], start=True, stop=True)
                        last.then_inc(drive_done, 1)
                        continue
                    n = side_number(job)
                    if n:
                        pe.wait_ge(side_stored, n)
                    if job[0] == "turn":
                        _, i, j = job
                        pe.wait_ge(rows_ready, 2 * i + 2)
                        if CHUNKS[i][1] == "value":
                            pe.wait_ge(z_ready, 1 + (i > 3))
                        for t in range(TT):
                            last = tr(ps[:, 3, t * P:(t + 1) * P], rows[:, i % 2, t, j * P:(j + 1) * P], P)
                    else:
                        q = job[1]
                        pe.wait_ge(states_ready, q + 1)
                        pe.wait_ge(skip_ready, q + 1)
                        b = q % 2
                        mm(ps[:, 3, 0:T], skip[:, :], uT[:, q, :], start=True, stop=False, skip_group_check=True)
                        for c, w, x in ((0, 0, 0), (0, 1, 1), (1, 0, 1), (1, 1, 0)):
                            for r in range(4):
                                last = mm(ps[32 * r:32 * r + 32, 3, 0:T], readT[:, c, q, 32 * r:32 * r + 32],
                                          rot[:, b, w, r, x * T:(x + 1) * T], start=False,
                                          stop=(c == 1 and w == 1), skip_group_check=True)
                    last.then_inc(side_done, 1)

            for it in range(8):
                for u in range(4):
                    for kind in range(3):
                        n = A_UNITS + it * RING + 3 * u + kind
                        s, use = ring_use(n)
                        if kind == 0:
                            pe.wait_ge(landed[s], 16 * (use + 1))
                            for kk in range(4):
                                k = 4 * u + kk
                                if it == 0:
                                    pe.wait_ge(h_ready, k + 1)
                                for t in range(TT):
                                    if k == 0 and it > 0:
                                        pe.wait_ge(rows_ready, 2 * it - 1 + t)
                                    if k == 0 and it == 0:
                                        pe.wait_ge(ada_copied, 1 + t)
                                    last = mm(ps[:, t, :], hT[:, k, t * P:(t + 1) * P],
                                              ring[:, s, kk * N:(kk + 1) * N], start=(k == 0), stop=(k == KD - 1),
                                              skip_group_check=True)
                            last.then_inc(consumed, 1)
                        else:
                            m = it * 8 + 2 * u + kind - 1
                            if m % KD == 0:
                                pe.wait_ge(ada_copied, 2 + m // KD)
                                if m == 0:
                                    pe.wait_ge(cw_stored, 1)
                            ada_unit(n, 2, m % KD).then_inc(consumed, 1)
                            if m % KD == KD - 1:
                                pe.drain().then_inc(ada_done, 1)
                    if u == 3:
                        pe.drain().then_inc(chunk_done, 1)
                    side(4 * it + u)
            for g in range(32, 36):
                side(g)

            def column_sums(bank, n):
                for c in range(CT_):
                    last = mm(ps[:, bank, 0:T], mean_w, n[:, c, :], start=(c == 0), stop=(c == CT_ - 1))
                return last

            def out_units(ms):
                for m in ms:
                    c, q = C_ORDER[m]
                    s, use = ring_use(A_UNITS + B_UNITS + m)
                    pe.wait_ge(landed[s], 16 * (use + 1))
                    src, k0 = (uT, 4 * q - 8) if q >= 2 else (conv, 4 * q)
                    if m == 0:
                        pe.wait_ge(rows_ready, 16)
                        pe.wait_ge(side_stored, len(SIDE))
                        pe.wait_ge(ada_copied, 6)
                    for kk in range(4):
                        if m == 0:
                            pe.wait_ge(ys_ready, CT_)
                        if m == 6:
                            pe.wait_ge(yc_ready, CT_)
                        for t in range(TT):
                            if m == 12 and kk == 0:
                                pe.wait_ge(x1_ready, t + 1)
                            first = q == 2 and kk == 0
                            end = q == 1 and kk == 3
                            last = mm(ps[:, OUT_BANKS[c][t], :], src[:, k0 + kk, t * P:(t + 1) * P],
                                      ring[:, s, kk * N:(kk + 1) * N], start=first, stop=end, skip_group_check=True)
                    last.then_inc(consumed, 1)
                    if q == 1:
                        pe.drain().then_inc(out_done, 1)

            pe.wait_ge(sum_consts, 1)
            pe.wait_ge(conv_step, CT_ * TAPS)
            column_sums(7, conv).then_inc(sums, 1)
            pe.wait_ge(squares, 1)
            column_sums(6, sq).then_inc(sums, 1)
            out_units([0, 1])
            pe.wait_ge(squares, 2)
            column_sums(7, sq).then_inc(sums, 1)
            out_units([2, 3])
            pe.wait_ge(squares, 3)
            column_sums(6, sq).then_inc(sums, 1)
            out_units(range(4, C_UNITS))

            for b in range(8):
                for k in (2 * b, 2 * b + 1):
                    for t in range(TT):
                        pe.wait_ge(xn_ready[t], 1)
                        if b >= 4:
                            pe.wait_ge((h2_even, h2_odd)[b % 2], 2 * ((b - 4) // 2) + 2)
                        o = (k % 2) * T + t * P
                        last = tr(ps[:, 4 + b % 4, o:o + P], xn[:, t, k:D:KD], P)
                last.then_inc(xn_turned, 1)
            pe.wait_ge(wr_ready, 2)
            pe.wait_ge(x1_ready, 8)
            for k in range(KD):
                b = k // 2
                pe.wait_ge((h2_even, h2_odd)[b % 2], 2 * (b // 2) + k % 2 + 1)
                last = mm(ps[0:NG + EXP, 0, 0:T], wr[:, k, :], xT[:, k, :], start=(k == 0), stop=(k == KD - 1))
            last.then_inc(logits_done, 1)
            pe.wait_ge(logits_biased, 1)
            for t in range(TT):
                last = tr(ps[:, 1, t * 64:t * 64 + NG + EXP], lgT[:, t * P:(t + 1) * P], NG + EXP)
            last.then_inc(logits_turned, 1)
            pe.wait_ge(sel_ready, 1)
            mm(ps[:, 2, 0:EXP], before, sel[:, 0, 2, :], start=True, stop=True)
            mm(ps[:, 2, EXP:2 * EXP], before, sel[:, 1, 2, :], start=True, stop=False)
            mm(ps[:, 2, EXP:2 * EXP], ones, sel[:, 0, 2, :], start=False, stop=True)
            mm(ps[:, 2, 2 * EXP:3 * EXP], ones, sel[:, 0, 2, :], start=True, stop=False)
            mm(ps[:, 2, 2 * EXP:3 * EXP], ones, sel[:, 1, 2, :], start=False, stop=True).then_inc(rank_done, 1)

            def job(j):
                pe.wait_ge(picks_ready, j + 1)
                for k in range(KD):
                    if k >= 2:
                        pe.wait_ge((tok_even, tok_odd)[k % 2], j * 8 + k // 2)
                    for t in range(TT):
                        last = mm(ps[:, 4 + k % 2, 0:T], xn[:, t, k:D:KD], pick[:, t, :], start=(t == 0), stop=(t == 1))
                    last.then_inc(gathered, 1)
                pe.wait_ge(added, j * 16)
                for pr in range(2):
                    for t in range(TT):
                        last = tr(ps[:, 6 + pr, t * P:(t + 1) * P], wpick[:, t, pr * P:(pr + 1) * P], P)
                last.then_inc(picks_turned, 1)
                pe.wait_ge(tok_even, j * 8 + 8)
                pe.wait_ge(tok_odd, j * 8 + 8)
                m = 0
                for pr in range(2):
                    for stage in range(3):
                        if stage == 2:
                            pe.wait_ge(hidden_ready, j * 2 + pr + 1)
                            for i in range(4):
                                last = tr(ps[:, 4 + pr, i * P:(i + 1) * P], hid[:, i * P:(i + 1) * P], P)
                            last.then_inc(hidden_turned, 1)
                            pe.wait_ge(hidden_stored, j * 2 + pr + 1)

                        def combine(n):
                            pe.wait_ge(down_stored, j * 8 + pr * 4 + n + 1)
                            if n == 0 and pr == 0:
                                pe.wait_ge(scatter_ready, j + 1)
                            for t in range(TT):
                                if n or pr:
                                    pe.wait_ge(added, j * 16 + pr * 8 + 2 * n + t - 1)
                                mm(ps[:, 6 + t, :], wpickT[:, pr, t * P:(t + 1) * P], yexp[:, n, :],
                                   start=True, stop=True).then_inc(combined, 1)

                        for u in range(4):
                            for x in range(2):
                                s = m % RING
                                pe.wait_ge(landed[s], j * 64 + 16 * (D_USES[s] + m // RING + 1))
                                half = slice(64 * x, 64 * x + 64)
                                for kk in range(4):
                                    if stage < 2:
                                        k = 4 * u + kk
                                        slot = (2 * pr + x) * SLOTS
                                        last = mm(ps[half, stage, :], xT[:, k, slot:slot + SLOTS],
                                                  ring[:, s, kk * N:(kk + 1) * N], start=(k == 0),
                                                  stop=(k == KD - 1), skip_group_check=True)
                                    else:
                                        last = mm(ps[half, 2 + u % 2, :], hidT[:, kk, half],
                                                  ring[:, s, kk * N:(kk + 1) * N], start=(kk == 0),
                                                  stop=(kk == 3), skip_group_check=True)
                                last.then_inc(consumed, 1)
                                m += 1
                            if stage == 2:
                                pe.drain().then_inc(down_done, 1)
                                if u >= 1:
                                    combine(u - 1)
                        if stage < 2:
                            pe.drain().then_inc((gate_done, up_done)[stage], 1)
                        else:
                            combine(3)

            with pe.Fori(0, NB) as j:
                job(j)
            pe.wait_ge(jobs_ready, 1)
            n_jobs = pe.value_load(jobn[0:1, 0:1], min_val=NB, max_val=JOBS)
            with pe.If(n_jobs > NB):
                with pe.Fori(NB, n_jobs) as j:
                    job(j)

        @block.scalar
        def _(act):
            A = nc.scalar.activation
            act.dma_start(ccol[:, :], col(a["c"][0])).then_inc(c_landed, 16)
            for dst, src in (
                (ldt[:, :], a["ssm_log_dt"][0].rearrange("(r g) -> r g", g=2)),
                (prm[:, 0, :], a["ssm_a_re"][0].rearrange("(r g) s -> r (g s)", g=2)),
                (prm[:, 1, :], a["ssm_a_im"][0].rearrange("(r g) s -> r (g s)", g=2)),
                (bst[:, 0, :], a["ssm_b_re"][0].rearrange("(r g) s h -> r (g s h)", g=2)),
                (bst[:, 1, :], a["ssm_b_im"][0].rearrange("(r g) s h -> r (g s h)", g=2)),
                (cst[:, 0, :, :], a["ssm_c_re"][0].rearrange("(q g) h s -> (g h) q s", q=QUADS)),
                (cst[:, 1, :, :], a["ssm_c_im"][0].rearrange("(q g) h s -> (g h) q s", q=QUADS)),
                (cwst[0:TAPS, :], a["conv_w"][0]),
                (cwst[TAPS:TAPS + 1, :], a["conv_b"]),
                (vst[0:8, :], a["conv_ln_g"][0].rearrange("(c p) -> c p", p=P)),
                (vst[8:16, :], a["conv_ln_b"][0].rearrange("(c p) -> c p", p=P)),
                (vst[16:24, :], a["out_norm_conv_g"][0].rearrange("(c p) -> c p", p=P)),
                (vst[24:32, :], a["out_norm_ssm_g"][0].rearrange("(c p) -> c p", p=P)),
                (vst[32:40, :], a["ssm_d"][0].rearrange("(c p) -> c p", p=P)),
            ):
                act.dma_start(dst, src).then_inc(setup_landed, 16)
            for dst, src in (
                (g1[:, :], col(a["norm1_g"][0])),
                (g2[:, :], col(a["norm2_g"][0])),
                (bada[:, :, :], a["b_ada"][0].rearrange("(m p k) -> p m k", m=6, k=KD)),
                (rbias[0:NG, :], a["router_group_b"][0].rearrange("(e o) -> e o", o=1)),
                (rbias[NG:NG + EXP, :], a["router_expert_b"][0].rearrange("g (e o) -> (g e) o", o=1)),
            ):
                act.dma_start(dst, src).then_inc(late_landed, 16)

            act.wait_ge(consts_ready, 1)
            for t in range(TT):
                act.wait_ge(x_landed, 16 * TT)
                A(ring[:, 8 + t, :], xr[:, t, :], ACT.Square, accum_out=ss[:, t:t + 1]).then_inc(x_squares, 1)
            act.wait_ge(x_var, 1)
            A(rstd[:, 2:4], rstd[:, 0:2], ACT.Sqrt).then_inc(x_root, 1)
            act.wait_ge(c_landed, 16)
            A(ccol[:, :], ccol[:, :], ACT.Silu).then_inc(c_silu, 1)
            act.wait_ge(setup_landed, 16 * 14)
            A(dt[:, :], ldt[:, :], ACT.Exp).then_inc(dt_ready, 1)
            act.wait_ge(decay_in, 1)
            A(prm[:, 6, :], prm[:, 2, :], ACT.Exp).then_inc(decay_ready, 1)
            act.wait_ge(angle_in, 1)
            A(prm[:, 7, :], prm[:, 5, :], ACT.Sin).then_inc(angle_ready, 1)
            A(prm[:, 9, :], prm[:, 5, :], ACT.Abs).then_inc(angle_ready, 1)
            act.wait_ge(angle_ready, 2)
            A(prm[:, 8, :], prm[:, 9, :], ACT.Sin, scale=-1.0, bias=halfpi[0:32, :]).then_inc(angle_ready, 1)
            for b in range(8):
                act.wait_ge(x_turned, b + 1)
                nc.scalar.copy(hT[:, 2 * b:2 * b + 2, :].rearrange("p k t -> p (k t)"),
                               ps[:, 4 + b % 4, :]).then_inc(x_stored, 1)

            def ada_copy(n, bank):
                act.wait_ge(ada_done, n + 1)
                if n:
                    act.wait_ge(mod_stored, 16 * n)
                nc.scalar.copy(modrow[:, :], ps[:, bank, :]).then_inc(ada_copied, 1)
                act.wait_ge(ada_copied, n + 1)
                part = (1, 0, 2, 3, 4, 5)[n]
                act.dma_start(mod_dram[part].rearrange("(j n) -> j n", n=N),
                              modrow[0:P:32, :]).then_inc(mod_stored, 16)

            def ada_fetch(n):
                part = (1, 0, 2, 3, 4, 5)[n]
                act.wait_ge(mod_stored, 16 * (n + 1))
                act.dma_start(mod[:, part, :], col(mod_dram[part])).then_inc(mod_landed, 16)

            ada_copy(0, 0)
            ada_fetch(0)
            act.wait_ge(phase_ready, 1)
            A(sinT, cosT, ACT.Sin, scale=TWO_PI_DOWN).then_inc(table_sin, 1)
            A(rot128[:, 1, :], rot128[:, 0, :], ACT.Sin, scale=TWO_PI_DOWN).then_inc(table_sin, 1)
            act.wait_ge(table_sin, 2)
            A(cosT, cosT, ACT.Abs).then_inc(table_abs, 1)
            A(rot128[:, 0, :], rot128[:, 0, :], ACT.Abs).then_inc(table_abs, 1)
            act.wait_ge(table_abs, 2)
            A(cosT, cosT, ACT.Sin, scale=-TWO_PI_DOWN, bias=halfpi[:, :]).then_inc(tables_ready, 1)
            A(rot128[:, 0, :], rot128[:, 0, :], ACT.Sin, scale=-TWO_PI_DOWN, bias=halfpi[:, :]).then_inc(tables_ready, 1)
            ada_copy(1, 1)
            ada_fetch(1)
            for b in range(8):
                c, q = (b % 4) // 2, (b % 2) * 4
                act.wait_ge(bc_turned, b + 1)
                dst = (driveT if b < 4 else readT)[:, c, q:q + 4, :].rearrange("p q s -> p (q s)")
                nc.scalar.copy(dst, ps[:, 4 + b % 4, :]).then_inc(bc_stored, 1)

            act.wait_ge(pads_ready, 1)

            def side(g):
                for job in side_jobs(g):
                    if job[0] == "drive":
                        continue
                    n = side_number(job)
                    act.wait_ge(side_done, n + 1)
                    if job[0] == "turn":
                        _, i, j = job
                        tile = TURNED[i] + j
                        kind = CHUNKS[i][1]
                        dst = {"u": uT[:, tile, :], "value": zT[:, tile, PAD:], "out_gate": sgT[:, tile, :]}[kind]
                        nc.scalar.copy(dst, ps[:, 3, 0:T]).then_inc(side_stored, 1)
                    else:
                        A(uT[:, job[1], :], ps[:, 3, 0:T], ACT.Gelu_apprx_tanh).then_inc(side_stored, 1)

            for it in range(8):
                for u in range(4):
                    side(4 * it + u)
                    if u == 1 and it in (2, 4, 6):
                        ada_fetch(1 + it // 2)
                kind = CHUNKS[it][1]
                act.wait_ge(chunk_done, it + 1)
                if it in (4, 6):
                    act.wait_ge(z_ready, it // 2 - 1)
                for t in range(TT):
                    f = ACT.Sigmoid if kind in ("gate", "out_gate") else ACT.Copy
                    A(rows[:, it % 2, t, :], ps[:, t, :], f).then_inc(rows_ready, 1)
                if it % 2:
                    ada_copy(2 + it // 2, 2)
            for g in range(32, 36):
                side(g)
            ada_fetch(5)

            act.dma_start(bada2, a["b_ada"][0].rearrange("(m p k) -> p m k", m=6, k=KD)).then_inc(bada_landed, 16)
            act.dma_start(wrg, a["router_group_w"][0].rearrange("(p k) g -> p k g", k=KD)).then_inc(wr_landed, 16)
            act.dma_start(wre, a["router_expert_w"][0].rearrange("g (p k) e -> p g k e", k=KD)).then_inc(wr_landed, 16)
            act.wait_ge(gated, CT_)
            A(sq, uT, ACT.Square).then_inc(squares, 1)
            act.wait_ge(sums, 2)
            A(stat[:, 0, :], ps[:, 6, 0:T], ACT.Sqrt, bias=eps[:, :]).then_inc(rooted, 1)
            act.wait_ge(centred, 1)
            A(sq, conv, ACT.Square).then_inc(squares, 1)
            act.wait_ge(sums, 3)
            A(stat[:, 1, :], ps[:, 7, 0:T], ACT.Sqrt, bias=eps[:, :]).then_inc(rooted, 1)
            act.wait_ge(scaled, 1)
            for c in range(CT_):
                A(conv[:, c, :], conv[:, c, :], ACT.Silu, scale=vT[:, 0, c:c + 1],
                  bias=vT[:, 1, c:c + 1]).then_inc(swished, 1)
            act.wait_ge(swished, CT_)
            A(sq, conv, ACT.Square).then_inc(squares, 1)
            act.wait_ge(sums, 4)
            A(stat[:, 2, :], ps[:, 6, 0:T], ACT.Sqrt, bias=eps[:, :]).then_inc(rooted, 1)
            act.wait_ge(gate_added, 2)
            for i, part in enumerate((2, 5)):
                act.dma_start(col(gate_dram[i]), mod[:, part, :]).then_inc(gate_stored, 16)
            act.wait_ge(gate_stored, 32)
            act.dma_start(gate1, gate_dram[0:1, :].to_broadcast([P, D])).then_inc(gate_landed, 16)

            for n in range(8):
                c, t = divmod(n, 2)
                act.wait_ge(x1_ready, n + 1)
                if n:
                    act.wait_ge(x1_squares, n)
                A(sq[:, 0:2, :].rearrange("p c t -> p (c t)"), x1[:, t, c * N:(c + 1) * N], ACT.Square,
                  accum_out=ss[:, t * 4 + c:t * 4 + c + 1]).then_inc(x1_squares, 1)
            act.wait_ge(n2_var, 1)
            A(rstd[:, 2:4], rstd[:, 0:2], ACT.Sqrt).then_inc(n2_root, 1)
            act.dma_start(gate2, gate_dram[1:2, :].to_broadcast([P, D])).then_inc(gate_landed, 16)
            act.dma_start(fgain, a["final_norm_g"].rearrange("(o d) -> o d", o=1).to_broadcast([P, D])).then_inc(gain_landed, 16)
            act.wait_ge(n2_rstd, 1)
            nc.scalar.mul(xn[:, 1, :], x1[:, 1, :], rstd[:, 1:2]).then_inc(xn_ready[1], 1)
            for b in range(1, 8, 2):
                act.wait_ge(xn_turned, b + 1)
                for i in range(2):
                    k = 2 * b + i
                    A(xT[:, k, :], ps[:, 4 + b % 4, i * T:(i + 1) * T], ACT.Identity, scale=mod[:, 4, k:k + 1],
                      bias=mod[:, 3, k:k + 1]).then_inc(h2_odd, 1)
            act.wait_ge(logits_done, 1)
            A(lgT[:, :], ps[0:NG + EXP, 0, 0:T], ACT.Identity, bias=rbias[:, :]).then_inc(logits_biased, 1)
            act.wait_ge(exp_in, 1)
            A(rt[:, :, 0:4], rt[:, :, 0:4], ACT.Exp).then_inc(exp_done, 1)
            act.wait_ge(exp_in, 2)
            A(rt[:, :, 6:7], rt[:, :, 5:6], ACT.Exp).then_inc(exp_done, 1)

            def job(j):
                for k in range(1, KD, 2):
                    act.wait_ge(gathered, j * KD + k + 1)
                    A(xT[:, k, :], ps[:, 5, 0:T], ACT.Identity, scale=mod[:, 4, k:k + 1],
                      bias=mod[:, 3, k:k + 1]).then_inc(tok_odd, 1)
                for pr in range(2):
                    act.wait_ge(gate_done, j * 2 + pr + 1)
                    A(silu, ps[:, 0, :], ACT.Silu).then_inc(gate_silu, 1)
                    act.wait_ge(hidden_turned, j * 2 + pr + 1)
                    nc.scalar.copy(hidT.rearrange("p j s -> p (j s)"), ps[:, 4 + pr, :]).then_inc(hidden_stored, 1)
                    for n in range(4):
                        act.wait_ge(down_done, j * 8 + pr * 4 + n + 1)
                        nc.scalar.copy(yexp[:, n, :], ps[:, 2 + n % 2, :]).then_inc(down_stored, 1)

            with act.Fori(0, NB) as j:
                job(j)
            act.wait_ge(jobs_ready, 1)
            n_jobs = act.value_load(jobn[0:1, 0:1], min_val=NB, max_val=JOBS)
            with act.If(n_jobs > NB):
                with act.Fori(NB, n_jobs) as j:
                    job(j)
            for t in range(TT):
                act.wait_ge(fin_sq_in, t + 1)
                if t:
                    act.wait_ge(fin_sq, t)
                A(junk, x1[:, t, :], ACT.Square, accum_out=ss[:, t:t + 1]).then_inc(fin_sq, 1)
                act.wait_ge(fin_var, t + 1)
                A(rstd[:, 2 + t:3 + t], rstd[:, t:t + 1], ACT.Sqrt).then_inc(fin_root, 1)

        @block.gpsimd
        def _(pool):
            gp_ = nc.gpsimd
            n = [0]

            def link(ins):
                n[0] += 1
                ins.then_inc(pool_order, 1)
                pool.wait_ge(pool_order, n[0])

            link(gp_.memset(ident[:, :], 0.0))
            link(gp_.affine_select(out=ident[:, :], in_=ident[:, :], compare_op=ALU.not_equal, fill=1.0, base=0,
                                   pattern=[[-1, P]], channel_multiplier=1))
            link(gp_.iota(iota_i, pattern=[[1, P]], base=0, channel_multiplier=0))
            link(gp_.iota(part_i, pattern=[[0, 1]], base=0, channel_multiplier=1))
            link(gp_.memset(halfpi[:, :], math.pi / 2))
            gp_.memset(eps[:, :], EPS).then_inc(consts_ready, 1)
            gp_.memset(at(114, 8 * KB), 0.0).then_inc(blocks_zero, 1)

            def diagonal(q):
                if q:
                    pool.wait_ge(side_done, side_number(("read", q - 1)) + 1)
                gp_.tensor_scalar(skip[:, :], ident[:, :], vT[:, 4, q:q + 1], None, ALU.mult).then_inc(skip_ready, 1)

            pool.wait_ge(cw_stored, 1)
            for q in range(QUADS):
                if q == 5:
                    pool.wait_ge(rows_ready, 8)
                    gp_.tensor_tensor(rows[:, 1, :, :], rows[:, 1, :, :], rows[:, 0, :, :], ALU.mult).then_inc(z_ready, 1)
                diagonal(q)
            pool.wait_ge(side_done, side_number(("read", QUADS - 1)) + 1)
            link(gp_.memset(ones, 1.0))
            link(gp_.affine_select(out=before, in_=ones, compare_op=ALU.is_gt, fill=0.0, base=0,
                                   pattern=[[1, P]], channel_multiplier=-1))
            gp_.memset(mean_w, 1.0 / CH).then_inc(sum_consts, 1)
            pool.wait_ge(rows_ready, 12)
            gp_.tensor_tensor(rows[:, 1, :, :], rows[:, 1, :, :], rows[:, 0, :, :], ALU.mult).then_inc(z_ready, 1)
            for c in range(CT_):
                pool.wait_ge(side_stored, side_number(("turn", 6 + c // 4, c % 4)) + 1)
                gp_.tensor_tensor(uT[:, c, :], uT[:, c, :], sgT[:, c, :], ALU.mult).then_inc(gated, 1)
            pool.wait_ge(wr_landed, 32)
            gp_.tensor_copy(wr[:, :, 0:NG], wrg[:, :, :]).then_inc(wr_ready, 1)
            gp_.tensor_copy(wr[:, :, NG:].rearrange("p k (g e) -> p g k e", g=NG), wre[:, :, :, :]).then_inc(wr_ready, 1)

            pool.wait_ge(counts_ready, 1)
            rounds = JOBS // NB
            most, flag, pos, e0, r0 = (jb[:, i, :] for i in range(5))
            over = jm[:, 0, 0:EXP]
            link(gp_.memset(flag[:, 0:NB], 1.0))
            for r in range(rounds):
                rb = slice(r * NB, (r + 1) * NB)
                if r:
                    link(gp_.tensor_scalar(over, counts, float(r * SLOTS), None, ALU.is_gt))
                    link(gp_.tensor_tensor(jm[:, 1, 0:16], over[:, 0:EXP:2], over[:, 1:EXP:2], ALU.add))
                    link(gp_.tensor_tensor(flag[:, rb], jm[:, 1, 0:16:2], jm[:, 1, 1:16:2], ALU.add))
                    link(gp_.tensor_scalar(flag[:, rb], flag[:, rb], 1.0, None, ALU.min))
                link(gp_.tensor_scalar(e0[:, rb], iota[:, 0:NB], float(BE), None, ALU.mult))
                link(gp_.memset(r0[:, rb], float(r * SLOTS)))
            link(gp_.memset(jm, 1.0))
            link(gp_.affine_select(out=jm, in_=jm, compare_op=ALU.is_gt, fill=0.0, base=0,
                                   pattern=[[1, JOBS], [-1, JOBS]], channel_multiplier=0))
            link(gp_.tensor_tensor(jm, jm, flag.unsqueeze(1).to_broadcast([P, JOBS, JOBS]), ALU.mult))

            def row_sums(dst):
                w = JOBS // 2
                while w:
                    link(gp_.tensor_tensor(jm[:, :, 0:w], jm[:, :, 0:w], jm[:, :, w:2 * w], ALU.add))
                    w //= 2
                link(gp_.tensor_copy(dst, jm[:, :, 0]))

            row_sums(pos)
            link(gp_.tensor_tensor(most, pos, flag, ALU.add))
            link(gp_.tensor_copy(jobn, most[0:1, JOBS - 1:JOBS]))
            link(gp_.tensor_scalar(jb[:, 5, :], flag, -1000.0, 1000.0, ALU.mult, ALU.add))
            link(gp_.tensor_tensor(pos, pos, jb[:, 5, :], ALU.add))
            for i, val in enumerate((e0, r0)):
                link(gp_.tensor_tensor(jm, pos.unsqueeze(1).to_broadcast([P, JOBS, JOBS]),
                                       iota[:, 0:JOBS].unsqueeze(2).to_broadcast([P, JOBS, JOBS]), ALU.subtract))
                link(gp_.tensor_scalar(jm, jm, 0.0, None, ALU.is_equal))
                link(gp_.tensor_tensor(jm, jm, val.unsqueeze(1).to_broadcast([P, JOBS, JOBS]), ALU.mult))
                row_sums(jobtab[:, i, :])
            gp_.tensor_copy(jobi, jobtab[0:1, 0, :]).then_inc(jobs_ready, 1)

        @block.vector
        def _(dve):
            V = nc.vector
            n = [0]

            def link(ins):
                n[0] += 1
                ins.then_inc(vec_order, 1)
                dve.wait_ge(vec_order, n[0])

            dve.wait_ge(consts_ready, 1)
            link(V.tensor_copy(steps, iota_i))
            link(V.tensor_copy(iota[:, :], steps[:, 0:SLOTS]))
            link(V.tensor_scalar(part_i, part_i, 4, 1, ALU.logical_shift_right, ALU.bitwise_and))
            link(V.tensor_copy(odd[:, 1:2], part_i))
            link(V.tensor_scalar(odd[:, 0:1], odd[:, 1:2], -1.0, 1.0, ALU.mult, ALU.add))
            dve.wait_ge(x_squares, TT)
            V.tensor_scalar(rstd[:, 0:2], ss[:, 0:2], 1.0 / D, EPS, ALU.mult, ALU.add).then_inc(x_var, 1)
            dve.wait_ge(x_root, 1)
            V.reciprocal(rstd[:, 0:2], rstd[:, 2:4]).then_inc(x_rstd, 1)
            dve.wait_ge(x_rstd, 1)
            for t in range(TT):
                V.tensor_scalar(xr[:, t, :], xr[:, t, :], rstd[:, t:t + 1], None, ALU.mult).then_inc(x_normed, 1)
            re, im, red, ang, k_, r_ = (prm[:, i, :] for i in range(6))
            mag, sin_, cos_, absr, turns = (prm[:, i, :] for i in (6, 7, 8, 9, 10))
            nr, ni, t1, t2, f_re, f_im, rden = (prm[:, i, :] for i in (11, 12, 13, 14, 15, 16, 17))
            dve.wait_ge(dt_ready, 1)
            dtb = dt[:, :].unsqueeze(2).to_broadcast([32, 2, S])

            def by_group(v):
                return v.rearrange("p (g s) -> p g s", g=2)

            V.tensor_tensor(by_group(red), by_group(re), dtb, ALU.mult).then_inc(decay_in, 1)
            link(V.tensor_tensor(by_group(ang), by_group(im), dtb, ALU.mult))
            link(V.tensor_scalar(k_, ang, 1.0 / (2 * math.pi), MAGIC, ALU.mult, ALU.add))
            link(V.tensor_scalar(k_, k_, MAGIC, None, ALU.subtract))
            link(V.scalar_tensor_tensor(r_, k_, -C1, ang, ALU.mult, ALU.add))
            link(V.scalar_tensor_tensor(r_, k_, -C2, r_, ALU.mult, ALU.add))
            link(V.scalar_tensor_tensor(r_, k_, -C3, r_, ALU.mult, ALU.add))
            link(V.tensor_scalar(r_, r_, PI_DOWN, -PI_DOWN, ALU.min, ALU.max))
            V.tensor_scalar(turns, r_, 1.0 / (2 * math.pi), None, ALU.mult).then_inc(angle_in, 1)
            dve.wait_ge(decay_ready, 1)
            dve.wait_ge(angle_ready, 3)
            link(V.tensor_tensor(nr, mag, cos_, ALU.mult))
            link(V.tensor_tensor(ni, mag, sin_, ALU.mult))
            link(V.tensor_scalar(nr, nr, 1.0, None, ALU.subtract))
            link(V.tensor_tensor(t1, re, re, ALU.mult))
            link(V.tensor_tensor(t2, im, im, ALU.mult))
            link(V.tensor_tensor(t1, t1, t2, ALU.add))
            link(V.reciprocal(rden, t1))
            link(V.tensor_tensor(t1, nr, re, ALU.mult))
            link(V.tensor_tensor(t2, ni, im, ALU.mult))
            link(V.tensor_tensor(t1, t1, t2, ALU.add))
            link(V.tensor_tensor(f_re, t1, rden, ALU.mult))
            link(V.tensor_tensor(t1, ni, re, ALU.mult))
            link(V.tensor_tensor(t2, nr, im, ALU.mult))
            link(V.tensor_tensor(t1, t1, t2, ALU.subtract))
            V.tensor_tensor(f_im, t1, rden, ALU.mult).then_inc(params_ready, 1)
            dve.wait_ge(cw_turned, 1)
            link(V.tensor_copy(cwT[:, :, :].rearrange("p c t -> p (c t)"), ps[:, 2, 0:256]))
            V.tensor_copy(vT[:, :, :].rearrange("p n c -> p (n c)"), ps[:, 2, 256:296]).then_inc(cw_stored, 1)
            dve.wait_ge(setup_landed, 16 * 14)
            for c in range(2):
                for g in range(2):
                    ins = V.tensor_scalar(cexp[:, c, :, g, :], cst[:, c, :, :], odd[:, g:g + 1], None, ALU.mult)
                    if c == 0 or g == 0:
                        link(ins)
                    else:
                        ins.then_inc(cexp_ready, 1)
            dve.wait_ge(params_turned, 1)
            V.tensor_copy(par[:, :, :].rearrange("p n q -> p (n q)"), ps[:, 3, 0:128]).then_inc(params_stored, 1)
            dve.wait_ge(params_stored, 1)
            link(V.tensor_copy(decay[:, :], par[:, 0, :]))
            dve.wait_ge(b_turned, 1)
            dve.wait_ge(blocks_zero, 1)
            b_re, b_im = (ps[:, 4 + c, :].rearrange("p (h r) -> p r h", h=HG) for c in range(2))
            fr, fi = (par[:, i, :].unsqueeze(2).to_broadcast([P, PAIRS, HG]) for i in (2, 3))
            m1, m2 = (btmp[:, i, 0:N].rearrange("p (r h) -> p r h", h=HG) for i in range(2))
            for c, (p1, p2, op) in enumerate(((b_re, b_im, ALU.subtract), (b_im, b_re, ALU.add))):
                link(V.tensor_tensor(m1, p1, fr, ALU.mult))
                link(V.tensor_tensor(m2, p2, fi, ALU.mult))
                for g in range(2):
                    half = slice(64 * g, 64 * g + 64)
                    ins = V.tensor_tensor(bdiag[half, c, :, g, :], m1[half], m2[half], op)
                    if c == 1 and g == 1:
                        ins.then_inc(bdiag_ready, 1)
                    else:
                        link(ins)
            dve.wait_ge(late_landed, 16 * 5)
            dve.wait_ge(mod_landed, 16)
            link(V.tensor_tensor(mod[:, 1, :], mod[:, 1, :], bada[:, 1, :], ALU.add))
            link(V.scalar_tensor_tensor(mod[:, 1, :], mod[:, 1, :], 1.0, g1[:, :], ALU.add, ALU.mult))
            th = par[:, 1, :].unsqueeze(2).to_broadcast([P, PAIRS, HALF])
            link(V.tensor_tensor(cosT, th, steps.unsqueeze(1).to_broadcast([P, PAIRS, HALF]), ALU.mult))
            link(V.tensor_scalar(sinT, cosT, MAGIC, MAGIC, ALU.add, ALU.subtract))
            link(V.tensor_tensor(cosT, cosT, sinT, ALU.subtract))
            link(V.tensor_scalar(rot128[:, 0, :], par[:, 1, :], float(HALF), None, ALU.mult))
            link(V.tensor_scalar(rot128[:, 1, :], rot128[:, 0, :], MAGIC, MAGIC, ALU.add, ALU.subtract))
            V.tensor_tensor(rot128[:, 0, :], rot128[:, 0, :], rot128[:, 1, :], ALU.subtract).then_inc(phase_ready, 1)
            dve.wait_ge(x_stored, 8)
            dve.wait_ge(mod_landed, 32)
            link(V.tensor_tensor(mod[:, 0, :], mod[:, 0, :], bada[:, 0, :], ALU.add))
            for k in range(KD):
                V.tensor_scalar(hT[:, k, :], hT[:, k, :], mod[:, 1, k:k + 1], mod[:, 0, k:k + 1], ALU.mult,
                                ALU.add).then_inc(h_ready, 1)
            dve.wait_ge(bc_stored, 8)
            V.memset(zT[:, :, 0:PAD], 0.0).then_inc(pads_ready, 1)

            dve.wait_ge(tables_ready, 2)
            for q in range(QUADS):
                b = q % 2
                c4 = cosT[:, 4 * q:4 * q + 4, :].unsqueeze(2).to_broadcast([P, 4, 4, HALF])
                s4 = sinT[:, 4 * q:4 * q + 4, :].unsqueeze(2).to_broadcast([P, 4, 4, HALF])
                s2 = sinT[:, 4 * q:4 * q + 4, :].unsqueeze(2).to_broadcast([P, 4, 2, HALF])
                drive = ps[:, 4:8, :].rearrange("p r (x t) -> p r x t", x=4)
                r1 = rot[:, b, 0, :, :]
                r2 = rot[:, b, 1, :, :]
                r1v = r1.rearrange("p r (x t) -> p r x t", x=4)
                r2v = r2.rearrange("p r (x t) -> p r x t", x=4)
                dve.wait_ge(drive_done, q + 1)
                if q >= 2:
                    dve.wait_ge(side_done, side_number(("read", q - 2)) + 1)
                link(V.tensor_tensor(r1v, drive, c4, ALU.mult))
                V.tensor_tensor(r2v, drive, s4, ALU.mult).then_inc(drive_read, 1)
                dve.wait_ge(drive_read, q + 1)
                link(V.tensor_tensor(r1[:, :, 0:T], r1[:, :, 0:T], r2[:, :, T:2 * T], ALU.add))
                link(V.tensor_tensor(r1[:, :, T:2 * T], r2[:, :, 0:T], r1[:, :, T:2 * T], ALU.subtract))
                for half in range(2):
                    for r in range(4):
                        m = decay[:, 4 * q + r:4 * q + r + 1].to_broadcast([P, HALF])
                        for x in range(2):
                            z = r1[:, r, x * T + half * HALF:x * T + (half + 1) * HALF]
                            init = carry[:, 2, r, x:x + 1] if half else 0.0
                            n[0] += 1
                            V.tensor_tensor_scan(z, m, z, init, ALU.mult, ALU.add).then_inc(vec_order, 1)
                    dve.wait_ge(vec_order, n[0])
                    if half == 0:
                        end = r1.rearrange("p r (x t) -> p r x t", x=2)[:, :, :, HALF - 1]
                        cc, sc = (rot128[:, i, 4 * q:4 * q + 4].unsqueeze(2).to_broadcast([P, 4, 2]) for i in range(2))
                        link(V.tensor_tensor(carry[:, 0, :, :], end, cc, ALU.mult))
                        link(V.tensor_tensor(carry[:, 1, :, :], end, sc, ALU.mult))
                        link(V.tensor_tensor(carry[:, 2, :, 0], carry[:, 0, :, 0], carry[:, 1, :, 1], ALU.add))
                        link(V.tensor_tensor(carry[:, 2, :, 1], carry[:, 0, :, 1], carry[:, 1, :, 0], ALU.subtract))
                link(V.tensor_scalar(r2[:, :, 0:T], r1[:, :, 0:T], -1.0, None, ALU.mult))
                link(V.tensor_tensor(r2v[:, :, 0:2, :], r2v[:, :, 0:2, :], s2, ALU.mult))
                link(V.tensor_tensor(r2v[:, :, 2:4, :], r1v[:, :, 2:4, :], s2, ALU.mult))
                V.tensor_tensor(r1v, r1v, c4, ALU.mult).then_inc(states_ready, 1)
                dve.wait_ge(states_ready, q + 1)

            done = 0
            for h in range(2):
                dve.wait_ge(side_stored, side_number(("turn", 3 + 2 * h, 3)) + 1)
                for j in range(TAPS):
                    for i in range(4):
                        c = 4 * h + i
                        z = zT[:, c, j:j + T]
                        if j == 0:
                            ins = V.tensor_scalar(conv[:, c, :], z, cwT[:, c, 0:1], cwT[:, c, TAPS:TAPS + 1],
                                                  ALU.mult, ALU.add)
                        else:
                            dve.wait_ge(conv_step, done - 3)
                            ins = V.scalar_tensor_tensor(conv[:, c, :], z, cwT[:, c, j:j + 1], conv[:, c, :],
                                                         ALU.mult, ALU.add)
                        ins.then_inc(conv_step, 1)
                        done += 1
            dve.wait_ge(mod_landed, 16 * 6)
            dve.wait_ge(bada_landed, 16)
            V.tensor_tensor(mod[:, 2, :], mod[:, 2, :], bada2[:, 2, :], ALU.add).then_inc(gate_added, 1)
            V.tensor_tensor(mod[:, 5, :], mod[:, 5, :], bada2[:, 5, :], ALU.add).then_inc(gate_added, 1)
            link(V.tensor_tensor(mod[:, 3, :], mod[:, 3, :], bada2[:, 3, :], ALU.add))
            link(V.tensor_tensor(mod[:, 4, :], mod[:, 4, :], bada2[:, 4, :], ALU.add))
            link(V.scalar_tensor_tensor(mod[:, 4, :], mod[:, 4, :], 1.0, g2[:, :], ALU.add, ALU.mult))

            def over_tiles(v):
                return v.unsqueeze(1).to_broadcast([P, CT_, T])

            dve.wait_ge(sums, 1)
            dve.wait_ge(conv_step, CT_ * TAPS)
            V.tensor_tensor(conv, conv, over_tiles(ps[:, 7, 0:T]), ALU.subtract).then_inc(centred, 1)
            dve.wait_ge(rooted, 1)
            link(V.reciprocal(stat[:, 0, :], stat[:, 0, :]))
            for c in range(CT_):
                V.scalar_tensor_tensor(uT[:, c, :], uT[:, c, :], vT[:, 3, c:c + 1], stat[:, 0, :], ALU.mult,
                                       ALU.mult).then_inc(ys_ready, 1)
            dve.wait_ge(rooted, 2)
            link(V.reciprocal(stat[:, 1, :], stat[:, 1, :]))
            V.tensor_tensor(conv, conv, over_tiles(stat[:, 1, :]), ALU.mult).then_inc(scaled, 1)
            dve.wait_ge(rooted, 3)
            link(V.reciprocal(stat[:, 2, :], stat[:, 2, :]))
            for c in range(CT_):
                V.scalar_tensor_tensor(conv[:, c, :], conv[:, c, :], vT[:, 2, c:c + 1], stat[:, 2, :], ALU.mult,
                                       ALU.mult).then_inc(yc_ready, 1)
            dve.wait_ge(gate_landed, 16)
            dve.wait_ge(x_again, 16)
            for m in range(8):
                c, t = divmod(m, 2)
                dve.wait_ge(out_done, c + 1)
                link(V.tensor_tensor(gtmp[:, t, :], ps[:, OUT_BANKS[c][t], :], gate1[:, c * N:(c + 1) * N], ALU.mult))
                cc = slice(c * N, (c + 1) * N)
                V.tensor_tensor(x1[:, t, cc], x1[:, t, cc], gtmp[:, t, :], ALU.add).then_inc(x1_ready, 1)
                dve.wait_ge(x1_ready, m + 1)
            dve.wait_ge(x1_squares, 8)
            link(V.tensor_reduce(rstd[:, 0:2], ss[:, :].rearrange("p (t c) -> p t c", t=TT), AX.X, ALU.add))
            V.tensor_scalar(rstd[:, 0:2], rstd[:, 0:2], 1.0 / D, EPS, ALU.mult, ALU.add).then_inc(n2_var, 1)
            dve.wait_ge(n2_root, 1)
            V.reciprocal(rstd[:, 0:2], rstd[:, 2:4]).then_inc(n2_rstd, 1)
            dve.wait_ge(n2_rstd, 1)
            V.tensor_scalar(xn[:, 0, :], x1[:, 0, :], rstd[:, 0:1], None, ALU.mult).then_inc(xn_ready[0], 1)
            for b in range(0, 8, 2):
                dve.wait_ge(xn_turned, b + 1)
                for i in range(2):
                    k = 2 * b + i
                    V.tensor_scalar(xT[:, k, :], ps[:, 4 + b % 4, i * T:(i + 1) * T], mod[:, 4, k:k + 1],
                                    mod[:, 3, k:k + 1], ALU.mult, ALU.add).then_inc(h2_even, 1)
            link(V.memset(acc, 0.0))
            link(V.memset(gp[:, :, :], -3.0e38))

            dve.wait_ge(logits_turned, 1)
            link(V.tensor_copy(lg[:, :, :], ps[:, 1, 0:128].rearrange("p (t e) -> p t e", t=TT)[:, :, 0:NG + EXP]))
            link(V.tensor_copy(gp[:, :, 0:NG], lg[:, :, 0:NG]))
            for t in range(TT):
                link(V.max(top[:, t, :], gp[:, t, :]))
                link(V.max_index(topi[:, t, :], top[:, t, :], gp[:, t, :]))
            V.tensor_tensor(rt[:, :, 0:4], lg[:, :, 0:NG], top[:, :, 0:1].to_broadcast([P, TT, NG]),
                            ALU.subtract).then_inc(exp_in, 1)
            gi = rt[:, :, 4:5]
            link(V.tensor_copy(gi, topi[:, :, 0:1]))
            onehot = comb[:, :, 0:NG]
            link(V.tensor_tensor(onehot, iota[:, 0:NG].unsqueeze(1).to_broadcast([P, TT, NG]),
                                 gi.to_broadcast([P, TT, NG]), ALU.is_equal))
            masked = sel[:, :, 0, :].rearrange("p t (e g) -> p t e g", g=NG)
            link(V.tensor_tensor(masked, lg[:, :, NG:].rearrange("p t (g e) -> p t e g", g=NG),
                                 onehot.unsqueeze(2).to_broadcast([P, TT, NE, NG]), ALU.mult))
            esel = rank[:, :, 0:NE]
            link(V.tensor_reduce(esel, masked, AX.X, ALU.add))
            for t in range(TT):
                link(V.max(etop[:, t, :], esel[:, t, :]))
                link(V.max_index(etopi[:, t, :], etop[:, t, :], esel[:, t, :]))
            V.tensor_tensor(rt[:, :, 5:6], etop[:, :, 1:2], etop[:, :, 0:1], ALU.subtract).then_inc(exp_in, 1)
            link(V.tensor_copy(rt[:, :, 8:10], etopi[:, :, 0:2]))
            link(V.scalar_tensor_tensor(rt[:, :, 8:10], gi.to_broadcast([P, TT, 2]), float(NE), rt[:, :, 8:10],
                                        ALU.mult, ALU.add))
            io = iota[:, 0:EXP].unsqueeze(1).to_broadcast([P, TT, EXP])
            for i in range(2):
                link(V.tensor_tensor(sel[:, :, i, :], io, rt[:, :, 8 + i:9 + i].to_broadcast([P, TT, EXP]), ALU.is_equal))
            V.tensor_tensor(sel[:, :, 2, :], sel[:, :, 0, :], sel[:, :, 1, :], ALU.add).then_inc(sel_ready, 1)
            dve.wait_ge(exp_done, 2)
            link(V.tensor_reduce(rt[:, :, 10:11], rt[:, :, 0:4], AX.X, ALU.add))
            link(V.tensor_scalar(rt[:, :, 11:12], rt[:, :, 6:7], 1.0, None, ALU.add))
            link(V.tensor_tensor(rt[:, :, 10:11], rt[:, :, 10:11], rt[:, :, 11:12], ALU.mult))
            link(V.reciprocal(rt[:, :, 12:13], rt[:, :, 10:11]))
            link(V.tensor_tensor(rt[:, :, 13:14], rt[:, :, 12:13], rt[:, :, 6:7], ALU.mult))
            dve.wait_ge(sel_ready, 1)
            for i in range(2):
                link(V.tensor_tensor(sel[:, :, i, :], sel[:, :, i, :], rt[:, :, 12 + i:13 + i].to_broadcast([P, TT, EXP]),
                                     ALU.mult))
            link(V.tensor_tensor(comb[:, :, :], sel[:, :, 0, :], sel[:, :, 1, :], ALU.add))
            dve.wait_ge(rank_done, 1)
            link(V.scalar_tensor_tensor(rank[:, :, :], ps[:, 2, 0:2 * EXP].rearrange("p (t e) -> p t e", t=TT), 1.0,
                                        sel[:, :, 2, :], ALU.add, ALU.mult))
            link(V.tensor_scalar(rank[:, :, :], rank[:, :, :], 1.0, None, ALU.subtract))
            V.tensor_copy(counts, ps[:, 2, 2 * EXP:3 * EXP]).then_inc(counts_ready, 1)
            dve.wait_ge(counts_ready, 1)

            JOB_STEPS = 6

            def job(j, e0, first_rank):
                c = [0]

                def step(ins):
                    c[0] += 1
                    ins.then_inc(job_order, 1)
                    dve.wait_ge(job_order, j * JOB_STEPS + c[0])

                if first_rank is None:
                    step(V.tensor_copy(rankc[:, :, :], rank[:, :, bass.ds(e0, BE)]))
                else:
                    step(V.tensor_scalar(rankc[:, :, :], rank[:, :, bass.ds(e0, BE)], first_rank, None, ALU.subtract))
                for t in range(TT):
                    step(V.tensor_tensor(pick[:, t, :].rearrange("p (e s) -> p e s", e=BE),
                                         iota[:, 0:SLOTS].unsqueeze(1).to_broadcast([P, BE, SLOTS]),
                                         rankc[:, t, :].unsqueeze(2).to_broadcast([P, BE, SLOTS]), ALU.is_equal))
                step(V.tensor_copy(rankc[:, :, :], comb[:, :, bass.ds(e0, BE)]))
                for t in range(TT):
                    ins = V.tensor_tensor(wpick[:, t, :].rearrange("p (e s) -> p e s", e=BE),
                                          pick[:, t, :].rearrange("p (e s) -> p e s", e=BE),
                                          rankc[:, t, :].unsqueeze(2).to_broadcast([P, BE, SLOTS]), ALU.mult)
                    if t == 0:
                        step(ins)
                    else:
                        ins.then_inc(picks_ready, 1)
                for k in range(0, KD, 2):
                    dve.wait_ge(gathered, j * KD + k + 1)
                    V.tensor_scalar(xT[:, k, :], ps[:, 4, 0:T], mod[:, 4, k:k + 1], mod[:, 3, k:k + 1], ALU.mult,
                                    ALU.add).then_inc(tok_even, 1)
                dve.wait_ge(picks_turned, j + 1)
                step(V.tensor_copy(wpickT[:, 0, :], ps[:, 6, 0:T]))
                V.tensor_copy(wpickT[:, 1, :], ps[:, 7, 0:T]).then_inc(scatter_ready, 1)
                for pr in range(2):
                    dve.wait_ge(up_done, j * 2 + pr + 1)
                    dve.wait_ge(gate_silu, j * 2 + pr + 1)
                    V.tensor_tensor(hid, silu, ps[:, 1, :], ALU.mult).then_inc(hidden_ready, 1)
                    for m in range(8):
                        nn, t = divmod(m, 2)
                        cc = slice(nn * N, (nn + 1) * N)
                        dve.wait_ge(combined, j * 16 + pr * 8 + m + 1)
                        V.tensor_tensor(acc[:, t, cc], acc[:, t, cc], ps[:, 6 + t, :], ALU.add).then_inc(added, 1)
                        dve.wait_ge(added, j * 16 + pr * 8 + m + 1)
                assert c[0] == JOB_STEPS

            with dve.Fori(0, NB) as j:
                job(j, j * BE, None)
            dve.wait_ge(jobs_ready, 1)
            n_jobs = dve.value_load(jobn[0:1, 0:1], min_val=NB, max_val=JOBS)
            with dve.If(n_jobs > NB):
                with dve.Fori(NB, n_jobs) as j:
                    e0 = dve.value_load(jobi[0:1, bass.ds(j, 1)], min_val=0, max_val=EXP - BE)
                    job(j, e0, jobtab[:, 1, bass.ds(j, 1)])
            f = [0]

            def flink(ins):
                f[0] += 1
                ins.then_inc(fin_order, 1)
                dve.wait_ge(fin_order, f[0])

            dve.wait_ge(gate_landed, 32)
            dve.wait_ge(gain_landed, 16)
            for t in range(TT):
                flink(V.tensor_tensor(acc[:, t, :], acc[:, t, :], gate2, ALU.mult))
                V.tensor_tensor(x1[:, t, :], x1[:, t, :], acc[:, t, :], ALU.add).then_inc(fin_sq_in, 1)
            for t in range(TT):
                dve.wait_ge(fin_sq, t + 1)
                V.tensor_scalar(rstd[:, t:t + 1], ss[:, t:t + 1], 1.0 / D, EPS, ALU.mult, ALU.add).then_inc(fin_var, 1)
                dve.wait_ge(fin_root, t + 1)
                flink(V.reciprocal(rstd[:, t:t + 1], rstd[:, 2 + t:3 + t]))
                V.scalar_tensor_tensor(acc[:, t, :], x1[:, t, :], rstd[:, t:t + 1], fgain, ALU.mult,
                                       ALU.mult).then_inc(fin_out, 1)


NAMES = ["x", "c", "w_ada", "b_ada", "norm1_g", "w_in", "conv_w", "conv_b", "conv_ln_g", "conv_ln_b", "ssm_a_re",
         "ssm_a_im", "ssm_b_re", "ssm_b_im", "ssm_c_re", "ssm_c_im", "ssm_d", "ssm_log_dt", "out_norm_conv_g",
         "out_norm_ssm_g", "w_out", "norm2_g", "router_group_w", "router_group_b", "router_expert_w",
         "router_expert_b", "exp_w_gate", "exp_w_up", "exp_w_down", "final_norm_g"]


def kernel(**inputs):
    import numpy as np
    import concourse.bacc as bacc
    from concourse.bass_utils import run_bass_kernel_spmd

    nc = bacc.Bacc("TRN2", target_bir_lowering=False, num_devices=1, dynamic_dma_scratch_size=1024)
    arrays, aps = {}, {}
    for name in NAMES:
        arr = np.ascontiguousarray(inputs[name])
        arrays[f"in_{name}"] = arr
        aps[name] = nc.dram_tensor(f"in_{name}", arr.shape, mybir.dt.from_np(arr.dtype), kind="ExternalInput").ap()
    out = nc.dram_tensor("out_x", [1, T, D], F32, kind="ExternalOutput").ap()
    trunk(nc, aps, out)
    got = run_bass_kernel_spmd(nc, [arrays], core_ids=[0])
    return got.results[0]["out_x"]
```

```python
import math
from contextlib import ExitStack

import concourse.bass as bass
from concourse import mybir

ALU = mybir.AluOpType
ACT = mybir.ActivationFunctionType
AX = mybir.AxisListType
F32 = mybir.dt.float32
I32 = mybir.dt.int32
U32 = mybir.dt.uint32

P = 128
D = 2048
T = 256
TT = T // P
KD = D // P
CH = 1024
CT_ = CH // P
TAPS = 31
PAD = TAPS - 1
G, HG, S = 64, 16, 64
PAIRS = G // 2
QUADS = PAIRS // 4
HALF = T // 2
NG, NE, F = 4, 8, 512
EXP = NG * NE
SLOTS = 64
BE = 4
NB = EXP // BE
JOBS = (T // SLOTS) * NB
N = 512
EPS = 1e-6
MAGIC = 1.5 * 2.0 ** 23
TWO_PI_DOWN = 6.283185
PI_DOWN = 3.1415925
C1 = 6.28125
C2 = 0.0019350051879882812
C3 = 2 * math.pi - C1 - C2

RING = 12
UNIT = 2048
A_UNITS, B_UNITS, C_UNITS, D_UNITS = 32, 96, 16, 48
B_ORDER = [8, 9, 10, 11, 0, 1, 2, 3, 4, 5, 6, 7]


def ring_use(n):
    if n < A_UNITS:
        return n % 8, n // 8
    r, s = divmod(n - A_UNITS, RING)
    s = B_ORDER[s]
    return s, r + (4 if s < 8 else 0)


D_BASE = A_UNITS + B_UNITS + C_UNITS
D_USES = [13 if s < 8 else 10 for s in range(RING)]

CHUNKS = [(2048, "u"), (1024, "gate"), (0, "value"), (1536, "gate"), (512, "value"), (2560, "u"),
          (3072, "out_gate"), (3584, "out_gate")]
FIRST_TILE = [0, 0, 0, 4, 4, 4, 0, 4]
U_CHUNKS, VALUE_CHUNKS = (0, 5), (2, 4)
ADA_PARTS = [2, 3, 4, 5]


DRIVE_AT = [4, 5, 7, 8, 24, 26, 28, 30]
READ_AT = [7, 8, 10, 11, 28, 30, 32, 34]
SUM_AT = [25, 27, 29]
SIDE_STEPS = 35


def side_jobs(g):
    return [("drive", q) for q in range(QUADS) if DRIVE_AT[q] == g] + \
        [("read", q) for q in range(QUADS) if READ_AT[q] == g] + \
        [("sum", n) for n in range(3) if SUM_AT[n] == g]


def tile_stored(q):
    return 2 * U_CHUNKS[q // 4] + (q % 4) // 2 + 1


def trunk(nc, a, out):
    ctx = ExitStack()
    with ctx:
        def sb(name, shape, dt=F32):
            return ctx.enter_context(nc.sbuf_tensor(name, shape, dt))

        def sem(name):
            return ctx.enter_context(nc.semaphore(name))

        ring = sb("ring", [P, RING, UNIT])
        KB = 256
        arena = sb("arena", [P, 122 * KB])

        def at(kb, words, parts=P):
            o = int(kb * KB)
            return arena[0:parts, o:o + words]

        hT = at(0, 16 * KB).rearrange("p (k t) -> p k t", k=KD)
        cosT = at(16, 16 * KB).rearrange("p (q t) -> p q t", q=PAIRS)
        sinT = at(32, 16 * KB).rearrange("p (q t) -> p q t", q=PAIRS)
        uT = at(48, 8 * KB).rearrange("p (c t) -> p c t", c=CT_)
        zT = at(56, CT_ * (PAD + T)).rearrange("p (c t) -> p c t", c=CT_)
        rot = at(66, 32 * KB).rearrange("p (b w r t) -> p b w r t", b=2, w=2, r=4)
        driveT = at(98, 8 * KB).rearrange("p (c q s) -> p c q s", c=2, q=QUADS)
        readT = at(106, 8 * KB).rearrange("p (c q s) -> p c q s", c=2, q=QUADS)
        apart = at(118, 4 * KB).rearrange("p (r t) -> p r t", r=4)
        vals = at(114, 4 * KB).rearrange("p (c t) -> p c t", c=4)
        sgT = at(56, 8 * KB).rearrange("p (c t) -> p c t", c=CT_)
        xr = at(66, 16 * KB).rearrange("p (t d) -> p t d", t=TT)
        bst = at(82, 16 * KB, 32).rearrange("p (c s) -> p c s", c=2)
        cst = at(48, 4 * KB).rearrange("p (c q s) -> p c q s", c=2, q=QUADS)
        cexp = at(52, 8 * KB).rearrange("p (c q g s) -> p c q g s", c=2, q=QUADS, g=2)
        cwst = at(60, 4 * KB, TAPS + 1)
        vst = at(64, P, 40)
        prm = at(98, 20 * P, 32).rearrange("p (n s) -> p n s", n=20)
        btmp = at(108, 4 * KB).rearrange("p (n f) -> p n f", n=2)
        bdiag = at(114, 8 * KB).rearrange("p (c r g h) -> p c r g h", c=2, r=PAIRS, g=2)
        conv = at(16, 8 * KB).rearrange("p (c t) -> p c t", c=CT_)
        sq = at(32, 8 * KB).rearrange("p (c t) -> p c t", c=CT_)
        stat = at(114, 2 * T).rearrange("p (n t) -> p n t", n=2)
        mean_w = at(116, P)
        csum = at(117, T)
        x1sq = at(24, N)
        x1T = at(0, 16 * KB).rearrange("p (k t) -> p k t", k=KD)
        x1 = at(66, 16 * KB).rearrange("p (t d) -> p t d", t=TT)
        gate1 = at(82, 8 * KB)
        gtmp = at(90, 4 * KB).rearrange("p (b n) -> p b n", b=2)
        xT = at(16, 16 * KB).rearrange("p (k t) -> p k t", k=KD)
        acc = at(32, 16 * KB).rearrange("p (t d) -> p t d", t=TT)
        yexp = at(48, 8 * KB).rearrange("p (n c) -> p n c", n=4)
        silu = at(56, 2 * KB)
        hid = at(58, 2 * KB)
        hidT = at(60, 2 * KB).rearrange("p (j s) -> p j s", j=4)
        onehot = at(0, 2 * KB).rearrange("p (x s) -> p x s", x=TT * BE)
        pick = at(62, 2 * KB).rearrange("p (t s) -> p t s", t=TT)
        wpick = at(64, 2 * KB).rearrange("p (t s) -> p t s", t=TT)
        junk = at(2, 2 * KB)
        wpickT = at(90, 2 * KB).rearrange("p (r t) -> p r t", r=2)
        gate2 = at(98, 8 * KB)
        fgain = at(106, 8 * KB)

        ident = sb("ident", [P, P])
        iota = sb("iota", [P, SLOTS])
        ccol = sb("ccol", [P, KD])
        g1 = sb("g1", [P, KD])
        g2 = sb("g2", [P, KD])
        mod = sb("mod", [P, 6, KD])
        own = sb("own", [P, 32])
        modrow = sb("modrow", [P, N])
        ss = sb("ss", [P, 8])
        rstd = sb("rstd", [P, 4])
        ldt = sb("ldt", [32, 2])
        dt = sb("dt", [32, 2])
        decay = sb("decay", [P, PAIRS])
        rot128 = sb("rot128", [P, 2, PAIRS])
        carry = sb("carry", [P, 3, 4, 2])
        vT = sb("vT", [P, 5, CT_])
        skip = sb("skip", [P, P])
        halfpi = sb("halfpi", [P, 1])
        eps = sb("eps", [P, 1])
        odd = sb("odd", [P, 2])
        cwT = at(65, 256).rearrange("p (c t) -> p c t", c=CT_)
        bada = at(64.5, 6 * KD).rearrange("p (m k) -> p m k", m=6)
        par = at(112, 4 * PAIRS).rearrange("p (n q) -> p n q", n=4)
        iota_i = at(112.5, P).bitcast(I32)
        steps = at(113, HALF)
        part_i = at(113.5, 1).bitcast(I32)
        place = [int(94 * KB)]

        def small(shape, dt_=F32, parts=P):
            words = math.prod(shape)
            v = arena[0:parts, place[0]:place[0] + words]
            place[0] += words
            if dt_ != F32:
                v = v.bitcast(dt_)
            if len(shape) == 2:
                v = v.rearrange("p (a b) -> p a b", a=shape[0])
            if len(shape) == 3:
                v = v.rearrange("p (a b c) -> p a b c", a=shape[0], b=shape[1])
            return v

        before = small([P])
        ones = small([P])
        lgT = small([T], parts=NG + EXP)
        sel = small([TT, 3, EXP])
        comb = small([TT, EXP])
        assert place[0] <= 98 * KB
        place = [int(92 * KB)]
        lg = small([TT, NG + EXP])
        gp = small([TT, 8])
        top = small([TT, 8])
        topi = small([TT, 8], U32)
        etop = small([TT, 8])
        etopi = small([TT, 8], U32)
        rt = small([TT, 16])
        rank = small([TT, EXP])
        rankc = small([TT, BE])
        counts = small([EXP])
        assert place[0] <= 94 * KB
        bada2 = at(110, 6 * KD).rearrange("p (m k) -> p m k", m=6)
        wr = at(98, KD * (NG + EXP)).rearrange("p (k e) -> p k e", k=KD)
        wrg = at(100.5, KD * NG).rearrange("p (k g) -> p k g", k=KD)
        wrb = at(103, KD * (NG + EXP)).rearrange("p (k e) -> p k e", k=KD)
        rbias = at(120.5, NG + EXP)
        ab_rows = at(121, P, 2 * KD)
        ab = at(121.5, 2 * KD)
        lbias = at(121.75, NG + EXP)
        wrbs = at(120.75, NG + EXP)
        wre = at(101, NG * KD * NE).rearrange("p (g k e) -> p g k e", g=NG, k=KD)
        jm = at(118, JOBS * JOBS).rearrange("p (j x) -> p j x", j=JOBS)
        jb = at(114, 6 * JOBS).rearrange("p (j x) -> p j x", j=6)
        jobtab = at(116, 2 * JOBS).rearrange("p (j x) -> p j x", j=2)
        jobi = at(116.5, JOBS, 1).bitcast(I32)
        jobn = at(117, 1, 1).bitcast(I32)

        ps = ctx.enter_context(nc.psum_tensor("ps", [P, 8, N], F32))

        ab_dram = nc.dram_tensor("scale_shift_scratch", [2, D], F32, kind="Internal").ap()
        gate_dram = nc.dram_tensor("gate_scratch", [2, D], F32, kind="Internal").ap()

        landed = [sem(f"unit_landed_{s}") for s in range(RING)]
        consumed = sem("units_consumed")
        x_landed = sem("x_landed")
        c_landed = sem("c_landed")
        setup_landed = sem("setup_landed")
        bada_landed = sem("ada_bias_landed")
        wr_landed = sem("router_weights_landed")
        late_landed = sem("late_setup_landed")
        consts_ready = sem("constants_ready")
        blocks_zero = sem("b_blocks_zeroed")
        token_consts = sem("token_sum_constants_ready")
        sum_consts = sem("sum_constants_ready")
        pool_order = sem("pool_order")
        vec_order = sem("vector_order")
        act_order = sem("scalar_order")
        x_squares = sem("x_squares")
        x_var = sem("x_variance")
        x_root = sem("x_root")
        x_rstd = sem("x_rstd")
        x_normed = sem("x_normed")
        x_turned = sem("x_turned")
        x_stored = sem("x_transposes_stored")
        c_silu = sem("c_silu")
        dt_ready = sem("dt_ready")
        decay_in = sem("decay_exponent_ready")
        decay_ready = sem("decay_ready")
        angle_in = sem("angle_reduced")
        angle_ready = sem("angle_sin_cos")
        params_ready = sem("ssm_params_ready")
        b_turned = sem("b_turned")
        cw_turned = sem("conv_weights_turned")
        cw_stored = sem("conv_weights_stored")
        params_turned = sem("ssm_params_turned")
        params_stored = sem("ssm_params_stored")
        bdiag_ready = sem("b_blocks_ready")
        cexp_ready = sem("c_blocks_ready")
        bc_turned = sem("b_c_blocks_turned")
        bc_stored = sem("b_c_blocks_stored")
        phase_ready = sem("table_phase_ready")
        table_sin = sem("table_sin_done")
        table_abs = sem("table_abs_done")
        tables_ready = sem("tables_ready")
        ada_done = sem("ada_part_done")
        ada_copied = sem("ada_part_copied")
        own_ready = sem("own_mask_ready")
        columns_ready = sem("mod_columns_ready")
        h_scaled = sem("h_scaled")
        h_ready = sem("h_ready")
        chunk_done = sem("chunk_done")
        chunk_stored = sem("chunk_bank_stored")
        z_ready = sem("z_tiles_ready")
        apart_zero = sem("pairs_apart_zeroed")
        apart_ready = sem("pairs_apart_ready")
        side_done = sem("side_bank_done")
        side_stored = sem("side_bank_stored")
        pads_ready = sem("conv_pads_ready")
        drive_done = sem("drive_done")
        drive_read = sem("drive_read")
        states_ready = sem("states_ready")
        skip_ready = sem("skip_diagonal_ready")
        conv_step = sem("conv_step")
        gated = sem("ssm_gated")
        squares = sem("squares_ready")
        reduced = sem("tiles_added")
        sums = sem("sums_done")
        sum_kept = sem("sums_kept")
        centred = sem("conv_centred")
        scaled = sem("conv_scaled")
        swished = sem("conv_swished")
        ys_ready = sem("ssm_normed")
        yc_ready = sem("conv_normed")
        gate_added = sem("gate_bias_added")
        gate_stored = sem("gate_in_dram")
        gate_landed = sem("gate_landed")
        gate2_landed = sem("gate2_landed")
        gain_landed = sem("final_gain_landed")
        x_again = sem("x_landed_again")
        out_done = sem("out_chunk_done")
        x1_ready = sem("x1_chunk_ready")
        x1_squares = sem("x1_squares")
        n2_var = sem("norm2_variance")
        n2_root = sem("norm2_root")
        n2_rstd = sem("norm2_rstd")
        ab_ready = sem("scale_shift_ready")
        ab_stored = sem("scale_shift_in_dram")
        ab_landed = sem("scale_shift_rows_landed")
        ab_turned = sem("scale_shift_turned")
        ab_kept = sem("scale_shift_by_channel")
        x1_turned = sem("x1_turned")
        x1_kept = sem("x1_transposes_stored")
        acc_ready = sem("acc_chunk_ready")
        weights_ready = sem("router_weights_scaled")
        lbias_done = sem("logit_bias_done")
        wr_ready = sem("router_weights_packed")
        logits_done = sem("logits_done")
        logits_biased = sem("logits_biased")
        logits_turned = sem("logits_turned")
        exp_in = sem("router_exp_in")
        exp_done = sem("router_exp_done")
        sel_ready = sem("selection_ready")
        rank_done = sem("rank_done")
        counts_ready = sem("counts_ready")
        jobs_ready = sem("jobs_ready")
        job_order = sem("vector_job_order")
        picks_ready = sem("picks_ready")
        wpicks_ready = sem("weighted_picks_ready")
        gathered = sem("tokens_gathered")
        tok_even = sem("tokens_even_stored")
        tok_odd = sem("tokens_odd_stored")
        picks_turned = sem("picks_turned")
        scatter_ready = sem("scatter_ready")
        gate_done = sem("expert_gate_done")
        gate_silu = sem("expert_gate_silu")
        up_done = sem("expert_up_done")
        hidden_ready = sem("hidden_ready")
        hidden_turned = sem("hidden_turned")
        hidden_stored = sem("hidden_stored")
        down_done = sem("down_done")
        down_stored = sem("down_stored")
        combined = sem("combined")
        added = sem("added")
        fin_sq = sem("final_squares")
        fin_var = sem("final_variance")
        fin_root = sem("final_root")
        fin_out = sem("final_rows_ready")
        out_landed = sem("out_landed")

        w_ada = a["w_ada"][0].rearrange("(p k) n -> k p n", k=KD)
        w_in = a["w_in"][0].rearrange("(p k) n -> p k n", k=KD)
        w_out = a["w_out"][0].rearrange("(k p) n -> p k n", p=P)
        w_gate = a["exp_w_gate"][0].rearrange("g e (p k) f -> (g e) p (k f)", k=KD)
        w_up = a["exp_w_up"][0].rearrange("g e (p k) f -> (g e) p (k f)", k=KD)
        w_down = a["exp_w_down"][0].rearrange("g e (j p) n -> (g e) p j n", p=P)

        def col(v):
            return v.rearrange("(p k) -> p k", k=KD)

        def b_unit(n):
            it, s = divmod(n, RING)
            u, kind = divmod(s, 3)
            if kind == 0:
                return ("in", it, u)
            m = it * 8 + 2 * u + kind - 1
            return ("ada", m // KD, m % KD)

        C_ORDER = [(n, q) for n in range(3) for q in (0, 1)] + [(n, q) for n in range(3) for q in (2, 3)] \
            + [(3, q) for q in range(4)]
        OUT_BANKS = [(0, 1), (4, 5), (2, 3), (0, 1)]

        block = ctx.enter_context(nc.Block())

        @block.sync
        def _(sp):
            sp.dma_start(ccol[:, :], col(a["c"][0])).then_inc(c_landed, 16)
            sp.dma_start(xr[:, 0, :], a["x"][0, 0:P, :]).then_inc(x_landed, 16)
            sp.dma_start(xr[:, 1, :], a["x"][0, P:T, :]).then_inc(x_landed, 16)
            last_user = {}

            def start(n, s, dst, src):
                if s in last_user:
                    sp.wait_ge(consumed, last_user[s] + 1)
                last_user[s] = n
                sp.dma_start(dst, src).then_inc(landed[s], 16)

            for n in range(A_UNITS):
                s, _u = ring_use(n)
                part, k = (1, 0)[n // KD], n % KD
                start(n, s, ring[:, s, :], w_ada[k, :, part * D:(part + 1) * D])
            for m in range(B_UNITS):
                n = A_UNITS + m
                s, _u = ring_use(n)
                kind, i, k = b_unit(m)
                if kind == "in":
                    c0 = CHUNKS[i][0]
                    start(n, s, ring[:, s, :].rearrange("p (k n) -> p k n", k=4),
                          w_in[:, 4 * k:4 * k + 4, c0:c0 + N])
                else:
                    c0 = ADA_PARTS[i] * D
                    start(n, s, ring[:, s, :], w_ada[k, :, c0:c0 + D])
            for m in range(C_UNITS):
                n = A_UNITS + B_UNITS + m
                s, _u = ring_use(n)
                c, q = C_ORDER[m]
                if m == 8:
                    sp.wait_ge(side_done, QUADS)
                    sp.dma_start(x1, a["x"][0].rearrange("(t p) d -> p t d", p=P)).then_inc(x_again, 16)
                start(n, s, ring[:, s, :].rearrange("p (k n) -> p k n", k=4),
                      w_out[:, 4 * q:4 * q + 4, c * N:(c + 1) * N])

            def job_units(j, e0):
                m = 0
                for pr in range(2):
                    for stage in range(3):
                        for u in range(4):
                            for x in range(2):
                                s = m % RING
                                e = e0 + (2 * pr + x)
                                sp.wait_ge(consumed, j * D_UNITS + (D_BASE + m - RING + 1))
                                if stage < 2:
                                    w = (w_gate, w_up)[stage]
                                    src = w[bass.ds(e, 1), :, u * UNIT:(u + 1) * UNIT].rearrange("e p n -> (e p) n")
                                    dst = ring[:, s, :]
                                else:
                                    src = w_down[bass.ds(e, 1), :, :, u * N:(u + 1) * N].rearrange("e p j n -> (e p) j n")
                                    dst = ring[:, s, :].rearrange("p (j n) -> p j n", j=4)
                                sp.dma_start(dst, src).then_inc(landed[s], 16)
                                m += 1

            with sp.Fori(0, NB) as j:
                job_units(j, j * BE)
            sp.wait_ge(jobs_ready, 1)
            n_jobs = sp.value_load(jobn[0:1, 0:1], min_val=NB, max_val=JOBS)
            with sp.If(n_jobs > NB):
                with sp.Fori(NB, n_jobs) as j:
                    e0 = sp.value_load(jobi[0:1, bass.ds(j, 1)], min_val=0, max_val=EXP - BE)
                    job_units(j, e0)
            for n in range(2 * TT):
                t, h = divmod(n, 2)
                cc = slice(h * D // 2, (h + 1) * D // 2)
                sp.wait_ge(fin_out, n + 1)
                sp.dma_start(out[0, t * P:(t + 1) * P, cc], acc[:, t, cc]).then_inc(out_landed, 16)
            sp.wait_ge(out_landed, 16 * 2 * TT)

        @block.tensor
        def _(pe):
            mm = nc.tensor.matmul

            def tr(dst, src, k):
                return nc.tensor.transpose(dst, src, ident[0:k, 0:k])

            def ada_unit(n, bank, k):
                s, u = ring_use(n)
                pe.wait_ge(landed[s], 16 * (u + 1))
                for j in range(4):
                    last = mm(ps[32 * j:32 * j + 32, bank, :], ccol[:, k:k + 1].to_broadcast([P, 32]), ring[:, s, j * N:(j + 1) * N],
                              start=(k == 0), stop=(k == KD - 1), skip_group_check=True)
                return last

            def turn_x(b):
                for k in (2 * b, 2 * b + 1):
                    for t in range(TT):
                        pe.wait_ge(x_normed, t + 1)
                        if b >= 4:
                            pe.wait_ge(x_stored, b - 3)
                        o = (k % 2) * T + t * P
                        last = tr(ps[:, 4 + b % 4, o:o + P], xr[:, t, k:D:KD], P)
                last.then_inc(x_turned, 1)

            pe.wait_ge(c_silu, 1)
            for k in range(KD):
                ada_unit(k, 0, k).then_inc(consumed, 1)
                if k == 0:
                    pe.wait_ge(consts_ready, 1)
                if 4 <= k < 12:
                    turn_x(k - 4)
            pe.drain().then_inc(ada_done, 1)
            pe.wait_ge(setup_landed, 16 * 14)
            for c in range(CT_):
                tr(ps[:, 2, c * 32:(c + 1) * 32], cwst[:, c * P:(c + 1) * P], 32)
            tr(ps[:, 2, 256:296], vst, 40).then_inc(cw_turned, 1)
            pe.wait_ge(x_stored, 8)
            for c in range(2):
                for h in range(HG):
                    last = tr(ps[:, 4 + c, h * 32:(h + 1) * 32],
                              bst[:, c, :].rearrange("p (s h) -> p h s", h=HG)[:, h, :], 32)
            last.then_inc(b_turned, 1)
            for k in range(KD):
                ada_unit(KD + k, 1, k).then_inc(consumed, 1)
                if k == 0:
                    pe.wait_ge(params_ready, 1)
                    for i, slot in enumerate((6, 10, 15, 16)):
                        last = tr(ps[:, 3, i * 32:(i + 1) * 32], prm[:, slot, :], 32)
                    last.then_inc(params_turned, 1)
                if k >= 8:
                    pe.wait_ge(bdiag_ready, 1)
                    pe.wait_ge(cexp_ready, 1)
                    b = k - 8
                    for q in range(4):
                        c, qq = (b % 4) // 2, (b % 2) * 4 + q
                        if b < 4:
                            src = bdiag[:, c, :, :, :].rearrange("p r g h -> p (r g h)")[:, qq * P:(qq + 1) * P]
                        else:
                            src = cexp[:, c, qq, :, :].rearrange("p g s -> p (g s)")
                        if b >= 4:
                            pe.wait_ge(bc_stored, b - 3)
                        last = tr(ps[:, 4 + b % 4, q * P:(q + 1) * P], src, P)
                    last.then_inc(bc_turned, 1)
            pe.drain().then_inc(ada_done, 1)

            def channel_sum(n):
                pe.wait_ge(sum_consts, 1)
                pe.wait_ge(reduced, n + 1)
                if n < 3:
                    pe.wait_ge(side_stored, sum(g < SUM_AT[n] for g in READ_AT))
                    if n:
                        pe.wait_ge(sum_kept, n)
                else:
                    pe.wait_ge(drive_read, QUADS)
                mm(ps[:, 3 if n < 3 else 7, 0:T], mean_w, csum, start=True, stop=True).then_inc(sums, 1)

            def side(g):
                for job, q in side_jobs(g):
                    if job == "drive":
                        pe.wait_ge(apart_ready, 4 * (q + 1))
                        pe.wait_ge(bc_stored, 8)
                        if q:
                            pe.wait_ge(drive_read, q)
                        for c in range(2):
                            for r in range(4):
                                last = mm(ps[:, 4 + r, c * T:(c + 1) * T], driveT[:, c, q, :], apart[:, r, :],
                                          start=True, stop=True)
                        last.then_inc(drive_done, 1)
                    elif job == "read":
                        if q:
                            pe.wait_ge(side_stored, q)
                        if READ_AT[q] > SUM_AT[0]:
                            pe.wait_ge(sum_kept, sum(g < READ_AT[q] for g in SUM_AT))
                        pe.wait_ge(states_ready, q + 1)
                        pe.wait_ge(skip_ready, q + 1)
                        b = q % 2
                        mm(ps[:, 3, 0:T], skip[:, :], uT[:, q, :], start=True, stop=False, skip_group_check=True)
                        for c, w, x in ((0, 0, 0), (0, 1, 1), (1, 0, 1), (1, 1, 0)):
                            for r in range(4):
                                last = mm(ps[32 * r:32 * r + 32, 3, 0:T], readT[:, c, q, 32 * r:32 * r + 32],
                                          rot[:, b, w, r, x * T:(x + 1) * T], start=False,
                                          stop=(c == 1 and w == 1), skip_group_check=True)
                        last.then_inc(side_done, 1)
                    else:
                        channel_sum(q)

            for it in range(8):
                for u in range(4):
                    for kind in range(3):
                        n = A_UNITS + it * RING + 3 * u + kind
                        s, use = ring_use(n)
                        if kind == 0:
                            pe.wait_ge(landed[s], 16 * (use + 1))
                            for kk in range(4):
                                k = 4 * u + kk
                                if it == 0:
                                    pe.wait_ge(h_ready, k + 1)
                                for j in range(4):
                                    if k == 0 and it > 0 and j % 2 == 0:
                                        pe.wait_ge(chunk_stored, 2 * it - 1 + j // 2)
                                    last = mm(ps[:, j // 2, (j % 2) * T:(j % 2 + 1) * T],
                                              ring[:, s, kk * N + j * P:kk * N + (j + 1) * P], hT[:, k, :],
                                              start=(k == 0 and j % 2 == 0), stop=(k == KD - 1), skip_group_check=True)
                            last.then_inc(consumed, 1)
                            if u == 3:
                                pe.drain().then_inc(chunk_done, 1)
                        else:
                            m = it * 8 + 2 * u + kind - 1
                            if m % KD == 0:
                                if m:
                                    pe.wait_ge(ada_copied, m // KD)
                                else:
                                    pe.wait_ge(cw_stored, 1)
                            ada_unit(n, 2, m % KD).then_inc(consumed, 1)
                            if m % KD == KD - 1:
                                pe.drain().then_inc(ada_done, 1)
                    side(4 * it + u)
            side(32)

            def out_units(ms):
                for m in ms:
                    c, q = C_ORDER[m]
                    s, use = ring_use(A_UNITS + B_UNITS + m)
                    pe.wait_ge(landed[s], 16 * (use + 1))
                    src, k0 = (uT, 4 * q - 8) if q >= 2 else (conv, 4 * q)
                    if m == 0:
                        pe.wait_ge(chunk_stored, 16)
                        pe.wait_ge(ada_copied, 4)
                        pe.wait_ge(yc_ready, CT_)
                    if m == 4:
                        pe.wait_ge(side_stored, QUADS)
                        pe.wait_ge(sum_kept, 3)
                    if m == 6:
                        pe.wait_ge(ys_ready, CT_)
                    for kk in range(4):
                        for t in range(TT):
                            if m == 12 and kk == 0:
                                pe.wait_ge(x1_ready, t + 1)
                            first = q == 0 and kk == 0
                            end = q == 3 and kk == 3
                            last = mm(ps[:, OUT_BANKS[c][t], :], src[:, k0 + kk, t * P:(t + 1) * P],
                                      ring[:, s, kk * N:(kk + 1) * N], start=first, stop=end, skip_group_check=True)
                    last.then_inc(consumed, 1)
                    if q == 3:
                        pe.drain().then_inc(out_done, 1)

            def turn_x1(n):
                pe.wait_ge(x1_ready, 2 * n + 2)
                for h in range(2):
                    if n or h:
                        pe.wait_ge(x1_kept, 2 * n + h - 1) if n else pe.wait_ge(ab_kept, 1)
                    for i in range(2):
                        k = 4 * n + 2 * h + i
                        for t in range(TT):
                            last = tr(ps[:, 6 + h, i * T + t * P:i * T + (t + 1) * P], x1[:, t, k * P:(k + 1) * P], P)
                    last.then_inc(x1_turned, 1)

            def logits(n):
                for k in range(4 * n, 4 * n + 4):
                    pe.wait_ge(x1_kept, k // 2 + 1)
                    last = mm(ps[0:NG + EXP, 4, 0:T], wr[:, k, :], x1T[:, k, :], start=(k == 0), stop=(k == KD - 1),
                              skip_group_check=True)
                return last

            out_units([0])
            side(33)
            out_units([1])
            side(34)
            out_units([2, 3])
            channel_sum(3)
            out_units(range(4, 10))
            pe.wait_ge(ab_landed, 16)
            tr(ps[:, 7, 0:2 * KD], ab_rows, 2 * KD).then_inc(ab_turned, 1)
            turn_x1(0)
            out_units([10, 11])
            turn_x1(1)
            out_units([12, 13])
            turn_x1(2)
            pe.wait_ge(weights_ready, 1)
            pe.wait_ge(token_consts, 1)
            mm(ps[:, 5, 0:NG + EXP], ones, wrbs, start=True, stop=True).then_inc(lbias_done, 1)
            logits(0)
            logits(1)
            out_units([14, 15])
            logits(2)
            turn_x1(3)
            logits(3).then_inc(logits_done, 1)
            pe.wait_ge(logits_biased, 1)
            for t in range(TT):
                last = tr(ps[:, 1, t * 64:t * 64 + NG + EXP], lgT[:, t * P:(t + 1) * P], NG + EXP)
            last.then_inc(logits_turned, 1)
            pe.wait_ge(sel_ready, 1)
            mm(ps[:, 2, 0:EXP], before, sel[:, 0, 2, :], start=True, stop=True)
            mm(ps[:, 2, EXP:2 * EXP], before, sel[:, 1, 2, :], start=True, stop=False)
            mm(ps[:, 2, EXP:2 * EXP], ones, sel[:, 0, 2, :], start=False, stop=True)
            mm(ps[:, 2, 2 * EXP:3 * EXP], ones, sel[:, 0, 2, :], start=True, stop=False)
            mm(ps[:, 2, 2 * EXP:3 * EXP], ones, sel[:, 1, 2, :], start=False, stop=True).then_inc(rank_done, 1)

            def job(j):
                def gather(u):
                    for k in range(4 * u, 4 * u + 4):
                        if k >= 2:
                            pe.wait_ge((tok_even, tok_odd)[k % 2], j * 8 + k // 2)
                        for t in range(TT):
                            last = mm(ps[:, 4 + k % 2, 0:T], x1[:, t, k:D:KD], pick[:, t, :], start=(t == 0), stop=(t == 1))
                        last.then_inc(gathered, 1)

                pe.wait_ge(picks_ready, j + 1)
                gather(0)
                m = 0
                for pr in range(2):
                    for stage in range(3):
                        if stage == 2:
                            pe.wait_ge(hidden_ready, j * 2 + pr + 1)
                            for i in range(4):
                                last = tr(ps[:, 4 + pr, i * P:(i + 1) * P], hid[:, i * P:(i + 1) * P], P)
                            last.then_inc(hidden_turned, 1)
                            pe.wait_ge(hidden_stored, j * 2 + pr + 1)

                        def combine(n):
                            pe.wait_ge(down_stored, j * 8 + pr * 4 + n + 1)
                            if n == 0 and pr == 0:
                                pe.wait_ge(scatter_ready, j + 1)
                            for t in range(TT):
                                if n or pr:
                                    pe.wait_ge(added, j * 16 + pr * 8 + 2 * n + t - 1)
                                mm(ps[:, 6 + t, :], wpickT[:, pr, t * P:(t + 1) * P], yexp[:, n, :],
                                   start=True, stop=True).then_inc(combined, 1)

                        for u in range(4):
                            if pr == 0 and stage == 0:
                                if u < 3:
                                    gather(u + 1)
                                else:
                                    pe.wait_ge(wpicks_ready, j + 1)
                                    pe.wait_ge(added, j * 16)
                                    for p2 in range(2):
                                        for t in range(TT):
                                            last = tr(ps[:, 6 + p2, t * P:(t + 1) * P], wpick[:, t, p2 * P:(p2 + 1) * P], P)
                                    last.then_inc(picks_turned, 1)
                                pe.wait_ge(tok_even, j * 8 + 2 * u + 2)
                                pe.wait_ge(tok_odd, j * 8 + 2 * u + 2)
                            for x in range(2):
                                s = m % RING
                                pe.wait_ge(landed[s], j * 64 + 16 * (D_USES[s] + m // RING + 1))
                                half = slice(64 * x, 64 * x + 64)
                                for kk in range(4):
                                    if stage < 2:
                                        k = 4 * u + kk
                                        slot = (2 * pr + x) * SLOTS
                                        last = mm(ps[half, stage, :], xT[:, k, slot:slot + SLOTS],
                                                  ring[:, s, kk * N:(kk + 1) * N], start=(k == 0),
                                                  stop=(k == KD - 1), skip_group_check=True)
                                    else:
                                        last = mm(ps[half, 2 + u % 2, :], hidT[:, kk, half],
                                                  ring[:, s, kk * N:(kk + 1) * N], start=(kk == 0),
                                                  stop=(kk == 3), skip_group_check=True)
                                last.then_inc(consumed, 1)
                                m += 1
                            if stage == 2:
                                pe.drain().then_inc(down_done, 1)
                                if u >= 1:
                                    combine(u - 1)
                        if stage < 2:
                            pe.drain().then_inc((gate_done, up_done)[stage], 1)
                        else:
                            combine(3)

            with pe.Fori(0, NB) as j:
                job(j)
            pe.wait_ge(jobs_ready, 1)
            n_jobs = pe.value_load(jobn[0:1, 0:1], min_val=NB, max_val=JOBS)
            with pe.If(n_jobs > NB):
                with pe.Fori(NB, n_jobs) as j:
                    job(j)

        @block.scalar
        def _(act):
            A = nc.scalar.activation
            for dst, src in (
                (ldt[:, :], a["ssm_log_dt"][0].rearrange("(r g) -> r g", g=2)),
                (prm[:, 0, :], a["ssm_a_re"][0].rearrange("(r g) s -> r (g s)", g=2)),
                (prm[:, 1, :], a["ssm_a_im"][0].rearrange("(r g) s -> r (g s)", g=2)),
                (bst[:, 0, :], a["ssm_b_re"][0].rearrange("(r g) s h -> r (g s h)", g=2)),
                (bst[:, 1, :], a["ssm_b_im"][0].rearrange("(r g) s h -> r (g s h)", g=2)),
                (cst[:, 0, :, :], a["ssm_c_re"][0].rearrange("(q g) h s -> (g h) q s", q=QUADS)),
                (cst[:, 1, :, :], a["ssm_c_im"][0].rearrange("(q g) h s -> (g h) q s", q=QUADS)),
                (cwst[0:TAPS, :], a["conv_w"][0]),
                (cwst[TAPS:TAPS + 1, :], a["conv_b"]),
                (vst[0:8, :], a["conv_ln_g"][0].rearrange("(c p) -> c p", p=P)),
                (vst[8:16, :], a["conv_ln_b"][0].rearrange("(c p) -> c p", p=P)),
                (vst[16:24, :], a["out_norm_conv_g"][0].rearrange("(c p) -> c p", p=P)),
                (vst[24:32, :], a["out_norm_ssm_g"][0].rearrange("(c p) -> c p", p=P)),
                (vst[32:40, :], a["ssm_d"][0].rearrange("(c p) -> c p", p=P)),
            ):
                act.dma_start(dst, src).then_inc(setup_landed, 16)
            for dst, src in (
                (g1[:, :], col(a["norm1_g"][0])),
                (g2[:, :], col(a["norm2_g"][0])),
                (bada[:, :, :], a["b_ada"][0].rearrange("(m p k) -> p m k", m=6, k=KD)),
            ):
                act.dma_start(dst, src).then_inc(late_landed, 16)

            act.wait_ge(c_landed, 16)
            A(ccol[:, :], ccol[:, :], ACT.Silu).then_inc(c_silu, 1)
            for t in range(TT):
                act.wait_ge(x_landed, 16 * TT)
                A(ring[:, 8 + t, :], xr[:, t, :], ACT.Square, accum_out=ss[:, t:t + 1]).then_inc(x_squares, 1)
            act.wait_ge(x_var, 1)
            A(rstd[:, 2:4], rstd[:, 0:2], ACT.Sqrt).then_inc(x_root, 1)
            for b in range(8):
                act.wait_ge(x_turned, b + 1)
                nc.scalar.copy(hT[:, 2 * b:2 * b + 2, :].rearrange("p k t -> p (k t)"),
                               ps[:, 4 + b % 4, :]).then_inc(x_stored, 1)
            act.wait_ge(setup_landed, 16 * 14)
            A(dt[:, :], ldt[:, :], ACT.Exp).then_inc(dt_ready, 1)
            act.wait_ge(decay_in, 1)
            A(prm[:, 6, :], prm[:, 2, :], ACT.Exp).then_inc(decay_ready, 1)
            act.wait_ge(angle_in, 1)
            A(prm[:, 7, :], prm[:, 5, :], ACT.Sin).then_inc(angle_ready, 1)
            A(prm[:, 9, :], prm[:, 5, :], ACT.Abs).then_inc(angle_ready, 1)
            act.wait_ge(angle_ready, 2)
            A(prm[:, 8, :], prm[:, 9, :], ACT.Sin, scale=-1.0, bias=halfpi[0:32, :]).then_inc(angle_ready, 1)
            def ada_copy(n):
                act.wait_ge(ada_done, n + 3)
                if n:
                    act.wait_ge(columns_ready, n)
                nc.scalar.copy(modrow[:, :], ps[:, 2, :]).then_inc(ada_copied, 1)

            act.wait_ge(phase_ready, 1)
            for b in range(8):
                c, q = (b % 4) // 2, (b % 2) * 4
                act.wait_ge(bc_turned, b + 1)
                dst = (driveT if b < 4 else readT)[:, c, q:q + 4, :].rearrange("p q s -> p (q s)")
                nc.scalar.copy(dst, ps[:, 4 + b % 4, :]).then_inc(bc_stored, 1)

            A(sinT, cosT, ACT.Sin, scale=TWO_PI_DOWN).then_inc(table_sin, 1)
            A(rot128[:, 1, :], rot128[:, 0, :], ACT.Sin, scale=TWO_PI_DOWN).then_inc(table_sin, 1)
            act.wait_ge(table_sin, 2)
            A(cosT, cosT, ACT.Abs).then_inc(table_abs, 1)
            A(rot128[:, 0, :], rot128[:, 0, :], ACT.Abs).then_inc(table_abs, 1)
            act.wait_ge(table_abs, 2)
            A(cosT, cosT, ACT.Sin, scale=-TWO_PI_DOWN, bias=halfpi[:, :]).then_inc(tables_ready, 1)
            A(rot128[:, 0, :], rot128[:, 0, :], ACT.Sin, scale=-TWO_PI_DOWN, bias=halfpi[:, :]).then_inc(tables_ready, 1)
            act.wait_ge(pads_ready, 1)
            KIND = {"u": (ACT.Copy, uT), "gate": (ACT.Sigmoid, zT[:, :, PAD:]), "value": (ACT.Copy, vals),
                    "out_gate": (ACT.Sigmoid, sgT)}
            for g in range(SIDE_STEPS):
                it, u = divmod(g, 4)
                if u == 3 and it < 8:
                    act.wait_ge(chunk_done, it + 1)
                    func, dst = KIND[CHUNKS[it][1]]
                    if it == VALUE_CHUNKS[1]:
                        act.wait_ge(z_ready, 1)
                    if it == 6:
                        act.wait_ge(conv_step, CT_ * TAPS)
                    for b in range(2):
                        c = (0 if CHUNKS[it][1] == "value" else FIRST_TILE[it]) + 2 * b
                        A(dst[:, c:c + 2, :], ps[:, b, :].rearrange("p (c t) -> p c t", c=2), func).then_inc(chunk_stored, 1)
                    if it % 2:
                        ada_copy(it // 2)
                for job, q in side_jobs(g):
                    if job == "read":
                        act.wait_ge(side_done, q + 1)
                        A(uT[:, q, :], ps[:, 3, 0:T], ACT.Gelu_apprx_tanh).then_inc(side_stored, 1)
                    if job == "sum":
                        act.wait_ge(sums, q + 1)
                        if q == 0:
                            nc.scalar.copy(stat[:, 0, :], ps[:, 3, 0:T]).then_inc(sum_kept, 1)
                        else:
                            if q == 2:
                                act.wait_ge(centred, 1)
                            A(stat[:, q % 2, :], ps[:, 3, 0:T], ACT.Sqrt, bias=eps[:, :]).then_inc(sum_kept, 1)
                if g + 1 in DRIVE_AT:
                    q = DRIVE_AT.index(g + 1)
                    act.wait_ge(apart_zero, 1)
                    act.wait_ge(chunk_stored, tile_stored(q))
                    if q:
                        act.wait_ge(drive_done, q)
                    for r in range(4):
                        rr = slice(32 * r, 32 * r + 32)
                        nc.scalar.copy(apart[rr, r, :], uT[rr, q, :]).then_inc(apart_ready, 1)
                if g == SUM_AT[0] + 1:
                    act.wait_ge(centred, 1)
                    A(sq, conv, ACT.Square).then_inc(squares, 1)
                if g == SUM_AT[1] + 1:
                    act.wait_ge(scaled, 1)
                    for c in range(CT_):
                        A(conv[:, c, :], conv[:, c, :], ACT.Silu, scale=vT[:, 0, c:c + 1],
                          bias=vT[:, 1, c:c + 1]).then_inc(swished, 1)
                    act.wait_ge(swished, CT_)
                    A(sq, conv, ACT.Square).then_inc(squares, 1)

            act.dma_start(bada2, a["b_ada"][0].rearrange("(m p k) -> p m k", m=6, k=KD)).then_inc(bada_landed, 16)
            for dst, src in (
                (wrg, a["router_group_w"][0].rearrange("(k p) g -> p k g", k=KD)),
                (wre[:, 0], a["router_expert_w"][0, 0].rearrange("(k p) e -> p k e", k=KD)),
                (wre[:, 1], a["router_expert_w"][0, 1].rearrange("(k p) e -> p k e", k=KD)),
                (wre[:, 2], a["router_expert_w"][0, 2].rearrange("(k p) e -> p k e", k=KD)),
                (wre[:, 3], a["router_expert_w"][0, 3].rearrange("(k p) e -> p k e", k=KD)),
                (rbias[:, 0:NG], a["router_group_b"].to_broadcast([P, NG])),
                (rbias[:, NG:], a["router_expert_b"].rearrange("o g e -> o (g e)").to_broadcast([P, EXP])),
            ):
                act.dma_start(dst, src).then_inc(wr_landed, 16)
            act.wait_ge(gated, 1)
            A(sq, uT, ACT.Square).then_inc(squares, 1)
            act.wait_ge(gate_added, 1)
            act.dma_start(col(gate_dram[0]), mod[:, 2, :]).then_inc(gate_stored, 16)
            act.wait_ge(sums, 4)
            act.wait_ge(scaled, 1)
            A(stat[:, 1, :], ps[:, 7, 0:T], ACT.Sqrt, bias=eps[:, :]).then_inc(sum_kept, 1)
            act.wait_ge(gate_stored, 16)
            act.dma_start(gate1, gate_dram[0:1, :].to_broadcast([P, D])).then_inc(gate_landed, 16)
            act.wait_ge(ab_ready, 1)
            for i, part in enumerate((4, 3)):
                act.dma_start(col(ab_dram[i]), mod[:, part, :]).then_inc(ab_stored, 16)
            act.wait_ge(gate_added, 2)
            act.dma_start(col(gate_dram[1]), mod[:, 5, :]).then_inc(gate_stored, 16)
            act.wait_ge(ab_stored, 32)
            act.dma_start(ab_rows, ab_dram.rearrange("i (k p) -> (i k) p", p=P)).then_inc(ab_landed, 16)

            def turned(n, h):
                act.wait_ge(x1_turned, 2 * n + h + 1)
                nc.scalar.copy(x1T[:, 4 * n + 2 * h:4 * n + 2 * h + 2, :].rearrange("p k t -> p (k t)"),
                               ps[:, 6 + h, :]).then_inc(x1_kept, 1)

            for n in range(8):
                c, t = divmod(n, 2)
                act.wait_ge(x1_ready, n + 1)
                if n:
                    act.wait_ge(x1_squares, n)
                A(x1sq, x1[:, t, c * N:(c + 1) * N], ACT.Square,
                  accum_out=ss[:, t * 4 + c:t * 4 + c + 1]).then_inc(x1_squares, 1)
                if t == 1 and c < 3:
                    for t2 in range(TT):
                        nc.scalar.copy(acc[:, t2, c * N:(c + 1) * N], x1[:, t2, c * N:(c + 1) * N]).then_inc(acc_ready, 1)
                    for h in range(2):
                        turned(c, h)
            act.wait_ge(n2_var, 1)
            A(rstd[:, 2:4], rstd[:, 0:2], ACT.Sqrt).then_inc(n2_root, 1)
            for h in range(2):
                turned(3, h)
            act.wait_ge(logits_done, 1)
            nc.scalar.copy(lgT[:, :], ps[0:NG + EXP, 4, 0:T]).then_inc(logits_biased, 1)
            for t2 in range(TT):
                nc.scalar.copy(acc[:, t2, 3 * N:], x1[:, t2, 3 * N:]).then_inc(acc_ready, 1)
            act.wait_ge(gate_stored, 32)
            act.dma_start(gate2, gate_dram[1:2, :].to_broadcast([P, D])).then_inc(gate2_landed, 16)
            act.dma_start(fgain, a["final_norm_g"].rearrange("(o d) -> o d", o=1).to_broadcast([P, D])).then_inc(gain_landed, 16)
            act.wait_ge(exp_in, 1)
            A(rt[:, :, 0:4], rt[:, :, 0:4], ACT.Exp).then_inc(exp_done, 1)
            act.wait_ge(exp_in, 2)
            A(rt[:, :, 6:7], rt[:, :, 5:6], ACT.Exp).then_inc(exp_done, 1)

            def job(j):
                for k in range(1, KD, 2):
                    act.wait_ge(gathered, j * KD + k + 1)
                    A(xT[:, k, :], ps[:, 5, 0:T], ACT.Identity, scale=mod[:, 4, k:k + 1],
                      bias=mod[:, 3, k:k + 1]).then_inc(tok_odd, 1)
                for pr in range(2):
                    act.wait_ge(gate_done, j * 2 + pr + 1)
                    A(silu, ps[:, 0, :], ACT.Silu).then_inc(gate_silu, 1)
                    act.wait_ge(hidden_turned, j * 2 + pr + 1)
                    nc.scalar.copy(hidT.rearrange("p j s -> p (j s)"), ps[:, 4 + pr, :]).then_inc(hidden_stored, 1)
                for m in range(8):
                    n, t = divmod(m, 2)
                    act.wait_ge(added, j * 16 + 8 + m + 1)
                    act.wait_ge(fin_sq, j * 8 + m)
                    A(junk, acc[:, t, n * N:(n + 1) * N], ACT.Square, accum_out=ss[:, t * 4 + n:t * 4 + n + 1]).then_inc(fin_sq, 1)

            with act.Fori(0, NB) as j:
                job(j)
            act.wait_ge(jobs_ready, 1)
            n_jobs = act.value_load(jobn[0:1, 0:1], min_val=NB, max_val=JOBS)
            with act.If(n_jobs > NB):
                with act.Fori(NB, n_jobs) as j:
                    job(j)
            act.wait_ge(fin_var, 1)
            A(rstd[:, 2:4], rstd[:, 0:2], ACT.Sqrt).then_inc(fin_root, 1)

        @block.gpsimd
        def _(pool):
            gp_ = nc.gpsimd
            n = [0]

            def link(ins):
                n[0] += 1
                ins.then_inc(pool_order, 1)
                pool.wait_ge(pool_order, n[0])

            link(gp_.memset(ident[:, :], 0.0))
            link(gp_.affine_select(out=ident[:, :], in_=ident[:, :], compare_op=ALU.not_equal, fill=1.0, base=0,
                                   pattern=[[-1, P]], channel_multiplier=1))
            link(gp_.iota(iota_i, pattern=[[1, P]], base=0, channel_multiplier=0))
            link(gp_.iota(part_i, pattern=[[0, 1]], base=0, channel_multiplier=1))
            link(gp_.memset(halfpi[:, :], math.pi / 2))
            gp_.memset(eps[:, :], EPS).then_inc(consts_ready, 1)
            gp_.memset(at(114, 8 * KB), 0.0).then_inc(blocks_zero, 1)

            def diagonal(q):
                if q:
                    pool.wait_ge(side_done, q)
                gp_.tensor_scalar(skip[:, :], ident[:, :], vT[:, 4, q:q + 1], None, ALU.mult).then_inc(skip_ready, 1)

            def columns(n):
                pool.wait_ge(ada_copied, n + 1)
                row = modrow[:, :].rearrange("p (i k) -> p i k", k=KD)
                link(gp_.tensor_tensor(row, row, own[:, :].unsqueeze(2).to_broadcast([P, 32, KD]), ALU.mult))
                w = 16
                while w > 1:
                    link(gp_.tensor_tensor(row[:, 0:w, :], row[:, 0:w, :], row[:, w:2 * w, :], ALU.add))
                    w //= 2
                gp_.tensor_tensor(mod[:, ADA_PARTS[n], :], row[:, 0, :], row[:, 1, :], ALU.add).then_inc(columns_ready, 1)

            pool.wait_ge(own_ready, 1)
            pool.wait_ge(cw_stored, 1)
            def z_tiles(h):
                pool.wait_ge(chunk_stored, 2 * VALUE_CHUNKS[h] + 2)
                z = zT[:, 4 * h:4 * h + 4, PAD:]
                return gp_.tensor_tensor(z, z, vals, ALU.mult).then_inc(z_ready, 1)

            pool.wait_ge(bc_turned, 8)
            gp_.memset(apart, 0.0).then_inc(apart_zero, 1)
            for q in range(5):
                diagonal(q)
                if q == 2:
                    columns(0)
            z_tiles(0)
            columns(1)
            z_tiles(1)
            pool.wait_ge(z_ready, 2)
            gp_.memset(mean_w, 1.0 / CH).then_inc(sum_consts, 1)
            columns(2)
            for q in range(5, QUADS):
                diagonal(q)
            columns(3)
            pool.wait_ge(side_done, QUADS)
            link(gp_.memset(ones, 1.0))
            gp_.affine_select(out=before, in_=ones, compare_op=ALU.is_gt, fill=0.0, base=0,
                              pattern=[[1, P]], channel_multiplier=-1).then_inc(token_consts, 1)
            pool.wait_ge(wr_landed, 16 * 7)
            gp_.tensor_copy(wr[:, :, 0:NG], wrg[:, :, :]).then_inc(wr_ready, 1)
            gp_.tensor_copy(wr[:, :, NG:].rearrange("p k (g e) -> p g k e", g=NG), wre[:, :, :, :]).then_inc(wr_ready, 1)

            pool.wait_ge(counts_ready, 1)
            rounds = JOBS // NB
            most, flag, pos, e0, r0 = (jb[:, i, :] for i in range(5))
            over = jm[:, 0, 0:EXP]
            link(gp_.memset(flag[:, 0:NB], 1.0))
            for r in range(rounds):
                rb = slice(r * NB, (r + 1) * NB)
                if r:
                    link(gp_.tensor_scalar(over, counts, float(r * SLOTS), None, ALU.is_gt))
                    link(gp_.tensor_tensor(jm[:, 1, 0:16], over[:, 0:EXP:2], over[:, 1:EXP:2], ALU.add))
                    link(gp_.tensor_tensor(flag[:, rb], jm[:, 1, 0:16:2], jm[:, 1, 1:16:2], ALU.add))
                    link(gp_.tensor_scalar(flag[:, rb], flag[:, rb], 1.0, None, ALU.min))
                link(gp_.tensor_scalar(e0[:, rb], iota[:, 0:NB], float(BE), None, ALU.mult))
                link(gp_.memset(r0[:, rb], float(r * SLOTS)))
            link(gp_.memset(jm, 1.0))
            link(gp_.affine_select(out=jm, in_=jm, compare_op=ALU.is_gt, fill=0.0, base=0,
                                   pattern=[[1, JOBS], [-1, JOBS]], channel_multiplier=0))
            link(gp_.tensor_tensor(jm, jm, flag.unsqueeze(1).to_broadcast([P, JOBS, JOBS]), ALU.mult))

            def row_sums(dst):
                w = JOBS // 2
                while w:
                    link(gp_.tensor_tensor(jm[:, :, 0:w], jm[:, :, 0:w], jm[:, :, w:2 * w], ALU.add))
                    w //= 2
                link(gp_.tensor_copy(dst, jm[:, :, 0]))

            row_sums(pos)
            link(gp_.tensor_tensor(most, pos, flag, ALU.add))
            link(gp_.tensor_copy(jobn, most[0:1, JOBS - 1:JOBS]))
            link(gp_.tensor_scalar(jb[:, 5, :], flag, -1000.0, 1000.0, ALU.mult, ALU.add))
            link(gp_.tensor_tensor(pos, pos, jb[:, 5, :], ALU.add))
            for i, val in enumerate((e0, r0)):
                link(gp_.tensor_tensor(jm, pos.unsqueeze(1).to_broadcast([P, JOBS, JOBS]),
                                       iota[:, 0:JOBS].unsqueeze(2).to_broadcast([P, JOBS, JOBS]), ALU.subtract))
                link(gp_.tensor_scalar(jm, jm, 0.0, None, ALU.is_equal))
                link(gp_.tensor_tensor(jm, jm, val.unsqueeze(1).to_broadcast([P, JOBS, JOBS]), ALU.mult))
                row_sums(jobtab[:, i, :])
            gp_.tensor_copy(jobi, jobtab[0:1, 0, :]).then_inc(jobs_ready, 1)

        @block.vector
        def _(dve):
            V = nc.vector
            n = [0]

            def link(ins):
                n[0] += 1
                ins.then_inc(vec_order, 1)
                dve.wait_ge(vec_order, n[0])

            dve.wait_ge(consts_ready, 1)
            link(V.tensor_copy(steps, iota_i))
            link(V.tensor_copy(iota[:, :], steps[:, 0:SLOTS]))
            link(V.tensor_scalar(part_i, part_i, 4, 1, ALU.logical_shift_right, ALU.bitwise_and))
            link(V.tensor_copy(odd[:, 1:2], part_i))
            link(V.tensor_scalar(odd[:, 0:1], odd[:, 1:2], -1.0, 1.0, ALU.mult, ALU.add))
            V.tensor_reduce(own[:, :], ident[:, :].rearrange("p (b i) -> p i b", b=4), AX.X, ALU.add).then_inc(own_ready, 1)
            dve.wait_ge(x_squares, TT)
            V.tensor_scalar(rstd[:, 0:2], ss[:, 0:2], 1.0 / D, EPS, ALU.mult, ALU.add).then_inc(x_var, 1)
            dve.wait_ge(x_root, 1)
            V.reciprocal(rstd[:, 0:2], rstd[:, 2:4]).then_inc(x_rstd, 1)
            dve.wait_ge(x_rstd, 1)
            for t in range(TT):
                V.tensor_scalar(xr[:, t, :], xr[:, t, :], rstd[:, t:t + 1], None, ALU.mult).then_inc(x_normed, 1)
            re, im, red, ang, k_, r_ = (prm[:, i, :] for i in range(6))
            mag, sin_, cos_, absr, turns = (prm[:, i, :] for i in (6, 7, 8, 9, 10))
            nr, ni, t1, t2, f_re, f_im, rden = (prm[:, i, :] for i in (11, 12, 13, 14, 15, 16, 17))
            dve.wait_ge(dt_ready, 1)
            dtb = dt[:, :].unsqueeze(2).to_broadcast([32, 2, S])

            def by_group(v):
                return v.rearrange("p (g s) -> p g s", g=2)

            V.tensor_tensor(by_group(red), by_group(re), dtb, ALU.mult).then_inc(decay_in, 1)
            link(V.tensor_tensor(by_group(ang), by_group(im), dtb, ALU.mult))
            link(V.tensor_scalar(k_, ang, 1.0 / (2 * math.pi), MAGIC, ALU.mult, ALU.add))
            link(V.tensor_scalar(k_, k_, MAGIC, None, ALU.subtract))
            link(V.scalar_tensor_tensor(r_, k_, -C1, ang, ALU.mult, ALU.add))
            link(V.scalar_tensor_tensor(r_, k_, -C2, r_, ALU.mult, ALU.add))
            link(V.scalar_tensor_tensor(r_, k_, -C3, r_, ALU.mult, ALU.add))
            link(V.tensor_scalar(r_, r_, PI_DOWN, -PI_DOWN, ALU.min, ALU.max))
            V.tensor_scalar(turns, r_, 1.0 / (2 * math.pi), None, ALU.mult).then_inc(angle_in, 1)
            dve.wait_ge(decay_ready, 1)
            dve.wait_ge(angle_ready, 3)
            link(V.tensor_tensor(nr, mag, cos_, ALU.mult))
            link(V.tensor_tensor(ni, mag, sin_, ALU.mult))
            link(V.tensor_scalar(nr, nr, 1.0, None, ALU.subtract))
            link(V.tensor_tensor(t1, re, re, ALU.mult))
            link(V.tensor_tensor(t2, im, im, ALU.mult))
            link(V.tensor_tensor(t1, t1, t2, ALU.add))
            link(V.reciprocal(rden, t1))
            link(V.tensor_tensor(t1, nr, re, ALU.mult))
            link(V.tensor_tensor(t2, ni, im, ALU.mult))
            link(V.tensor_tensor(t1, t1, t2, ALU.add))
            link(V.tensor_tensor(f_re, t1, rden, ALU.mult))
            link(V.tensor_tensor(t1, ni, re, ALU.mult))
            link(V.tensor_tensor(t2, nr, im, ALU.mult))
            link(V.tensor_tensor(t1, t1, t2, ALU.subtract))
            V.tensor_tensor(f_im, t1, rden, ALU.mult).then_inc(params_ready, 1)
            dve.wait_ge(cw_turned, 1)
            link(V.tensor_copy(cwT[:, :, :].rearrange("p c t -> p (c t)"), ps[:, 2, 0:256]))
            V.tensor_copy(vT[:, :, :].rearrange("p n c -> p (n c)"), ps[:, 2, 256:296]).then_inc(cw_stored, 1)
            dve.wait_ge(setup_landed, 16 * 14)
            for c in range(2):
                for g in range(2):
                    ins = V.tensor_scalar(cexp[:, c, :, g, :], cst[:, c, :, :], odd[:, g:g + 1], None, ALU.mult)
                    if c == 0 or g == 0:
                        link(ins)
                    else:
                        ins.then_inc(cexp_ready, 1)
            dve.wait_ge(params_turned, 1)
            V.tensor_copy(par[:, :, :].rearrange("p n q -> p (n q)"), ps[:, 3, 0:128]).then_inc(params_stored, 1)
            dve.wait_ge(params_stored, 1)
            link(V.tensor_copy(decay[:, :], par[:, 0, :]))
            dve.wait_ge(b_turned, 1)
            dve.wait_ge(blocks_zero, 1)
            b_re, b_im = (ps[:, 4 + c, :].rearrange("p (h r) -> p r h", h=HG) for c in range(2))
            fr, fi = (par[:, i, :].unsqueeze(2).to_broadcast([P, PAIRS, HG]) for i in (2, 3))
            m1, m2 = (btmp[:, i, 0:N].rearrange("p (r h) -> p r h", h=HG) for i in range(2))
            for c, (p1, p2, op) in enumerate(((b_re, b_im, ALU.subtract), (b_im, b_re, ALU.add))):
                link(V.tensor_tensor(m1, p1, fr, ALU.mult))
                link(V.tensor_tensor(m2, p2, fi, ALU.mult))
                for g in range(2):
                    half = slice(64 * g, 64 * g + 64)
                    ins = V.tensor_tensor(bdiag[half, c, :, g, :], m1[half], m2[half], op)
                    if c == 1 and g == 1:
                        ins.then_inc(bdiag_ready, 1)
                    else:
                        link(ins)
            th = par[:, 1, :].unsqueeze(2).to_broadcast([P, PAIRS, HALF])
            link(V.tensor_tensor(cosT, th, steps.unsqueeze(1).to_broadcast([P, PAIRS, HALF]), ALU.mult))
            link(V.tensor_scalar(sinT, cosT, MAGIC, MAGIC, ALU.add, ALU.subtract))
            link(V.tensor_tensor(cosT, cosT, sinT, ALU.subtract))
            link(V.tensor_scalar(rot128[:, 0, :], par[:, 1, :], float(HALF), None, ALU.mult))
            link(V.tensor_scalar(rot128[:, 1, :], rot128[:, 0, :], MAGIC, MAGIC, ALU.add, ALU.subtract))
            V.tensor_tensor(rot128[:, 0, :], rot128[:, 0, :], rot128[:, 1, :], ALU.subtract).then_inc(phase_ready, 1)
            def columns(bank, part):
                dve.wait_ge(ada_done, bank + 1)
                link(V.tensor_tensor(modrow[:, :].rearrange("p (i k) -> p i k", k=KD),
                                     ps[:, bank, :].rearrange("p (i k) -> p i k", k=KD),
                                     own[:, :].unsqueeze(2).to_broadcast([P, 32, KD]), ALU.mult))
                link(V.tensor_reduce(mod[:, part, :], modrow[:, :].rearrange("p (i k) -> p k i", k=KD), AX.X, ALU.add))

            dve.wait_ge(late_landed, 16 * 3)
            columns(0, 1)
            link(V.tensor_tensor(mod[:, 1, :], mod[:, 1, :], bada[:, 1, :], ALU.add))
            link(V.scalar_tensor_tensor(mod[:, 1, :], mod[:, 1, :], 1.0, g1[:, :], ALU.add, ALU.mult))
            dve.wait_ge(x_stored, 8)
            columns(1, 0)
            link(V.tensor_tensor(mod[:, 0, :], mod[:, 0, :], bada[:, 0, :], ALU.add))
            for k in range(KD):
                V.tensor_scalar(hT[:, k, :], hT[:, k, :], mod[:, 1, k:k + 1], mod[:, 0, k:k + 1], ALU.mult,
                                ALU.add).then_inc(h_ready, 1)
            dve.wait_ge(bc_stored, 8)
            V.memset(zT[:, :, 0:PAD], 0.0).then_inc(pads_ready, 1)

            dve.wait_ge(tables_ready, 2)
            def quad(q, middle=None):
                b = q % 2
                c4 = cosT[:, 4 * q:4 * q + 4, :].unsqueeze(2).to_broadcast([P, 4, 4, HALF])
                s4 = sinT[:, 4 * q:4 * q + 4, :].unsqueeze(2).to_broadcast([P, 4, 4, HALF])
                s2 = sinT[:, 4 * q:4 * q + 4, :].unsqueeze(2).to_broadcast([P, 4, 2, HALF])
                drive = ps[:, 4:8, :].rearrange("p r (x t) -> p r x t", x=4)
                r1 = rot[:, b, 0, :, :]
                r2 = rot[:, b, 1, :, :]
                r1v = r1.rearrange("p r (x t) -> p r x t", x=4)
                r2v = r2.rearrange("p r (x t) -> p r x t", x=4)
                dve.wait_ge(drive_done, q + 1)
                if q >= 2:
                    dve.wait_ge(side_done, q - 1)
                link(V.tensor_tensor(r1v, drive, c4, ALU.mult))
                V.tensor_tensor(r2v, drive, s4, ALU.mult).then_inc(drive_read, 1)
                dve.wait_ge(drive_read, q + 1)
                link(V.tensor_tensor(r1[:, :, 0:T], r1[:, :, 0:T], r2[:, :, T:2 * T], ALU.add))
                link(V.tensor_tensor(r1[:, :, T:2 * T], r2[:, :, 0:T], r1[:, :, T:2 * T], ALU.subtract))
                for half in range(2):
                    for r in range(4):
                        m = decay[:, 4 * q + r:4 * q + r + 1].to_broadcast([P, HALF])
                        for x in range(2):
                            z = r1[:, r, x * T + half * HALF:x * T + (half + 1) * HALF]
                            init = carry[:, 2, r, x:x + 1] if half else 0.0
                            n[0] += 1
                            V.tensor_tensor_scan(z, m, z, init, ALU.mult, ALU.add).then_inc(vec_order, 1)
                    dve.wait_ge(vec_order, n[0])
                    if half == 0:
                        end = r1.rearrange("p r (x t) -> p r x t", x=2)[:, :, :, HALF - 1]
                        cc, sc = (rot128[:, i, 4 * q:4 * q + 4].unsqueeze(2).to_broadcast([P, 4, 2]) for i in range(2))
                        link(V.tensor_tensor(carry[:, 0, :, :], end, cc, ALU.mult))
                        link(V.tensor_tensor(carry[:, 1, :, :], end, sc, ALU.mult))
                        link(V.tensor_tensor(carry[:, 2, :, 0], carry[:, 0, :, 0], carry[:, 1, :, 1], ALU.add))
                        link(V.tensor_tensor(carry[:, 2, :, 1], carry[:, 0, :, 1], carry[:, 1, :, 0], ALU.subtract))
                if middle:
                    middle()
                link(V.tensor_scalar(r2[:, :, 0:T], r1[:, :, 0:T], -1.0, None, ALU.mult))
                link(V.tensor_tensor(r2v[:, :, 0:2, :], r2v[:, :, 0:2, :], s2, ALU.mult))
                link(V.tensor_tensor(r2v[:, :, 2:4, :], r1v[:, :, 2:4, :], s2, ALU.mult))
                V.tensor_tensor(r1v, r1v, c4, ALU.mult).then_inc(states_ready, 1)
                dve.wait_ge(states_ready, q + 1)

            def convolve(h):
                dve.wait_ge(z_ready, h + 1)
                for j in range(TAPS):
                    for i in range(4):
                        c = 4 * h + i
                        done = 4 * (TAPS * h + j) + i
                        z = zT[:, c, j:j + T]
                        if j == 0:
                            ins = V.tensor_scalar(conv[:, c, :], z, cwT[:, c, 0:1], cwT[:, c, TAPS:TAPS + 1],
                                                  ALU.mult, ALU.add)
                        else:
                            dve.wait_ge(conv_step, done - 3)
                            ins = V.scalar_tensor_tensor(conv[:, c, :], z, cwT[:, c, j:j + 1], conv[:, c, :],
                                                         ALU.mult, ALU.add)
                        ins.then_inc(conv_step, 1)

            def over_tiles(v):
                return v.unsqueeze(1).to_broadcast([P, CT_, T])

            def add_tiles(v):
                V.tensor_reduce(csum, v.rearrange("p c t -> p t c"), AX.X, ALU.add).then_inc(reduced, 1)

            def centre():
                dve.wait_ge(sum_kept, 1)
                V.tensor_tensor(conv, conv, over_tiles(stat[:, 0, :]), ALU.subtract).then_inc(centred, 1)

            def add_squares(n):
                dve.wait_ge(squares, n)
                dve.wait_ge(sums, n)
                add_tiles(sq)

            def scale_conv():
                dve.wait_ge(sum_kept, 2)
                dve.wait_ge(centred, 1)
                link(V.reciprocal(stat[:, 1, :], stat[:, 1, :]))
                V.tensor_tensor(conv, conv, over_tiles(stat[:, 1, :]), ALU.mult).then_inc(scaled, 1)

            def norm_conv():
                dve.wait_ge(sum_kept, 3)
                link(V.reciprocal(stat[:, 0, :], stat[:, 0, :]))
                for c in range(CT_):
                    V.scalar_tensor_tensor(conv[:, c, :], conv[:, c, :], vT[:, 2, c:c + 1], stat[:, 0, :], ALU.mult,
                                           ALU.mult).then_inc(yc_ready, 1)

            for q in range(4):
                quad(q)
            convolve(0)
            convolve(1)
            dve.wait_ge(sum_consts, 1)
            dve.wait_ge(conv_step, CT_ * TAPS)
            add_tiles(conv)
            quad(4, centre)
            add_squares(1)
            quad(5, scale_conv)
            add_squares(2)
            quad(6, norm_conv)
            quad(7)
            dve.wait_ge(chunk_stored, 16)
            dve.wait_ge(side_stored, QUADS)
            V.tensor_tensor(uT, uT, sgT, ALU.mult).then_inc(gated, 1)
            dve.wait_ge(columns_ready, 3)
            dve.wait_ge(bada_landed, 16)
            V.tensor_tensor(mod[:, 2, :], mod[:, 2, :], bada2[:, 2, :], ALU.add).then_inc(gate_added, 1)
            link(V.tensor_tensor(mod[:, 4, :], mod[:, 4, :], bada2[:, 4, :], ALU.add))
            link(V.scalar_tensor_tensor(mod[:, 4, :], mod[:, 4, :], 1.0, g2[:, :], ALU.add, ALU.mult))
            V.tensor_tensor(mod[:, 3, :], mod[:, 3, :], bada2[:, 3, :], ALU.add).then_inc(ab_ready, 1)
            add_squares(3)
            dve.wait_ge(sum_kept, 4)
            dve.wait_ge(gated, 1)
            link(V.reciprocal(stat[:, 1, :], stat[:, 1, :]))
            for c in range(CT_):
                V.scalar_tensor_tensor(uT[:, c, :], uT[:, c, :], vT[:, 3, c:c + 1], stat[:, 1, :], ALU.mult,
                                       ALU.mult).then_inc(ys_ready, 1)
            dve.wait_ge(columns_ready, 4)
            V.tensor_tensor(mod[:, 5, :], mod[:, 5, :], bada2[:, 5, :], ALU.add).then_inc(gate_added, 1)
            dve.wait_ge(gate_landed, 16)
            dve.wait_ge(x_again, 16)
            for m in range(8):
                c, t = divmod(m, 2)
                if m == 4:
                    dve.wait_ge(ab_turned, 1)
                    V.tensor_copy(ab, ps[:, 7, 0:2 * KD]).then_inc(ab_kept, 1)
                    dve.wait_ge(ab_kept, 1)
                    dve.wait_ge(wr_ready, 2)
                    scale, shift = (ab[:, i * KD:(i + 1) * KD].unsqueeze(2).to_broadcast([P, KD, NG + EXP]) for i in range(2))
                    link(V.tensor_tensor(wrb, wr, shift, ALU.mult))
                    link(V.tensor_reduce(wrbs, wrb.rearrange("p k e -> p e k"), AX.X, ALU.add))
                    V.tensor_tensor(wr, wr, scale, ALU.mult).then_inc(weights_ready, 1)
                dve.wait_ge(out_done, c + 1)
                link(V.tensor_tensor(gtmp[:, t, :], ps[:, OUT_BANKS[c][t], :], gate1[:, c * N:(c + 1) * N], ALU.mult))
                cc = slice(c * N, (c + 1) * N)
                V.tensor_tensor(x1[:, t, cc], x1[:, t, cc], gtmp[:, t, :], ALU.add).then_inc(x1_ready, 1)
                dve.wait_ge(x1_ready, m + 1)
            dve.wait_ge(x1_squares, 8)
            link(V.tensor_reduce(rstd[:, 0:2], ss[:, :].rearrange("p (t c) -> p t c", t=TT), AX.X, ALU.add))
            V.tensor_scalar(rstd[:, 0:2], rstd[:, 0:2], 1.0 / D, EPS, ALU.mult, ALU.add).then_inc(n2_var, 1)
            dve.wait_ge(n2_root, 1)
            V.reciprocal(rstd[:, 0:2], rstd[:, 2:4]).then_inc(n2_rstd, 1)
            dve.wait_ge(n2_rstd, 1)
            dve.wait_ge(lbias_done, 1)
            link(V.tensor_tensor(lbias, ps[:, 5, 0:NG + EXP], rbias, ALU.add))
            link(V.memset(gp[:, :, :], -3.0e38))

            dve.wait_ge(logits_turned, 1)
            for t in range(TT):
                link(V.scalar_tensor_tensor(lg[:, t, :], ps[:, 1, t * 64:t * 64 + NG + EXP], rstd[:, t:t + 1], lbias,
                                            ALU.mult, ALU.add))
            link(V.tensor_copy(gp[:, :, 0:NG], lg[:, :, 0:NG]))
            for t in range(TT):
                link(V.max(top[:, t, :], gp[:, t, :]))
                link(V.max_index(topi[:, t, :], top[:, t, :], gp[:, t, :]))
            V.tensor_tensor(rt[:, :, 0:4], lg[:, :, 0:NG], top[:, :, 0:1].to_broadcast([P, TT, NG]),
                            ALU.subtract).then_inc(exp_in, 1)
            gi = rt[:, :, 4:5]
            link(V.tensor_copy(gi, topi[:, :, 0:1]))
            group_hot = comb[:, :, 0:NG]
            link(V.tensor_tensor(group_hot, iota[:, 0:NG].unsqueeze(1).to_broadcast([P, TT, NG]),
                                 gi.to_broadcast([P, TT, NG]), ALU.is_equal))
            masked = sel[:, :, 0, :].rearrange("p t (e g) -> p t e g", g=NG)
            link(V.tensor_tensor(masked, lg[:, :, NG:].rearrange("p t (g e) -> p t e g", g=NG),
                                 group_hot.unsqueeze(2).to_broadcast([P, TT, NE, NG]), ALU.mult))
            esel = rank[:, :, 0:NE]
            link(V.tensor_reduce(esel, masked, AX.X, ALU.add))
            for t in range(TT):
                link(V.max(etop[:, t, :], esel[:, t, :]))
                link(V.max_index(etopi[:, t, :], etop[:, t, :], esel[:, t, :]))
            V.tensor_tensor(rt[:, :, 5:6], etop[:, :, 1:2], etop[:, :, 0:1], ALU.subtract).then_inc(exp_in, 1)
            link(V.tensor_copy(rt[:, :, 8:10], etopi[:, :, 0:2]))
            link(V.scalar_tensor_tensor(rt[:, :, 8:10], gi.to_broadcast([P, TT, 2]), float(NE), rt[:, :, 8:10],
                                        ALU.mult, ALU.add))
            io = iota[:, 0:EXP].unsqueeze(1).to_broadcast([P, TT, EXP])
            for i in range(2):
                link(V.tensor_tensor(sel[:, :, i, :], io, rt[:, :, 8 + i:9 + i].to_broadcast([P, TT, EXP]), ALU.is_equal))
            V.tensor_tensor(sel[:, :, 2, :], sel[:, :, 0, :], sel[:, :, 1, :], ALU.add).then_inc(sel_ready, 1)
            dve.wait_ge(exp_done, 2)
            link(V.tensor_reduce(rt[:, :, 10:11], rt[:, :, 0:4], AX.X, ALU.add))
            link(V.tensor_scalar(rt[:, :, 11:12], rt[:, :, 6:7], 1.0, None, ALU.add))
            link(V.tensor_tensor(rt[:, :, 10:11], rt[:, :, 10:11], rt[:, :, 11:12], ALU.mult))
            link(V.reciprocal(rt[:, :, 12:13], rt[:, :, 10:11]))
            link(V.tensor_tensor(rt[:, :, 13:14], rt[:, :, 12:13], rt[:, :, 6:7], ALU.mult))
            dve.wait_ge(sel_ready, 1)
            for i in range(2):
                link(V.tensor_tensor(sel[:, :, i, :], sel[:, :, i, :], rt[:, :, 12 + i:13 + i].to_broadcast([P, TT, EXP]),
                                     ALU.mult))
            link(V.tensor_tensor(comb[:, :, :], sel[:, :, 0, :], sel[:, :, 1, :], ALU.add))
            dve.wait_ge(rank_done, 1)
            link(V.scalar_tensor_tensor(rank[:, :, :], ps[:, 2, 0:2 * EXP].rearrange("p (t e) -> p t e", t=TT), 1.0,
                                        sel[:, :, 2, :], ALU.add, ALU.mult))
            link(V.tensor_scalar(rank[:, :, :], rank[:, :, :], 1.0, None, ALU.subtract))
            V.tensor_copy(counts, ps[:, 2, 2 * EXP:3 * EXP]).then_inc(counts_ready, 1)
            dve.wait_ge(counts_ready, 1)

            JOB_STEPS = 4

            def job(j, e0, first_rank):
                c = [0]

                def step(ins):
                    c[0] += 1
                    ins.then_inc(job_order, 1)
                    dve.wait_ge(job_order, j * JOB_STEPS + c[0])

                ranks = rankc.rearrange("p t e -> p (t e)")
                if first_rank is None:
                    step(V.tensor_copy(rankc[:, :, :], rank[:, :, bass.ds(e0, BE)]))
                else:
                    step(V.tensor_scalar(rankc[:, :, :], rank[:, :, bass.ds(e0, BE)], first_rank, None, ALU.subtract))
                each = [P, TT * BE, SLOTS]
                step(V.tensor_tensor(onehot, iota[:, 0:SLOTS].unsqueeze(1).to_broadcast(each),
                                     ranks.unsqueeze(2).to_broadcast(each), ALU.is_equal))
                V.tensor_tensor(pick, onehot.rearrange("p (t e) s -> p t (e s)", t=TT),
                                rstd[:, 0:2].unsqueeze(2).to_broadcast([P, TT, BE * SLOTS]), ALU.mult).then_inc(picks_ready, 1)
                step(V.tensor_copy(rankc[:, :, :], comb[:, :, bass.ds(e0, BE)]))
                V.tensor_tensor(wpick.rearrange("p t (e s) -> p (t e) s", e=BE), onehot,
                                ranks.unsqueeze(2).to_broadcast(each), ALU.mult).then_inc(wpicks_ready, 1)
                for k in range(0, KD, 2):
                    dve.wait_ge(gathered, j * KD + k + 1)
                    V.tensor_scalar(xT[:, k, :], ps[:, 4, 0:T], mod[:, 4, k:k + 1], mod[:, 3, k:k + 1], ALU.mult,
                                    ALU.add).then_inc(tok_even, 1)
                dve.wait_ge(picks_turned, j + 1)
                step(V.tensor_copy(wpickT[:, 0, :], ps[:, 6, 0:T]))
                V.tensor_copy(wpickT[:, 1, :], ps[:, 7, 0:T]).then_inc(scatter_ready, 1)
                for pr in range(2):
                    dve.wait_ge(up_done, j * 2 + pr + 1)
                    dve.wait_ge(gate_silu, j * 2 + pr + 1)
                    V.tensor_tensor(hid, silu, ps[:, 1, :], ALU.mult).then_inc(hidden_ready, 1)
                    for n in range(5):
                        if n < 4:
                            dve.wait_ge(down_done, j * 8 + pr * 4 + n + 1)
                            V.tensor_tensor(yexp[:, n, :], ps[:, 2 + n % 2, :], gate2[:, n * N:(n + 1) * N],
                                            ALU.mult).then_inc(down_stored, 1)
                        if n:
                            for t in range(TT):
                                m = 2 * (n - 1) + t
                                cc = slice((n - 1) * N, n * N)
                                dve.wait_ge(combined, j * 16 + pr * 8 + m + 1)
                                V.tensor_tensor(acc[:, t, cc], acc[:, t, cc], ps[:, 6 + t, :], ALU.add).then_inc(added, 1)
                                dve.wait_ge(added, j * 16 + pr * 8 + m + 1)
                assert c[0] == JOB_STEPS

            dve.wait_ge(gate2_landed, 16)
            dve.wait_ge(acc_ready, 8)
            with dve.Fori(0, NB) as j:
                job(j, j * BE, None)
            dve.wait_ge(jobs_ready, 1)
            n_jobs = dve.value_load(jobn[0:1, 0:1], min_val=NB, max_val=JOBS)
            with dve.If(n_jobs > NB):
                with dve.Fori(NB, n_jobs) as j:
                    e0 = dve.value_load(jobi[0:1, bass.ds(j, 1)], min_val=0, max_val=EXP - BE)
                    job(j, e0, jobtab[:, 1, bass.ds(j, 1)])
            dve.wait_ge(gain_landed, 16)
            dve.wait_ge(fin_sq, n_jobs * 8)
            link(V.tensor_reduce(rstd[:, 0:2], ss[:, :].rearrange("p (t c) -> p t c", t=TT), AX.X, ALU.add))
            V.tensor_scalar(rstd[:, 0:2], rstd[:, 0:2], 1.0 / D, EPS, ALU.mult, ALU.add).then_inc(fin_var, 1)
            dve.wait_ge(fin_root, 1)
            link(V.reciprocal(rstd[:, 0:2], rstd[:, 2:4]))
            for t in range(TT):
                for h in range(2):
                    cc = slice(h * D // 2, (h + 1) * D // 2)
                    V.scalar_tensor_tensor(acc[:, t, cc], acc[:, t, cc], rstd[:, t:t + 1], fgain[:, cc], ALU.mult,
                                           ALU.mult).then_inc(fin_out, 1)


NAMES = ["x", "c", "w_ada", "b_ada", "norm1_g", "w_in", "conv_w", "conv_b", "conv_ln_g", "conv_ln_b", "ssm_a_re",
         "ssm_a_im", "ssm_b_re", "ssm_b_im", "ssm_c_re", "ssm_c_im", "ssm_d", "ssm_log_dt", "out_norm_conv_g",
         "out_norm_ssm_g", "w_out", "norm2_g", "router_group_w", "router_group_b", "router_expert_w",
         "router_expert_b", "exp_w_gate", "exp_w_up", "exp_w_down", "final_norm_g"]


def kernel(**inputs):
    import numpy as np
    import concourse.bacc as bacc
    from concourse.bass_utils import run_bass_kernel_spmd

    nc = bacc.Bacc("TRN2", target_bir_lowering=False, num_devices=1, dynamic_dma_scratch_size=1024)
    arrays, aps = {}, {}
    for name in NAMES:
        arr = np.ascontiguousarray(inputs[name])
        arrays[f"in_{name}"] = arr
        aps[name] = nc.dram_tensor(f"in_{name}", arr.shape, mybir.dt.from_np(arr.dtype), kind="ExternalInput").ap()
    out = nc.dram_tensor("out_x", [1, T, D], F32, kind="ExternalOutput").ap()
    trunk(nc, aps, out)
    got = run_bass_kernel_spmd(nc, [arrays], core_ids=[0])
    return got.results[0]["out_x"]
```

```python
import math
from contextlib import ExitStack

import concourse.bass as bass
from concourse import mybir

ALU = mybir.AluOpType
ACT = mybir.ActivationFunctionType
AX = mybir.AxisListType
F32 = mybir.dt.float32
I32 = mybir.dt.int32
U32 = mybir.dt.uint32

P = 128
D = 2048
T = 256
TT = T // P
KD = D // P
CH = 1024
CT_ = CH // P
TAPS = 31
PAD = TAPS - 1
G, HG, S = 64, 16, 64
PAIRS = G // 2
QUADS = PAIRS // 4
HALF = T // 2
NG, NE, F = 4, 8, 512
EXP = NG * NE
SLOTS = 64
BE = 4
NB = EXP // BE
JOBS = (T // SLOTS) * NB
N = 512
EPS = 1e-6
MAGIC = 1.5 * 2.0 ** 23
TWO_PI_DOWN = 6.283185
PI_DOWN = 3.1415925
C1 = 6.28125
C2 = 0.0019350051879882812
C3 = 2 * math.pi - C1 - C2

RING = 12
UNIT = 2048
A_UNITS, B_UNITS, C_UNITS, D_UNITS = 36, 92, 16, 48
SCALE, CHUNK_0, SHIFT = 0, 16, 20


def ring_use(n):
    if n < A_UNITS:
        if CHUNK_0 <= n < SHIFT:
            return 8 + n - CHUNK_0, 0
        n = n - 4 if n >= SHIFT else n
        return n % 8, n // 8
    r, s = divmod(n - A_UNITS, RING)
    return s, r + (4 if s < 8 else 1)


def turn(n):
    if CHUNK_0 <= n < SHIFT:
        return n + KD
    return n - 4 if SHIFT <= n < A_UNITS else n


D_BASE = A_UNITS + B_UNITS + C_UNITS
D_USES = [13 if s < 8 else 10 for s in range(RING)]

CHUNKS = [(2048, "u"), (1024, "gate"), (0, "value"), (1536, "gate"), (512, "value"), (2560, "u"),
          (3072, "out_gate"), (3584, "out_gate")]
FIRST_TILE = [0, 0, 0, 4, 4, 4, 0, 4]
U_CHUNKS, VALUE_CHUNKS = (0, 5), (2, 4)
ADA_PARTS = [2, 3, 4, 5]


DRIVE_AT = [4, 5, 7, 8, 24, 26, 28, 30]
READ_AT = [7, 8, 10, 11, 28, 30, 32, 34]
SUM_AT = [25, 27, 29]
SIDE_STEPS = 35


def side_jobs(g):
    return [("drive", q) for q in range(QUADS) if DRIVE_AT[q] == g] + \
        [("read", q) for q in range(QUADS) if READ_AT[q] == g] + \
        [("sum", n) for n in range(3) if SUM_AT[n] == g]


def tile_stored(q):
    return 2 * U_CHUNKS[q // 4] + (q % 4) // 2 + 1


def trunk(nc, a, out):
    ctx = ExitStack()
    with ctx:
        def sb(name, shape, dt=F32):
            return ctx.enter_context(nc.sbuf_tensor(name, shape, dt))

        def sem(name):
            return ctx.enter_context(nc.semaphore(name))

        ring = sb("ring", [P, RING, UNIT])
        KB = 256
        arena = sb("arena", [P, 122 * KB])

        def at(kb, words, parts=P):
            o = int(kb * KB)
            return arena[0:parts, o:o + words]

        hT = at(0, 16 * KB).rearrange("p (k t) -> p k t", k=KD)
        cosT = at(16, 16 * KB).rearrange("p (q t) -> p q t", q=PAIRS)
        sinT = at(32, 16 * KB).rearrange("p (q t) -> p q t", q=PAIRS)
        uT = at(48, 8 * KB).rearrange("p (c t) -> p c t", c=CT_)
        zT = at(56, CT_ * (PAD + T)).rearrange("p (c t) -> p c t", c=CT_)
        rot = at(66, 32 * KB).rearrange("p (b w r t) -> p b w r t", b=2, w=2, r=4)
        driveT = at(98, 8 * KB).rearrange("p (c q s) -> p c q s", c=2, q=QUADS)
        readT = at(106, 8 * KB).rearrange("p (c q s) -> p c q s", c=2, q=QUADS)
        apart = at(118, 4 * KB).rearrange("p (r t) -> p r t", r=4)
        vals = at(114, 4 * KB).rearrange("p (c t) -> p c t", c=4)
        sgT = at(56, 8 * KB).rearrange("p (c t) -> p c t", c=CT_)
        xr = at(66, 16 * KB).rearrange("p (t d) -> p t d", t=TT)
        bst = at(82, 16 * KB, 32).rearrange("p (c s) -> p c s", c=2)
        cst = at(48, 4 * KB).rearrange("p (c q s) -> p c q s", c=2, q=QUADS)
        cexp = at(52, 8 * KB).rearrange("p (c q g s) -> p c q g s", c=2, q=QUADS, g=2)
        cwst = at(60, 4 * KB, TAPS + 1)
        vst = at(64, P, 40)
        prm = at(98, 20 * P, 32).rearrange("p (n s) -> p n s", n=20)
        btmp = at(108, 4 * KB).rearrange("p (n f) -> p n f", n=2)
        bdiag = at(114, 8 * KB).rearrange("p (c r g h) -> p c r g h", c=2, r=PAIRS, g=2)
        conv = at(16, 8 * KB).rearrange("p (c t) -> p c t", c=CT_)
        sq = at(32, 8 * KB).rearrange("p (c t) -> p c t", c=CT_)
        stat = at(114, 2 * T).rearrange("p (n t) -> p n t", n=2)
        mean_w = at(116, P)
        csum = at(117, T)
        x1sq = at(118, N)
        x1T = at(0, 16 * KB).rearrange("p (k t) -> p k t", k=KD)
        x1 = at(66, 16 * KB).rearrange("p (t d) -> p t d", t=TT)
        gate1 = at(82, 8 * KB)
        gtmp = at(90, 4 * KB).rearrange("p (b n) -> p b n", b=2)
        xT = at(16, 16 * KB).rearrange("p (k t) -> p k t", k=KD)
        acc = at(32, 16 * KB).rearrange("p (t d) -> p t d", t=TT)
        yexp = at(48, 8 * KB).rearrange("p (n c) -> p n c", n=4)
        silu = at(56, 2 * KB)
        hid = at(58, 2 * KB)
        hidT = at(60, 2 * KB).rearrange("p (j s) -> p j s", j=4)
        onehot = at(0, 2 * KB).rearrange("p (x s) -> p x s", x=TT * BE)
        pick = at(62, 2 * KB).rearrange("p (t s) -> p t s", t=TT)
        wpick = at(64, 2 * KB).rearrange("p (t s) -> p t s", t=TT)
        junk = at(2, 2 * KB)
        wpickT = at(90, 2 * KB).rearrange("p (r t) -> p r t", r=2)
        gate2 = at(98, 8 * KB)
        fgain = at(106, 8 * KB)

        ident = sb("ident", [P, P])
        iota = sb("iota", [P, SLOTS])
        ccol = sb("ccol", [P, KD])
        bada1 = at(64.5, 2 * KD).rearrange("p (m k) -> p m k", m=2)
        g1 = at(64.75, KD)
        g2 = sb("g2", [P, KD])
        mod = sb("mod", [P, 6, KD])
        bada = sb("bada", [P, 4, KD])
        own = sb("own", [P, 32])
        modrow = sb("modrow", [P, N])
        ss = sb("ss", [P, 8])
        rstd = sb("rstd", [P, 4])
        decay = sb("decay", [P, PAIRS])
        rot128 = sb("rot128", [P, 2, PAIRS])
        carry = sb("carry", [P, 3, 4, 2])
        vT = sb("vT", [P, 5, CT_])
        skip = sb("skip", [P, P])
        tiny = at(64.9375, 16)
        halfpi, eps = tiny[:, 0:1], tiny[:, 1:2]
        ldt, dt = tiny[0:32, 2:4], tiny[0:32, 4:6]
        chunk_shift = tiny[:, 8:12]
        thirty_second = tiny[:, 12:13]
        odd = tiny[:, 6:8]
        cwT = at(65, 256).rearrange("p (c t) -> p c t", c=CT_)
        par = at(112, 4 * PAIRS).rearrange("p (n q) -> p n q", n=4)
        iota_i = at(112.5, P).bitcast(I32)
        steps = at(113, HALF)
        part_i = at(113.5, 1).bitcast(I32)
        place = [int(94 * KB)]

        def small(shape, dt_=F32, parts=P):
            words = math.prod(shape)
            v = arena[0:parts, place[0]:place[0] + words]
            place[0] += words
            if dt_ != F32:
                v = v.bitcast(dt_)
            if len(shape) == 2:
                v = v.rearrange("p (a b) -> p a b", a=shape[0])
            if len(shape) == 3:
                v = v.rearrange("p (a b c) -> p a b c", a=shape[0], b=shape[1])
            return v

        before = small([P])
        ones = small([P])
        lgT = small([T], parts=NG + EXP)
        sel = small([TT, 3, EXP])
        comb = small([TT, EXP])
        assert place[0] <= 98 * KB
        place = [int(92 * KB)]
        lg = small([TT, NG + EXP])
        gp = small([TT, 8])
        top = small([TT, 8])
        topi = small([TT, 8], U32)
        etop = small([TT, 8])
        etopi = small([TT, 8], U32)
        rt = small([TT, 16])
        rank = small([TT, EXP])
        rankc = small([TT, BE])
        counts = small([EXP])
        assert place[0] <= 94 * KB
        wr = at(56, KD * (NG + EXP)).rearrange("p (k e) -> p k e", k=KD)
        wrg = at(58.5, KD * NG).rearrange("p (k g) -> p k g", k=KD)
        wrb = at(61, KD * (NG + EXP)).rearrange("p (k e) -> p k e", k=KD)
        rbias = at(120.5, NG + EXP)
        ab_rows = at(116.5, P, 2 * KD)
        ab = at(121.5, 2 * KD)
        lbias = at(121.75, NG + EXP)
        wrbs = at(120.75, NG + EXP)
        wre = at(59, NG * KD * NE).rearrange("p (g k e) -> p g k e", g=NG, k=KD)
        jm = at(118, JOBS * JOBS).rearrange("p (j x) -> p j x", j=JOBS)
        jb = at(114, 6 * JOBS).rearrange("p (j x) -> p j x", j=6)
        jobtab = at(116, 2 * JOBS).rearrange("p (j x) -> p j x", j=2)
        jobi = at(116.5, JOBS, 1).bitcast(I32)
        jobn = at(117, 1, 1).bitcast(I32)

        ps = ctx.enter_context(nc.psum_tensor("ps", [P, 8, N], F32))

        ab_dram = nc.dram_tensor("scale_shift_scratch", [2, D], F32, kind="Internal").ap()
        gate_dram = nc.dram_tensor("gate_scratch", [2, D], F32, kind="Internal").ap()

        landed = [sem(f"unit_landed_{s}") for s in range(RING)]
        consumed = sem("units_consumed")
        x_landed = sem("x_landed")
        c_landed = sem("c_landed")
        setup_landed = sem("setup_landed")
        wr_landed = sem("router_weights_landed")
        late_landed = sem("late_setup_landed")
        consts_ready = sem("constants_ready")
        blocks_zero = sem("b_blocks_zeroed")
        token_consts = sem("token_sum_constants_ready")
        sum_consts = sem("sum_constants_ready")
        pool_order = sem("pool_order")
        vec_order = sem("vector_order")
        x_squares = sem("x_squares")
        x_var = sem("x_variance")
        x_root = sem("x_root")
        x_rstd = sem("x_rstd")
        x_normed = sem("x_normed")
        x_turned = sem("x_turned")
        x_stored = sem("x_transposes_stored")
        c_silu = sem("c_silu")
        dt_ready = sem("dt_ready")
        decay_in = sem("decay_exponent_ready")
        decay_ready = sem("decay_ready")
        angle_in = sem("angle_reduced")
        angle_ready = sem("angle_sin_cos")
        params_ready = sem("ssm_params_ready")
        b_turned = sem("b_turned")
        cw_turned = sem("conv_weights_turned")
        cw_stored = sem("conv_weights_stored")
        params_turned = sem("ssm_params_turned")
        params_stored = sem("ssm_params_stored")
        bdiag_ready = sem("b_blocks_ready")
        cexp_ready = sem("c_blocks_ready")
        bc_turned = sem("b_c_blocks_turned")
        bc_stored = sem("b_c_blocks_stored")
        phase_ready = sem("table_phase_ready")
        table_sin = sem("table_sin_done")
        table_abs = sem("table_abs_done")
        tables_ready = sem("tables_ready")
        ada_done = sem("ada_part_done")
        ada_copied = sem("ada_part_copied")
        own_ready = sem("own_mask_ready")
        columns_ready = sem("mod_columns_ready")
        parts_ready = sem("mod_parts_ready")
        scaled_x = sem("x_scaled")
        shift_ready = sem("shift1_ready")
        shift_rows = sem("shift_rows_done")
        shift_rows_kept = sem("shift_rows_kept")
        shift_columns = sem("shift_columns_done")
        shift_kept = sem("shift_columns_kept")
        h_ready = sem("h_ready")
        chunk_done = sem("chunk_done")
        chunk_stored = sem("chunk_bank_stored")
        z_ready = sem("z_tiles_ready")
        apart_zero = sem("pairs_apart_zeroed")
        apart_ready = sem("pairs_apart_ready")
        side_done = sem("side_bank_done")
        side_stored = sem("side_bank_stored")
        pads_ready = sem("conv_pads_ready")
        drive_done = sem("drive_done")
        drive_read = sem("drive_read")
        states_ready = sem("states_ready")
        skip_ready = sem("skip_diagonal_ready")
        conv_step = sem("conv_step")
        gated = sem("ssm_gated")
        squares = sem("squares_ready")
        reduced = sem("tiles_added")
        sums = sem("sums_done")
        sum_kept = sem("sums_kept")
        centred = sem("conv_centred")
        scaled = sem("conv_scaled")
        swished = sem("conv_swished")
        ys_ready = sem("ssm_normed")
        yc_ready = sem("conv_normed")
        gate_stored = sem("gate_in_dram")
        gate_landed = sem("gate_landed")
        gate2_landed = sem("gate2_landed")
        gain_landed = sem("final_gain_landed")
        x_again = sem("x_landed_again")
        out_done = sem("out_chunk_done")
        x1_ready = sem("x1_chunk_ready")
        x1_squares = sem("x1_squares")
        n2_var = sem("norm2_variance")
        n2_root = sem("norm2_root")
        n2_rstd = sem("norm2_rstd")
        ab_stored = sem("scale_shift_in_dram")
        ab_landed = sem("scale_shift_rows_landed")
        ab_turned = sem("scale_shift_turned")
        ab_kept = sem("scale_shift_by_channel")
        x1_turned = sem("x1_turned")
        x1_kept = sem("x1_transposes_stored")
        x1_last_kept = sem("x1_last_transposes_stored")
        acc_ready = sem("acc_chunk_ready")
        weights_ready = sem("router_weights_scaled")
        lbias_done = sem("logit_bias_done")
        wr_ready = sem("router_weights_packed")
        logits_done = sem("logits_done")
        logits_biased = sem("logits_biased")
        logits_turned = sem("logits_turned")
        exp_in = sem("router_exp_in")
        exp_done = sem("router_exp_done")
        sel_ready = sem("selection_ready")
        rank_done = sem("rank_done")
        counts_ready = sem("counts_ready")
        jobs_ready = sem("jobs_ready")
        job_order = sem("vector_job_order")
        picks_ready = sem("picks_ready")
        wpicks_ready = sem("weighted_picks_ready")
        gathered = sem("tokens_gathered")
        tok_even = sem("tokens_even_stored")
        tok_odd = sem("tokens_odd_stored")
        picks_turned = sem("picks_turned")
        scatter_ready = sem("scatter_ready")
        gate_done = sem("expert_gate_done")
        gate_silu = sem("expert_gate_silu")
        up_done = sem("expert_up_done")
        hidden_ready = sem("hidden_ready")
        hidden_turned = sem("hidden_turned")
        hidden_stored = sem("hidden_stored")
        down_done = sem("down_done")
        down_stored = sem("down_stored")
        combined = sem("combined")
        added = sem("added")
        fin_sq = sem("final_squares")
        fin_var = sem("final_variance")
        fin_root = sem("final_root")
        fin_out = sem("final_rows_ready")
        out_landed = sem("out_landed")

        w_ada = a["w_ada"][0].rearrange("(p k) n -> k p n", k=KD)
        w_in = a["w_in"][0].rearrange("(p k) n -> p k n", k=KD)
        w_out = a["w_out"][0].rearrange("(k p) n -> p k n", p=P)
        w_gate = a["exp_w_gate"][0].rearrange("g e (p k) f -> (g e) p (k f)", k=KD)
        w_up = a["exp_w_up"][0].rearrange("g e (p k) f -> (g e) p (k f)", k=KD)
        w_down = a["exp_w_down"][0].rearrange("g e (j p) n -> (g e) p j n", p=P)

        def col(v):
            return v.rearrange("(p k) -> p k", k=KD)

        B_LIST, PART_END = [], []
        ada = 0
        for g in range(4, 32):
            if g > 4:
                B_LIST.append((g, "in", g // 4, g % 4))
            for _ in range(3 if g < 20 and g % 2 else 2):
                B_LIST.append((g, "ada", ada // KD, ada % KD))
                ada += 1
                if ada % KD == 0:
                    PART_END.append(g)
            if g == 4:
                B_LIST.append((g, "in", g // 4, g % 4))
        assert len(B_LIST) == B_UNITS

        C_ORDER = [(n, q) for n in range(3) for q in (0, 1)] + [(n, q) for n in range(3) for q in (2, 3)] \
            + [(3, q) for q in range(4)]
        OUT_BANKS = [(0, 1), (4, 5), (2, 3), (0, 1)]

        block = ctx.enter_context(nc.Block())

        @block.sync
        def _(sp):
            sp.dma_start(ccol[:, :], col(a["c"][0])).then_inc(c_landed, 16)
            sp.dma_start(xr[:, 0, :], a["x"][0, 0:P, :]).then_inc(x_landed, 16)
            sp.dma_start(xr[:, 1, :], a["x"][0, P:T, :]).then_inc(x_landed, 16)
            last_user = {}

            def start(n, s, dst, src):
                if s in last_user:
                    sp.wait_ge(consumed, turn(last_user[s]) + 1)
                last_user[s] = n
                sp.dma_start(dst, src).then_inc(landed[s], 16)

            def w_in_unit(n, chunk, k):
                s, _u = ring_use(n)
                c0 = CHUNKS[chunk][0]
                start(n, s, ring[:, s, :].rearrange("p (k n) -> p k n", k=4), w_in[:, 4 * k:4 * k + 4, c0:c0 + N])

            for n in range(A_UNITS):
                if CHUNK_0 <= n < SHIFT:
                    if n == CHUNK_0:
                        sp.wait_ge(x_squares, TT)
                    w_in_unit(n, 0, n - CHUNK_0)
                    continue
                s, _u = ring_use(n)
                part, k = (1, n) if n < CHUNK_0 else (0, n - SHIFT)
                start(n, s, ring[:, s, :], w_ada[k, :, part * D:(part + 1) * D])
            for m in range(B_UNITS):
                n = A_UNITS + m
                s, _u = ring_use(n)
                _g, kind, i, k = B_LIST[m]
                if kind == "in":
                    w_in_unit(n, i, k)
                else:
                    c0 = ADA_PARTS[i] * D
                    start(n, s, ring[:, s, :], w_ada[k, :, c0:c0 + D])
            for m in range(C_UNITS):
                n = A_UNITS + B_UNITS + m
                s, _u = ring_use(n)
                c, q = C_ORDER[m]
                if m == 8:
                    sp.wait_ge(side_done, QUADS)
                    sp.dma_start(x1, a["x"][0].rearrange("(t p) d -> p t d", p=P)).then_inc(x_again, 16)
                start(n, s, ring[:, s, :].rearrange("p (k n) -> p k n", k=4),
                      w_out[:, 4 * q:4 * q + 4, c * N:(c + 1) * N])

            def job_units(j, e0):
                m = 0
                for pr in range(2):
                    for stage in range(3):
                        for u in range(4):
                            for x in range(2):
                                s = m % RING
                                e = e0 + (2 * pr + x)
                                sp.wait_ge(consumed, j * D_UNITS + (D_BASE + m - RING + 1))
                                if stage < 2:
                                    w = (w_gate, w_up)[stage]
                                    src = w[bass.ds(e, 1), :, u * UNIT:(u + 1) * UNIT].rearrange("e p n -> (e p) n")
                                    dst = ring[:, s, :]
                                else:
                                    src = w_down[bass.ds(e, 1), :, :, u * N:(u + 1) * N].rearrange("e p j n -> (e p) j n")
                                    dst = ring[:, s, :].rearrange("p (j n) -> p j n", j=4)
                                sp.dma_start(dst, src).then_inc(landed[s], 16)
                                m += 1

            with sp.Fori(0, NB) as j:
                job_units(j, j * BE)
            sp.wait_ge(jobs_ready, 1)
            n_jobs = sp.value_load(jobn[0:1, 0:1], min_val=NB, max_val=JOBS)
            with sp.If(n_jobs > NB):
                with sp.Fori(NB, n_jobs) as j:
                    e0 = sp.value_load(jobi[0:1, bass.ds(j, 1)], min_val=0, max_val=EXP - BE)
                    job_units(j, e0)
            for n in range(2 * TT):
                t, h = divmod(n, 2)
                cc = slice(h * D // 2, (h + 1) * D // 2)
                sp.wait_ge(fin_out, n + 1)
                sp.dma_start(out[0, t * P:(t + 1) * P, cc], acc[:, t, cc]).then_inc(out_landed, 16)
            sp.wait_ge(out_landed, 16 * 2 * TT)

        @block.tensor
        def _(pe):
            mm = nc.tensor.matmul

            def tr(dst, src, k):
                return nc.tensor.transpose(dst, src, ident[0:k, 0:k])

            def ada_unit(n, bank, k):
                s, u = ring_use(n)
                pe.wait_ge(landed[s], 16 * (u + 1))
                for j in range(4):
                    last = mm(ps[32 * j:32 * j + 32, bank, :], ccol[:, k:k + 1].to_broadcast([P, 32]), ring[:, s, j * N:(j + 1) * N],
                              start=(k == 0), stop=(k == KD - 1), skip_group_check=True)
                return last

            def turn_x(b):
                for k in (2 * b, 2 * b + 1):
                    for t in range(TT):
                        pe.wait_ge(x_normed, t + 1)
                        if b >= 4:
                            pe.wait_ge(x_stored, b - 3)
                        o = (k % 2) * T + t * P
                        last = tr(ps[:, 4 + b % 4, o:o + P], xr[:, t, k:D:KD], P)
                last.then_inc(x_turned, 1)

            def chunk_unit(n, it, u):
                s, use = ring_use(n)
                pe.wait_ge(landed[s], 16 * (use + 1))
                for kk in range(4):
                    k = 4 * u + kk
                    if it == 0:
                        pe.wait_ge(scaled_x, k + 1)
                    if it == 1:
                        pe.wait_ge(h_ready, k + 1)
                    for j in range(4):
                        if k == 0 and it > 0 and j % 2 == 0:
                            pe.wait_ge(chunk_stored, 2 * it - 1 + j // 2)
                        last = mm(ps[:, j // 2, (j % 2) * T:(j % 2 + 1) * T],
                                  ring[:, s, kk * N + j * P:kk * N + (j + 1) * P], hT[:, k, :],
                                  start=(k == 0 and j % 2 == 0), stop=(k == KD - 1), skip_group_check=True)
                return last

            pe.wait_ge(c_silu, 1)
            for k in range(KD):
                ada_unit(k, 0, k).then_inc(consumed, 1)
                if k == 0:
                    pe.wait_ge(consts_ready, 1)
                if 4 <= k < 8:
                    turn_x(2 * (k - 4))
                    turn_x(2 * (k - 4) + 1)
                if k == 9:
                    pe.wait_ge(setup_landed, 16 * 14)
                    for c in range(CT_):
                        tr(ps[:, 2, c * 32:(c + 1) * 32], cwst[:, c * P:(c + 1) * P], 32)
                    tr(ps[:, 2, 256:296], vst, 40).then_inc(cw_turned, 1)
                if k == 11:
                    pe.wait_ge(x_stored, 8)
                    for c in range(2):
                        for h in range(HG):
                            last = tr(ps[:, 4 + c, h * 32:(h + 1) * 32],
                                      bst[:, c, :].rearrange("p (s h) -> p h s", h=HG)[:, h, :], 32)
                    last.then_inc(b_turned, 1)
                if k == 14:
                    pe.wait_ge(params_ready, 1)
                    for i, slot in enumerate((6, 10, 15, 16)):
                        last = tr(ps[:, 3, i * 32:(i + 1) * 32], prm[:, slot, :], 32)
                    last.then_inc(params_turned, 1)
            pe.drain().then_inc(ada_done, 1)
            for u in range(2):
                chunk_unit(CHUNK_0 + u, 0, u)
            pe.wait_ge(cw_stored, 1)
            for k in range(KD):
                ada_unit(SHIFT + k, 2, k).then_inc(consumed, 1)
                if k in (3, 6):
                    chunk_unit(CHUNK_0 + 1 + k // 3, 0, 1 + k // 3)
                if k == 6:
                    pe.drain().then_inc(chunk_done, 1)
                if k >= 8:
                    pe.wait_ge(bdiag_ready, 1)
                    pe.wait_ge(cexp_ready, 1)
                    b = k - 8
                    for q in range(4):
                        c, qq = (b % 4) // 2, (b % 2) * 4 + q
                        if b < 4:
                            src = bdiag[:, c, :, :, :].rearrange("p r g h -> p (r g h)")[:, qq * P:(qq + 1) * P]
                        else:
                            src = cexp[:, c, qq, :, :].rearrange("p g s -> p (g s)")
                        if b >= 4:
                            pe.wait_ge(bc_stored, b - 3)
                        last = tr(ps[:, 4 + b % 4, q * P:(q + 1) * P], src, P)
                    last.then_inc(bc_turned, 1)
            pe.drain().then_inc(ada_done, 1)
            pe.wait_ge(shift_ready, 1)
            pe.wait_ge(params_stored, 1)
            for i in range(4):
                s, _u = ring_use(CHUNK_0 + i)
                for j in range(4):
                    k = 4 * i + j
                    last = mm(ps[32 * j:32 * j + 32, 3, :], mod[:, 0, k:k + 1].to_broadcast([P, 32]),
                              ring[:, s, j * N:(j + 1) * N], start=(i == 0), stop=(i == 3), skip_group_check=True)
                last.then_inc(consumed, 1)
            pe.drain().then_inc(shift_rows, 1)
            pe.wait_ge(shift_rows_kept, 1)
            for j in range(4):
                last = mm(ps[:, 3, j:j + 1], modrow[:, j * P:(j + 1) * P], thirty_second, start=True, stop=True)
            last.then_inc(shift_columns, 1)

            def channel_sum(n):
                pe.wait_ge(sum_consts, 1)
                pe.wait_ge(reduced, n + 1)
                if n < 3:
                    pe.wait_ge(side_stored, sum(g < SUM_AT[n] for g in READ_AT))
                    if n:
                        pe.wait_ge(sum_kept, n)
                else:
                    pe.wait_ge(drive_read, QUADS)
                mm(ps[:, 3 if n < 3 else 7, 0:T], mean_w, csum, start=True, stop=True).then_inc(sums, 1)

            def side(g):
                for job, q in side_jobs(g):
                    if job == "drive":
                        pe.wait_ge(apart_ready, 4 * (q + 1))
                        pe.wait_ge(bc_stored, 8)
                        if q:
                            pe.wait_ge(drive_read, q)
                        for c in range(2):
                            for r in range(4):
                                last = mm(ps[:, 4 + r, c * T:(c + 1) * T], driveT[:, c, q, :], apart[:, r, :],
                                          start=True, stop=True)
                        last.then_inc(drive_done, 1)
                    elif job == "read":
                        if q:
                            pe.wait_ge(side_stored, q)
                        if READ_AT[q] > SUM_AT[0]:
                            pe.wait_ge(sum_kept, sum(g < READ_AT[q] for g in SUM_AT))
                        pe.wait_ge(states_ready, q + 1)
                        pe.wait_ge(skip_ready, q + 1)
                        b = q % 2
                        mm(ps[:, 3, 0:T], skip[:, :], uT[:, q, :], start=True, stop=False, skip_group_check=True)
                        for c, w, x in ((0, 0, 0), (0, 1, 1), (1, 0, 1), (1, 1, 0)):
                            for r in range(4):
                                last = mm(ps[32 * r:32 * r + 32, 3, 0:T], readT[:, c, q, 32 * r:32 * r + 32],
                                          rot[:, b, w, r, x * T:(x + 1) * T], start=False,
                                          stop=(c == 1 and w == 1), skip_group_check=True)
                        last.then_inc(side_done, 1)
                    else:
                        channel_sum(q)

            for g in range(4, 32):
                for m, (step, kind, i, k) in enumerate(B_LIST):
                    if step != g:
                        continue
                    n = A_UNITS + m
                    if kind == "in":
                        chunk_unit(n, i, k).then_inc(consumed, 1)
                        if k == 3:
                            pe.drain().then_inc(chunk_done, 1)
                    else:
                        if k == 0 and i:
                            pe.wait_ge(ada_copied, i)
                        if k == 0 and i == 0:
                            pe.wait_ge(shift_ready, 1)
                        ada_unit(n, 2, k).then_inc(consumed, 1)
                        if k == KD - 1:
                            pe.drain().then_inc(ada_done, 1)
                side(g)
            side(32)

            def out_units(ms):
                for m in ms:
                    c, q = C_ORDER[m]
                    s, use = ring_use(A_UNITS + B_UNITS + m)
                    pe.wait_ge(landed[s], 16 * (use + 1))
                    src, k0 = (uT, 4 * q - 8) if q >= 2 else (conv, 4 * q)
                    if m == 0:
                        pe.wait_ge(chunk_stored, 16)
                        pe.wait_ge(ada_copied, 4)
                        pe.wait_ge(yc_ready, CT_)
                    if m == 4:
                        pe.wait_ge(side_stored, QUADS)
                        pe.wait_ge(sum_kept, 3)
                    if m == 6:
                        pe.wait_ge(ys_ready, CT_)
                    for kk in range(4):
                        for t in range(TT):
                            if m == 12 and kk == 0:
                                pe.wait_ge(x1_ready, t + 1)
                            first = q == 0 and kk == 0
                            end = q == 3 and kk == 3
                            last = mm(ps[:, OUT_BANKS[c][t], :], src[:, k0 + kk, t * P:(t + 1) * P],
                                      ring[:, s, kk * N:(kk + 1) * N], start=first, stop=end, skip_group_check=True)
                    last.then_inc(consumed, 1)
                    if q == 3:
                        pe.drain().then_inc(out_done, 1)

            def turn_x1(n):
                for t in range(TT):
                    pe.wait_ge(x1_ready, 2 * n + t + 1)
                    for h in range(2):
                        if n:
                            pe.wait_ge(x1_kept, 2 * n + h - 1)
                        else:
                            pe.wait_ge(ab_kept, 1)
                        for i in range(2):
                            k = 4 * n + 2 * h + i
                            last = tr(ps[:, 6 + h, i * T + t * P:i * T + (t + 1) * P], x1[:, t, k * P:(k + 1) * P], P)
                        if t == 1:
                            last.then_inc(x1_turned, 1)

            def logits(n):
                for k in range(4 * n, 4 * n + 4):
                    if k < 14:
                        pe.wait_ge(x1_kept, k // 2 + 1)
                    else:
                        pe.wait_ge(x1_last_kept, 1)
                    last = mm(ps[0:NG + EXP, 4, 0:T], wr[:, k, :], x1T[:, k, :], start=(k == 0), stop=(k == KD - 1),
                              skip_group_check=True)
                return last

            out_units([0])
            side(33)
            out_units([1])
            side(34)
            out_units([2, 3])
            channel_sum(3)
            out_units([4])
            pe.wait_ge(ab_landed, 16)
            tr(ps[:, 6, 0:2 * KD], ab_rows, 2 * KD).then_inc(ab_turned, 1)
            out_units(range(5, 10))
            turn_x1(0)
            out_units([10, 11])
            turn_x1(1)
            out_units([12, 13])
            turn_x1(2)
            pe.wait_ge(weights_ready, 1)
            pe.wait_ge(token_consts, 1)
            mm(ps[:, 5, 0:NG + EXP], ones, wrbs, start=True, stop=True).then_inc(lbias_done, 1)
            logits(0)
            logits(1)
            out_units([14, 15])
            logits(2)
            turn_x1(3)
            logits(3).then_inc(logits_done, 1)
            pe.wait_ge(logits_biased, 1)
            for t in range(TT):
                last = tr(ps[:, 1, t * 64:t * 64 + NG + EXP], lgT[:, t * P:(t + 1) * P], NG + EXP)
            last.then_inc(logits_turned, 1)
            pe.wait_ge(sel_ready, 1)
            mm(ps[:, 2, 0:EXP], before, sel[:, 0, 2, :], start=True, stop=True)
            mm(ps[:, 2, EXP:2 * EXP], before, sel[:, 1, 2, :], start=True, stop=False)
            mm(ps[:, 2, EXP:2 * EXP], ones, sel[:, 0, 2, :], start=False, stop=True)
            mm(ps[:, 2, 2 * EXP:3 * EXP], ones, sel[:, 0, 2, :], start=True, stop=False)
            mm(ps[:, 2, 2 * EXP:3 * EXP], ones, sel[:, 1, 2, :], start=False, stop=True).then_inc(rank_done, 1)

            def job(j):
                def gather(pr, u):
                    for k in range(4 * u, 4 * u + 4):
                        if k >= 2:
                            pe.wait_ge((tok_even, tok_odd)[k % 2], j * 16 + 8 * pr + k // 2)
                        for t in range(TT):
                            last = mm(ps[:, 4 + k % 2, 0:P], x1[:, t, k:D:KD], pick[:, t, pr * P:(pr + 1) * P],
                                      start=(t == 0), stop=(t == 1))
                        last.then_inc(gathered, 1)

                pe.wait_ge(picks_ready, j + 1)
                m = 0
                for pr in range(2):
                    gather(pr, 0)
                    for stage in range(3):
                        if stage == 2:
                            pe.wait_ge(hidden_ready, j * 2 + pr + 1)
                            for i in range(4):
                                last = tr(ps[:, 4 + pr, i * P:(i + 1) * P], hid[:, i * P:(i + 1) * P], P)
                            last.then_inc(hidden_turned, 1)
                            pe.wait_ge(hidden_stored, j * 2 + pr + 1)

                        def combine(n):
                            pe.wait_ge(down_stored, j * 8 + pr * 4 + n + 1)
                            if n == 0 and pr == 0:
                                pe.wait_ge(scatter_ready, j + 1)
                            for t in range(TT):
                                if n or pr:
                                    pe.wait_ge(added, j * 16 + pr * 8 + 2 * n + t - 1)
                                mm(ps[:, 6 + t, :], wpickT[:, pr, t * P:(t + 1) * P], yexp[:, n, :],
                                   start=True, stop=True).then_inc(combined, 1)

                        for u in range(4):
                            if stage == 0:
                                if u < 3:
                                    gather(pr, u + 1)
                                elif pr == 0:
                                    pe.wait_ge(wpicks_ready, j + 1)
                                    for p2 in range(2):
                                        for t in range(TT):
                                            last = tr(ps[:, 6 + p2, t * P:(t + 1) * P], wpick[:, t, p2 * P:(p2 + 1) * P], P)
                                    last.then_inc(picks_turned, 1)
                                pe.wait_ge(tok_even, j * 16 + 8 * pr + 2 * u + 2)
                                pe.wait_ge(tok_odd, j * 16 + 8 * pr + 2 * u + 2)
                            for x in range(2):
                                s = (m + x) % RING
                                pe.wait_ge(landed[s], j * 64 + 16 * (D_USES[s] + (m + x) // RING + 1))
                            for kk in range(4):
                                for x in range(2):
                                    s = (m + x) % RING
                                    half = slice(64 * x, 64 * x + 64)
                                    if stage < 2:
                                        k = 4 * u + kk
                                        slot = (2 * pr + x) * SLOTS
                                        last = mm(ps[half, stage, :], xT[:, k, slot:slot + SLOTS],
                                                  ring[:, s, kk * N:(kk + 1) * N], start=(k == 0),
                                                  stop=(k == KD - 1), skip_group_check=True)
                                    else:
                                        last = mm(ps[half, 2 + u % 2, :], hidT[:, kk, half],
                                                  ring[:, s, kk * N:(kk + 1) * N], start=(kk == 0),
                                                  stop=(kk == 3), skip_group_check=True)
                                    if kk == 3:
                                        last.then_inc(consumed, 1)
                            m += 2
                            if stage == 2:
                                pe.drain().then_inc(down_done, 1)
                                if u >= 1:
                                    combine(u - 1)
                        if stage < 2:
                            pe.drain().then_inc((gate_done, up_done)[stage], 1)
                        else:
                            combine(3)

            with pe.Fori(0, NB) as j:
                job(j)
            pe.wait_ge(jobs_ready, 1)
            n_jobs = pe.value_load(jobn[0:1, 0:1], min_val=NB, max_val=JOBS)
            with pe.If(n_jobs > NB):
                with pe.Fori(NB, n_jobs) as j:
                    job(j)

        @block.scalar
        def _(act):
            A = nc.scalar.activation
            for dst, src in (
                (ldt[:, :], a["ssm_log_dt"][0].rearrange("(r g) -> r g", g=2)),
                (prm[:, 0, :], a["ssm_a_re"][0].rearrange("(r g) s -> r (g s)", g=2)),
                (prm[:, 1, :], a["ssm_a_im"][0].rearrange("(r g) s -> r (g s)", g=2)),
                (bst[:, 0, :], a["ssm_b_re"][0].rearrange("(r g) s h -> r (g s h)", g=2)),
                (bst[:, 1, :], a["ssm_b_im"][0].rearrange("(r g) s h -> r (g s h)", g=2)),
                (cst[:, 0, :, :], a["ssm_c_re"][0].rearrange("(q g) h s -> (g h) q s", q=QUADS)),
                (cst[:, 1, :, :], a["ssm_c_im"][0].rearrange("(q g) h s -> (g h) q s", q=QUADS)),
                (cwst[0:TAPS, :], a["conv_w"][0]),
                (cwst[TAPS:TAPS + 1, :], a["conv_b"]),
                (vst[0:8, :], a["conv_ln_g"][0].rearrange("(c p) -> c p", p=P)),
                (vst[8:16, :], a["conv_ln_b"][0].rearrange("(c p) -> c p", p=P)),
                (vst[16:24, :], a["out_norm_conv_g"][0].rearrange("(c p) -> c p", p=P)),
                (vst[24:32, :], a["out_norm_ssm_g"][0].rearrange("(c p) -> c p", p=P)),
                (vst[32:40, :], a["ssm_d"][0].rearrange("(c p) -> c p", p=P)),
            ):
                act.dma_start(dst, src).then_inc(setup_landed, 16)
            for dst, src in (
                (g1[:, :], col(a["norm1_g"][0])),
                (g2[:, :], col(a["norm2_g"][0])),
                (bada1, a["b_ada"][0, 0:2 * D].rearrange("(m p k) -> p m k", m=2, k=KD)),
                (bada[:, :, :], a["b_ada"][0, 2 * D:].rearrange("(m p k) -> p m k", m=4, k=KD)),
            ):
                act.dma_start(dst, src).then_inc(late_landed, 16)

            act.wait_ge(c_landed, 16)
            A(ccol[:, :], ccol[:, :], ACT.Silu).then_inc(c_silu, 1)
            for t in range(TT):
                act.wait_ge(x_landed, 16 * TT)
                A(ring[:, 8 + t, :], xr[:, t, :], ACT.Square, accum_out=ss[:, t:t + 1]).then_inc(x_squares, 1)
            act.wait_ge(x_var, 1)
            A(rstd[:, 2:4], rstd[:, 0:2], ACT.Sqrt).then_inc(x_root, 1)
            for b in range(8):
                act.wait_ge(x_turned, b + 1)
                nc.scalar.copy(hT[:, 2 * b:2 * b + 2, :].rearrange("p k t -> p (k t)"),
                               ps[:, 4 + b % 4, :]).then_inc(x_stored, 1)
            act.wait_ge(setup_landed, 16 * 14)
            A(dt[:, :], ldt[:, :], ACT.Exp).then_inc(dt_ready, 1)
            act.wait_ge(decay_in, 1)
            A(prm[:, 6, :], prm[:, 2, :], ACT.Exp).then_inc(decay_ready, 1)
            act.wait_ge(angle_in, 1)
            A(prm[:, 7, :], prm[:, 5, :], ACT.Sin).then_inc(angle_ready, 1)
            A(prm[:, 9, :], prm[:, 5, :], ACT.Abs).then_inc(angle_ready, 1)
            act.wait_ge(angle_ready, 2)
            A(prm[:, 8, :], prm[:, 9, :], ACT.Sin, scale=-1.0, bias=halfpi[0:32, :]).then_inc(angle_ready, 1)
            def ada_copy(n):
                act.wait_ge(ada_done, n + 3)
                if n:
                    act.wait_ge(columns_ready, n)
                nc.scalar.copy(modrow[:, :], ps[:, 2, :]).then_inc(ada_copied, 1)

            act.wait_ge(phase_ready, 1)
            for b in range(8):
                c, q = (b % 4) // 2, (b % 2) * 4
                act.wait_ge(bc_turned, b + 1)
                dst = (driveT if b < 4 else readT)[:, c, q:q + 4, :].rearrange("p q s -> p (q s)")
                nc.scalar.copy(dst, ps[:, 4 + b % 4, :]).then_inc(bc_stored, 1)

            A(sinT, cosT, ACT.Sin, scale=TWO_PI_DOWN).then_inc(table_sin, 1)
            A(rot128[:, 1, :], rot128[:, 0, :], ACT.Sin, scale=TWO_PI_DOWN).then_inc(table_sin, 1)
            act.wait_ge(table_sin, 2)
            A(cosT, cosT, ACT.Abs).then_inc(table_abs, 1)
            A(rot128[:, 0, :], rot128[:, 0, :], ACT.Abs).then_inc(table_abs, 1)
            act.wait_ge(table_abs, 2)
            A(cosT, cosT, ACT.Sin, scale=-TWO_PI_DOWN, bias=halfpi[:, :]).then_inc(tables_ready, 1)
            A(rot128[:, 0, :], rot128[:, 0, :], ACT.Sin, scale=-TWO_PI_DOWN, bias=halfpi[:, :]).then_inc(tables_ready, 1)
            act.wait_ge(pads_ready, 1)
            KIND = {"u": (ACT.Copy, uT), "gate": (ACT.Sigmoid, zT[:, :, PAD:]), "value": (ACT.Copy, vals),
                    "out_gate": (ACT.Sigmoid, sgT)}
            for g in range(SIDE_STEPS):
                it, u = divmod(g, 4)
                if u == 3 and it < 8:
                    act.wait_ge(chunk_done, it + 1)
                    func, dst = KIND[CHUNKS[it][1]]
                    if it == VALUE_CHUNKS[1]:
                        act.wait_ge(z_ready, 1)
                    if it == 6:
                        act.wait_ge(conv_step, CT_ * TAPS)
                    if it == 0:
                        act.wait_ge(shift_kept, 1)
                        for c in range(4):
                            ins = A(uT[:, c, :], ps[:, c // 2, (c % 2) * T:(c % 2 + 1) * T], ACT.Identity,
                                    bias=chunk_shift[:, c:c + 1])
                            if c % 2:
                                ins.then_inc(chunk_stored, 1)
                    for b in range(2 if it else 0):
                        c = (0 if CHUNKS[it][1] == "value" else FIRST_TILE[it]) + 2 * b
                        A(dst[:, c:c + 2, :], ps[:, b, :].rearrange("p (c t) -> p c t", c=2), func).then_inc(chunk_stored, 1)
                if g in PART_END:
                    ada_copy(PART_END.index(g))
                for job, q in side_jobs(g):
                    if job == "read":
                        act.wait_ge(side_done, q + 1)
                        A(uT[:, q, :], ps[:, 3, 0:T], ACT.Gelu_apprx_tanh).then_inc(side_stored, 1)
                    if job == "sum":
                        act.wait_ge(sums, q + 1)
                        if q == 0:
                            nc.scalar.copy(stat[:, 0, :], ps[:, 3, 0:T]).then_inc(sum_kept, 1)
                        else:
                            if q == 2:
                                act.wait_ge(centred, 1)
                            A(stat[:, q % 2, :], ps[:, 3, 0:T], ACT.Sqrt, bias=eps[:, :]).then_inc(sum_kept, 1)
                if g + 1 in DRIVE_AT:
                    q = DRIVE_AT.index(g + 1)
                    act.wait_ge(apart_zero, 1)
                    act.wait_ge(chunk_stored, tile_stored(q))
                    if q:
                        act.wait_ge(drive_done, q)
                    for r in range(4):
                        rr = slice(32 * r, 32 * r + 32)
                        nc.scalar.copy(apart[rr, r, :], uT[rr, q, :]).then_inc(apart_ready, 1)
                if g == SUM_AT[0] + 1:
                    act.wait_ge(centred, 1)
                    A(sq, conv, ACT.Square).then_inc(squares, 1)
                if g == SUM_AT[1] + 1:
                    act.wait_ge(scaled, 1)
                    for c in range(CT_):
                        A(conv[:, c, :], conv[:, c, :], ACT.Silu, scale=vT[:, 0, c:c + 1],
                          bias=vT[:, 1, c:c + 1]).then_inc(swished, 1)
                    act.wait_ge(swished, CT_)
                    A(sq, conv, ACT.Square).then_inc(squares, 1)

                if g == 14:
                    act.wait_ge(parts_ready, 1)
                    act.dma_start(col(gate_dram[0]), mod[:, 2, :]).then_inc(gate_stored, 16)
                if g == 26:
                    act.wait_ge(parts_ready, 3)
                    for i, part in enumerate((4, 3)):
                        act.dma_start(col(ab_dram[i]), mod[:, part, :]).then_inc(ab_stored, 16)
                if g == 30:
                    act.wait_ge(ab_stored, 32)
                    act.wait_ge(z_ready, 2)
                    act.dma_start(ab_rows, ab_dram.rearrange("i (k p) -> (i k) p", p=P)).then_inc(ab_landed, 16)

            act.wait_ge(gate_stored, 16)
            act.dma_start(gate1, gate_dram[0:1, :].to_broadcast([P, D])).then_inc(gate_landed, 16)
            act.wait_ge(gated, 1)
            A(sq, uT, ACT.Square).then_inc(squares, 1)
            for dst, src in (
                (wrg, a["router_group_w"][0].rearrange("(k p) g -> p k g", k=KD)),
                (wre[:, 0], a["router_expert_w"][0, 0].rearrange("(k p) e -> p k e", k=KD)),
                (wre[:, 1], a["router_expert_w"][0, 1].rearrange("(k p) e -> p k e", k=KD)),
                (wre[:, 2], a["router_expert_w"][0, 2].rearrange("(k p) e -> p k e", k=KD)),
                (wre[:, 3], a["router_expert_w"][0, 3].rearrange("(k p) e -> p k e", k=KD)),
                (rbias[:, 0:NG], a["router_group_b"].to_broadcast([P, NG])),
                (rbias[:, NG:], a["router_expert_b"].rearrange("o g e -> o (g e)").to_broadcast([P, EXP])),
            ):
                act.dma_start(dst, src).then_inc(wr_landed, 16)
            act.wait_ge(sums, 4)
            act.wait_ge(scaled, 1)
            A(stat[:, 1, :], ps[:, 7, 0:T], ACT.Sqrt, bias=eps[:, :]).then_inc(sum_kept, 1)
            act.wait_ge(parts_ready, 4)
            act.dma_start(col(gate_dram[1]), mod[:, 5, :]).then_inc(gate_stored, 16)

            def turned(n, h):
                act.wait_ge(x1_turned, 2 * n + h + 1)
                nc.scalar.copy(x1T[:, 4 * n + 2 * h:4 * n + 2 * h + 2, :].rearrange("p k t -> p (k t)"),
                               ps[:, 6 + h, :]).then_inc(x1_kept, 1)

            def square_x1(c):
                for t in range(TT):
                    n = 2 * c + t
                    act.wait_ge(x1_ready, n + 1)
                    if n:
                        act.wait_ge(x1_squares, n)
                    A(x1sq, x1[:, t, c * N:(c + 1) * N], ACT.Square,
                      accum_out=ss[:, t * 4 + c:t * 4 + c + 1]).then_inc(x1_squares, 1)

            square_x1(0)
            square_x1(1)
            for c in range(3):
                for h in range(2):
                    turned(c, h)
                if c == 0:
                    square_x1(2)
            square_x1(3)
            turned(3, 0)
            act.wait_ge(n2_var, 1)
            A(rstd[:, 2:4], rstd[:, 0:2], ACT.Sqrt).then_inc(n2_root, 1)
            act.wait_ge(logits_done, 1)
            nc.scalar.copy(lgT[:, :], ps[0:NG + EXP, 4, 0:T]).then_inc(logits_biased, 1)
            act.wait_ge(exp_in, 1)
            A(rt[:, :, 0:4], rt[:, :, 0:4], ACT.Exp).then_inc(exp_done, 1)
            act.wait_ge(exp_in, 2)
            A(rt[:, :, 6:7], rt[:, :, 5:6], ACT.Exp).then_inc(exp_done, 1)
            for t in range(TT):
                nc.scalar.copy(acc[:, t, :], x1[:, t, :]).then_inc(acc_ready, 1)
            act.wait_ge(gate_stored, 32)
            act.dma_start(gate2, gate_dram[1:2, :].to_broadcast([P, D])).then_inc(gate2_landed, 16)
            act.dma_start(fgain, a["final_norm_g"].rearrange("(o d) -> o d", o=1).to_broadcast([P, D])).then_inc(gain_landed, 16)

            def job(j):
                for pr in range(2):
                    for k in range(1, KD, 2):
                        act.wait_ge(gathered, j * 2 * KD + pr * KD + k + 1)
                        A(xT[:, k, pr * P:(pr + 1) * P], ps[:, 5, 0:P], ACT.Identity, scale=mod[:, 4, k:k + 1],
                          bias=mod[:, 3, k:k + 1]).then_inc(tok_odd, 1)
                    act.wait_ge(gate_done, j * 2 + pr + 1)
                    A(silu, ps[:, 0, :], ACT.Silu).then_inc(gate_silu, 1)
                    act.wait_ge(hidden_turned, j * 2 + pr + 1)
                    nc.scalar.copy(hidT.rearrange("p j s -> p (j s)"), ps[:, 4 + pr, :]).then_inc(hidden_stored, 1)
                for m in range(8):
                    n, t = divmod(m, 2)
                    act.wait_ge(added, j * 16 + 8 + m + 1)
                    if m:
                        act.wait_ge(fin_sq, j * 8 + m)
                    A(junk, acc[:, t, n * N:(n + 1) * N], ACT.Square, accum_out=ss[:, t * 4 + n:t * 4 + n + 1]).then_inc(fin_sq, 1)
                act.wait_ge(fin_sq, j * 8 + 8)

            with act.Fori(0, NB) as j:
                job(j)
            act.wait_ge(jobs_ready, 1)
            n_jobs = act.value_load(jobn[0:1, 0:1], min_val=NB, max_val=JOBS)
            with act.If(n_jobs > NB):
                with act.Fori(NB, n_jobs) as j:
                    job(j)
            act.wait_ge(fin_var, 1)
            A(rstd[:, 2:4], rstd[:, 0:2], ACT.Sqrt).then_inc(fin_root, 1)

        @block.gpsimd
        def _(pool):
            gp_ = nc.gpsimd
            n = [0]

            def link(ins):
                n[0] += 1
                ins.then_inc(pool_order, 1)
                pool.wait_ge(pool_order, n[0])

            link(gp_.memset(ident[:, :], 0.0))
            link(gp_.affine_select(out=ident[:, :], in_=ident[:, :], compare_op=ALU.not_equal, fill=1.0, base=0,
                                   pattern=[[-1, P]], channel_multiplier=1))
            link(gp_.iota(iota_i, pattern=[[1, P]], base=0, channel_multiplier=0))
            link(gp_.iota(part_i, pattern=[[0, 1]], base=0, channel_multiplier=1))
            link(gp_.memset(halfpi[:, :], math.pi / 2))
            link(gp_.memset(thirty_second, 1.0 / 32))
            gp_.memset(eps[:, :], EPS).then_inc(consts_ready, 1)
            gp_.memset(at(114, 8 * KB), 0.0).then_inc(blocks_zero, 1)

            def diagonal(q):
                if q:
                    pool.wait_ge(side_done, q)
                gp_.tensor_scalar(skip[:, :], ident[:, :], vT[:, 4, q:q + 1], None, ALU.mult).then_inc(skip_ready, 1)

            def columns(n):
                pool.wait_ge(ada_copied, n + 1)
                row = modrow[:, :].rearrange("p (i k) -> p i k", k=KD)
                link(gp_.tensor_tensor(row, row, own[:, :].unsqueeze(2).to_broadcast([P, 32, KD]), ALU.mult))
                w = 16
                while w > 1:
                    link(gp_.tensor_tensor(row[:, 0:w, :], row[:, 0:w, :], row[:, w:2 * w, :], ALU.add))
                    w //= 2
                part = mod[:, ADA_PARTS[n], :]
                gp_.tensor_tensor(part, row[:, 0, :], row[:, 1, :], ALU.add).then_inc(columns_ready, 1)
                pool.wait_ge(columns_ready, n + 1)
                pool.wait_ge(late_landed, 16 * 4)
                last = gp_.tensor_tensor(part, part, bada[:, n, :], ALU.add)
                if ADA_PARTS[n] == 4:
                    link(last)
                    link(gp_.tensor_scalar(part, part, 1.0, None, ALU.add))
                    last = gp_.tensor_tensor(part, part, g2[:, :], ALU.mult)
                last.then_inc(parts_ready, 1)

            pool.wait_ge(own_ready, 1)
            pool.wait_ge(cw_stored, 1)
            def z_tiles(h):
                pool.wait_ge(chunk_stored, 2 * VALUE_CHUNKS[h] + 2)
                z = zT[:, 4 * h:4 * h + 4, PAD:]
                return gp_.tensor_tensor(z, z, vals, ALU.mult).then_inc(z_ready, 1)

            pool.wait_ge(bc_turned, 8)
            gp_.memset(apart, 0.0).then_inc(apart_zero, 1)
            for q in range(5):
                diagonal(q)
                if q == 2:
                    columns(0)
            z_tiles(0)
            columns(1)
            z_tiles(1)
            pool.wait_ge(z_ready, 2)
            gp_.memset(mean_w, 1.0 / CH).then_inc(sum_consts, 1)
            columns(2)
            for q in range(5, QUADS):
                diagonal(q)
            columns(3)
            pool.wait_ge(side_done, QUADS)
            link(gp_.memset(ones, 1.0))
            gp_.affine_select(out=before, in_=ones, compare_op=ALU.is_gt, fill=0.0, base=0,
                              pattern=[[1, P]], channel_multiplier=-1).then_inc(token_consts, 1)
            pool.wait_ge(wr_landed, 16 * 7)
            gp_.tensor_copy(wr[:, :, 0:NG], wrg[:, :, :]).then_inc(wr_ready, 1)
            gp_.tensor_copy(wr[:, :, NG:].rearrange("p k (g e) -> p g k e", g=NG), wre[:, :, :, :]).then_inc(wr_ready, 1)

            pool.wait_ge(counts_ready, 1)
            rounds = JOBS // NB
            most, flag, pos, e0, r0 = (jb[:, i, :] for i in range(5))
            over = jm[:, 0, 0:EXP]
            link(gp_.memset(flag[:, 0:NB], 1.0))
            for r in range(rounds):
                rb = slice(r * NB, (r + 1) * NB)
                if r:
                    link(gp_.tensor_scalar(over, counts, float(r * SLOTS), None, ALU.is_gt))
                    link(gp_.tensor_tensor(jm[:, 1, 0:16], over[:, 0:EXP:2], over[:, 1:EXP:2], ALU.add))
                    link(gp_.tensor_tensor(flag[:, rb], jm[:, 1, 0:16:2], jm[:, 1, 1:16:2], ALU.add))
                    link(gp_.tensor_scalar(flag[:, rb], flag[:, rb], 1.0, None, ALU.min))
                link(gp_.tensor_scalar(e0[:, rb], iota[:, 0:NB], float(BE), None, ALU.mult))
                link(gp_.memset(r0[:, rb], float(r * SLOTS)))
            link(gp_.memset(jm, 1.0))
            link(gp_.affine_select(out=jm, in_=jm, compare_op=ALU.is_gt, fill=0.0, base=0,
                                   pattern=[[1, JOBS], [-1, JOBS]], channel_multiplier=0))
            link(gp_.tensor_tensor(jm, jm, flag.unsqueeze(1).to_broadcast([P, JOBS, JOBS]), ALU.mult))

            def row_sums(dst):
                w = JOBS // 2
                while w:
                    link(gp_.tensor_tensor(jm[:, :, 0:w], jm[:, :, 0:w], jm[:, :, w:2 * w], ALU.add))
                    w //= 2
                link(gp_.tensor_copy(dst, jm[:, :, 0]))

            row_sums(pos)
            link(gp_.tensor_tensor(most, pos, flag, ALU.add))
            link(gp_.tensor_copy(jobn, most[0:1, JOBS - 1:JOBS]))
            link(gp_.tensor_scalar(jb[:, 5, :], flag, -1000.0, 1000.0, ALU.mult, ALU.add))
            link(gp_.tensor_tensor(pos, pos, jb[:, 5, :], ALU.add))
            for i, val in enumerate((e0, r0)):
                link(gp_.tensor_tensor(jm, pos.unsqueeze(1).to_broadcast([P, JOBS, JOBS]),
                                       iota[:, 0:JOBS].unsqueeze(2).to_broadcast([P, JOBS, JOBS]), ALU.subtract))
                link(gp_.tensor_scalar(jm, jm, 0.0, None, ALU.is_equal))
                link(gp_.tensor_tensor(jm, jm, val.unsqueeze(1).to_broadcast([P, JOBS, JOBS]), ALU.mult))
                row_sums(jobtab[:, i, :])
            gp_.tensor_copy(jobi, jobtab[0:1, 0, :]).then_inc(jobs_ready, 1)

        @block.vector
        def _(dve):
            V = nc.vector
            n = [0]

            def link(ins):
                n[0] += 1
                ins.then_inc(vec_order, 1)
                dve.wait_ge(vec_order, n[0])

            dve.wait_ge(consts_ready, 1)
            link(V.tensor_copy(steps, iota_i))
            link(V.tensor_copy(iota[:, :], steps[:, 0:SLOTS]))
            link(V.tensor_scalar(part_i, part_i, 4, 1, ALU.logical_shift_right, ALU.bitwise_and))
            link(V.tensor_copy(odd[:, 1:2], part_i))
            link(V.tensor_scalar(odd[:, 0:1], odd[:, 1:2], -1.0, 1.0, ALU.mult, ALU.add))
            V.tensor_reduce(own[:, :], ident[:, :].rearrange("p (b i) -> p i b", b=4), AX.X, ALU.add).then_inc(own_ready, 1)
            dve.wait_ge(x_squares, TT)
            V.tensor_scalar(rstd[:, 0:2], ss[:, 0:2], 1.0 / D, EPS, ALU.mult, ALU.add).then_inc(x_var, 1)
            dve.wait_ge(x_root, 1)
            V.reciprocal(rstd[:, 0:2], rstd[:, 2:4]).then_inc(x_rstd, 1)
            dve.wait_ge(x_rstd, 1)
            for t in range(TT):
                V.tensor_scalar(xr[:, t, :], xr[:, t, :], rstd[:, t:t + 1], None, ALU.mult).then_inc(x_normed, 1)
            re, im, red, ang, k_, r_ = (prm[:, i, :] for i in range(6))
            mag, sin_, cos_, absr, turns = (prm[:, i, :] for i in (6, 7, 8, 9, 10))
            nr, ni, t1, t2, f_re, f_im, rden = (prm[:, i, :] for i in (11, 12, 13, 14, 15, 16, 17))
            dve.wait_ge(dt_ready, 1)
            dtb = dt[:, :].unsqueeze(2).to_broadcast([32, 2, S])

            def by_group(v):
                return v.rearrange("p (g s) -> p g s", g=2)

            V.tensor_tensor(by_group(red), by_group(re), dtb, ALU.mult).then_inc(decay_in, 1)
            link(V.tensor_tensor(by_group(ang), by_group(im), dtb, ALU.mult))
            link(V.tensor_scalar(k_, ang, 1.0 / (2 * math.pi), MAGIC, ALU.mult, ALU.add))
            link(V.tensor_scalar(k_, k_, MAGIC, None, ALU.subtract))
            link(V.scalar_tensor_tensor(r_, k_, -C1, ang, ALU.mult, ALU.add))
            link(V.scalar_tensor_tensor(r_, k_, -C2, r_, ALU.mult, ALU.add))
            link(V.scalar_tensor_tensor(r_, k_, -C3, r_, ALU.mult, ALU.add))
            link(V.tensor_scalar(r_, r_, PI_DOWN, -PI_DOWN, ALU.min, ALU.max))
            V.tensor_scalar(turns, r_, 1.0 / (2 * math.pi), None, ALU.mult).then_inc(angle_in, 1)
            dve.wait_ge(decay_ready, 1)
            dve.wait_ge(angle_ready, 3)
            link(V.tensor_tensor(nr, mag, cos_, ALU.mult))
            link(V.tensor_tensor(ni, mag, sin_, ALU.mult))
            link(V.tensor_scalar(nr, nr, 1.0, None, ALU.subtract))
            link(V.tensor_tensor(t1, re, re, ALU.mult))
            link(V.tensor_tensor(t2, im, im, ALU.mult))
            link(V.tensor_tensor(t1, t1, t2, ALU.add))
            link(V.reciprocal(rden, t1))
            link(V.tensor_tensor(t1, nr, re, ALU.mult))
            link(V.tensor_tensor(t2, ni, im, ALU.mult))
            link(V.tensor_tensor(t1, t1, t2, ALU.add))
            link(V.tensor_tensor(f_re, t1, rden, ALU.mult))
            link(V.tensor_tensor(t1, ni, re, ALU.mult))
            link(V.tensor_tensor(t2, nr, im, ALU.mult))
            link(V.tensor_tensor(t1, t1, t2, ALU.subtract))
            V.tensor_tensor(f_im, t1, rden, ALU.mult).then_inc(params_ready, 1)
            dve.wait_ge(cw_turned, 1)
            link(V.tensor_copy(cwT[:, :, :].rearrange("p c t -> p (c t)"), ps[:, 2, 0:256]))
            V.tensor_copy(vT[:, :, :].rearrange("p n c -> p (n c)"), ps[:, 2, 256:296]).then_inc(cw_stored, 1)
            def columns(bank, part):
                dve.wait_ge(ada_done, 1 + bank // 2)
                link(V.tensor_tensor(modrow[:, :].rearrange("p (i k) -> p i k", k=KD),
                                     ps[:, bank, :].rearrange("p (i k) -> p i k", k=KD),
                                     own[:, :].unsqueeze(2).to_broadcast([P, 32, KD]), ALU.mult))
                link(V.tensor_reduce(mod[:, part, :], modrow[:, :].rearrange("p (i k) -> p k i", k=KD), AX.X, ALU.add))

            dve.wait_ge(late_landed, 16 * 4)
            columns(0, 1)
            link(V.tensor_tensor(mod[:, 1, :], mod[:, 1, :], bada1[:, 1, :], ALU.add))
            link(V.scalar_tensor_tensor(mod[:, 1, :], mod[:, 1, :], 1.0, g1[:, :], ALU.add, ALU.mult))
            dve.wait_ge(x_stored, 8)
            for k in range(KD):
                V.tensor_scalar(hT[:, k, :], hT[:, k, :], mod[:, 1, k:k + 1], None, ALU.mult).then_inc(scaled_x, 1)
            dve.wait_ge(scaled_x, KD)
            dve.wait_ge(setup_landed, 16 * 14)
            for c in range(2):
                for g in range(2):
                    ins = V.tensor_scalar(cexp[:, c, :, g, :], cst[:, c, :, :], odd[:, g:g + 1], None, ALU.mult)
                    if c == 0 or g == 0:
                        link(ins)
                    else:
                        ins.then_inc(cexp_ready, 1)
            dve.wait_ge(params_turned, 1)
            V.tensor_copy(par[:, :, :].rearrange("p n q -> p (n q)"), ps[:, 3, 0:128]).then_inc(params_stored, 1)
            dve.wait_ge(params_stored, 1)
            link(V.tensor_copy(decay[:, :], par[:, 0, :]))
            dve.wait_ge(b_turned, 1)
            dve.wait_ge(blocks_zero, 1)
            b_re, b_im = (ps[:, 4 + c, :].rearrange("p (h r) -> p r h", h=HG) for c in range(2))
            fr, fi = (par[:, i, :].unsqueeze(2).to_broadcast([P, PAIRS, HG]) for i in (2, 3))
            m1, m2 = (btmp[:, i, 0:N].rearrange("p (r h) -> p r h", h=HG) for i in range(2))
            for c, (p1, p2, op) in enumerate(((b_re, b_im, ALU.subtract), (b_im, b_re, ALU.add))):
                link(V.tensor_tensor(m1, p1, fr, ALU.mult))
                link(V.tensor_tensor(m2, p2, fi, ALU.mult))
                for g in range(2):
                    half = slice(64 * g, 64 * g + 64)
                    ins = V.tensor_tensor(bdiag[half, c, :, g, :], m1[half], m2[half], op)
                    if c == 1 and g == 1:
                        ins.then_inc(bdiag_ready, 1)
                    else:
                        link(ins)
            th = par[:, 1, :].unsqueeze(2).to_broadcast([P, PAIRS, HALF])
            link(V.tensor_tensor(cosT, th, steps.unsqueeze(1).to_broadcast([P, PAIRS, HALF]), ALU.mult))
            link(V.tensor_scalar(sinT, cosT, MAGIC, MAGIC, ALU.add, ALU.subtract))
            link(V.tensor_tensor(cosT, cosT, sinT, ALU.subtract))
            link(V.tensor_scalar(rot128[:, 0, :], par[:, 1, :], float(HALF), None, ALU.mult))
            link(V.tensor_scalar(rot128[:, 1, :], rot128[:, 0, :], MAGIC, MAGIC, ALU.add, ALU.subtract))
            V.tensor_tensor(rot128[:, 0, :], rot128[:, 0, :], rot128[:, 1, :], ALU.subtract).then_inc(phase_ready, 1)
            columns(2, 0)
            V.tensor_tensor(mod[:, 0, :], mod[:, 0, :], bada1[:, 0, :], ALU.add).then_inc(shift_ready, 1)
            dve.wait_ge(shift_ready, 1)
            dve.wait_ge(shift_rows, 1)
            V.tensor_copy(modrow[:, :], ps[:, 3, :]).then_inc(shift_rows_kept, 1)
            dve.wait_ge(chunk_done, 1)
            for k in range(KD):
                V.tensor_scalar(hT[:, k, :], hT[:, k, :], mod[:, 0, k:k + 1], None, ALU.add).then_inc(h_ready, 1)
                if k == 3:
                    dve.wait_ge(shift_columns, 1)
                    V.tensor_copy(chunk_shift, ps[:, 3, 0:4]).then_inc(shift_kept, 1)
            dve.wait_ge(bc_stored, 8)
            V.memset(zT[:, :, 0:PAD], 0.0).then_inc(pads_ready, 1)

            dve.wait_ge(tables_ready, 2)
            def quad(q, middle=None):
                b = q % 2
                c4 = cosT[:, 4 * q:4 * q + 4, :].unsqueeze(2).to_broadcast([P, 4, 4, HALF])
                s4 = sinT[:, 4 * q:4 * q + 4, :].unsqueeze(2).to_broadcast([P, 4, 4, HALF])
                s2 = sinT[:, 4 * q:4 * q + 4, :].unsqueeze(2).to_broadcast([P, 4, 2, HALF])
                drive = ps[:, 4:8, :].rearrange("p r (x t) -> p r x t", x=4)
                r1 = rot[:, b, 0, :, :]
                r2 = rot[:, b, 1, :, :]
                r1v = r1.rearrange("p r (x t) -> p r x t", x=4)
                r2v = r2.rearrange("p r (x t) -> p r x t", x=4)
                dve.wait_ge(drive_done, q + 1)
                if q >= 2:
                    dve.wait_ge(side_done, q - 1)
                link(V.tensor_tensor(r1v, drive, c4, ALU.mult))
                V.tensor_tensor(r2v, drive, s4, ALU.mult).then_inc(drive_read, 1)
                dve.wait_ge(drive_read, q + 1)
                link(V.tensor_tensor(r1[:, :, 0:T], r1[:, :, 0:T], r2[:, :, T:2 * T], ALU.add))
                link(V.tensor_tensor(r1[:, :, T:2 * T], r2[:, :, 0:T], r1[:, :, T:2 * T], ALU.subtract))
                for half in range(2):
                    for r in range(4):
                        m = decay[:, 4 * q + r:4 * q + r + 1].to_broadcast([P, HALF])
                        for x in range(2):
                            z = r1[:, r, x * T + half * HALF:x * T + (half + 1) * HALF]
                            init = carry[:, 2, r, x:x + 1] if half else 0.0
                            n[0] += 1
                            V.tensor_tensor_scan(z, m, z, init, ALU.mult, ALU.add).then_inc(vec_order, 1)
                    dve.wait_ge(vec_order, n[0])
                    if half == 0:
                        end = r1.rearrange("p r (x t) -> p r x t", x=2)[:, :, :, HALF - 1]
                        cc, sc = (rot128[:, i, 4 * q:4 * q + 4].unsqueeze(2).to_broadcast([P, 4, 2]) for i in range(2))
                        link(V.tensor_tensor(carry[:, 0, :, :], end, cc, ALU.mult))
                        link(V.tensor_tensor(carry[:, 1, :, :], end, sc, ALU.mult))
                        link(V.tensor_tensor(carry[:, 2, :, 0], carry[:, 0, :, 0], carry[:, 1, :, 1], ALU.add))
                        link(V.tensor_tensor(carry[:, 2, :, 1], carry[:, 0, :, 1], carry[:, 1, :, 0], ALU.subtract))
                if middle:
                    middle()
                link(V.tensor_scalar(r2[:, :, 0:T], r1[:, :, 0:T], -1.0, None, ALU.mult))
                link(V.tensor_tensor(r2v[:, :, 0:2, :], r2v[:, :, 0:2, :], s2, ALU.mult))
                link(V.tensor_tensor(r2v[:, :, 2:4, :], r1v[:, :, 2:4, :], s2, ALU.mult))
                V.tensor_tensor(r1v, r1v, c4, ALU.mult).then_inc(states_ready, 1)
                dve.wait_ge(states_ready, q + 1)

            def convolve(h):
                dve.wait_ge(z_ready, h + 1)
                for j in range(TAPS):
                    for i in range(4):
                        c = 4 * h + i
                        done = 4 * (TAPS * h + j) + i
                        z = zT[:, c, j:j + T]
                        if j == 0:
                            ins = V.tensor_scalar(conv[:, c, :], z, cwT[:, c, 0:1], cwT[:, c, TAPS:TAPS + 1],
                                                  ALU.mult, ALU.add)
                        else:
                            dve.wait_ge(conv_step, done - 3)
                            ins = V.scalar_tensor_tensor(conv[:, c, :], z, cwT[:, c, j:j + 1], conv[:, c, :],
                                                         ALU.mult, ALU.add)
                        ins.then_inc(conv_step, 1)

            def over_tiles(v):
                return v.unsqueeze(1).to_broadcast([P, CT_, T])

            def add_tiles(v):
                V.tensor_reduce(csum, v.rearrange("p c t -> p t c"), AX.X, ALU.add).then_inc(reduced, 1)

            def centre():
                dve.wait_ge(sum_kept, 1)
                V.tensor_tensor(conv, conv, over_tiles(stat[:, 0, :]), ALU.subtract).then_inc(centred, 1)

            def add_squares(n):
                dve.wait_ge(squares, n)
                dve.wait_ge(sums, n)
                add_tiles(sq)

            def scale_conv():
                dve.wait_ge(sum_kept, 2)
                dve.wait_ge(centred, 1)
                link(V.reciprocal(stat[:, 1, :], stat[:, 1, :]))
                V.tensor_tensor(conv, conv, over_tiles(stat[:, 1, :]), ALU.mult).then_inc(scaled, 1)

            def norm_conv():
                dve.wait_ge(sum_kept, 3)
                link(V.reciprocal(stat[:, 0, :], stat[:, 0, :]))
                for c in range(CT_):
                    V.scalar_tensor_tensor(conv[:, c, :], conv[:, c, :], vT[:, 2, c:c + 1], stat[:, 0, :], ALU.mult,
                                           ALU.mult).then_inc(yc_ready, 1)

            for q in range(4):
                quad(q)
            convolve(0)
            convolve(1)
            dve.wait_ge(sum_consts, 1)
            dve.wait_ge(conv_step, CT_ * TAPS)
            add_tiles(conv)
            quad(4, centre)
            add_squares(1)
            quad(5, scale_conv)
            add_squares(2)
            quad(6, norm_conv)
            quad(7)
            dve.wait_ge(chunk_stored, 16)
            dve.wait_ge(side_stored, QUADS)
            V.tensor_tensor(uT, uT, sgT, ALU.mult).then_inc(gated, 1)
            dve.wait_ge(squares, 3)
            add_tiles(sq)
            dve.wait_ge(sum_kept, 4)
            dve.wait_ge(gated, 1)
            link(V.reciprocal(stat[:, 1, :], stat[:, 1, :]))
            for c in range(CT_):
                V.scalar_tensor_tensor(uT[:, c, :], uT[:, c, :], vT[:, 3, c:c + 1], stat[:, 1, :], ALU.mult,
                                       ALU.mult).then_inc(ys_ready, 1)
            dve.wait_ge(ab_turned, 1)
            V.tensor_copy(ab, ps[:, 6, 0:2 * KD]).then_inc(ab_kept, 1)
            dve.wait_ge(ab_kept, 1)
            dve.wait_ge(parts_ready, 3)
            dve.wait_ge(gate_landed, 16)
            dve.wait_ge(x_again, 16)
            for m in range(8):
                c, t = divmod(m, 2)
                if m == 4:
                    dve.wait_ge(wr_ready, 2)
                    scale, shift = (ab[:, i * KD:(i + 1) * KD].unsqueeze(2).to_broadcast([P, KD, NG + EXP]) for i in range(2))
                    link(V.tensor_tensor(wrb, wr, shift, ALU.mult))
                    link(V.tensor_reduce(wrbs, wrb.rearrange("p k e -> p e k"), AX.X, ALU.add))
                    V.tensor_tensor(wr, wr, scale, ALU.mult).then_inc(weights_ready, 1)
                dve.wait_ge(out_done, c + 1)
                link(V.tensor_tensor(gtmp[:, t, :], ps[:, OUT_BANKS[c][t], :], gate1[:, c * N:(c + 1) * N], ALU.mult))
                cc = slice(c * N, (c + 1) * N)
                V.tensor_tensor(x1[:, t, cc], x1[:, t, cc], gtmp[:, t, :], ALU.add).then_inc(x1_ready, 1)
                dve.wait_ge(x1_ready, m + 1)
            dve.wait_ge(x1_turned, 8)
            V.tensor_copy(x1T[:, 14:16, :].rearrange("p k t -> p (k t)"), ps[:, 7, :]).then_inc(x1_last_kept, 1)
            dve.wait_ge(x1_squares, 8)
            link(V.tensor_reduce(rstd[:, 0:2], ss[:, :].rearrange("p (t c) -> p t c", t=TT), AX.X, ALU.add))
            V.tensor_scalar(rstd[:, 0:2], rstd[:, 0:2], 1.0 / D, EPS, ALU.mult, ALU.add).then_inc(n2_var, 1)
            dve.wait_ge(n2_root, 1)
            V.reciprocal(rstd[:, 0:2], rstd[:, 2:4]).then_inc(n2_rstd, 1)
            dve.wait_ge(n2_rstd, 1)
            dve.wait_ge(lbias_done, 1)
            link(V.tensor_tensor(lbias, ps[:, 5, 0:NG + EXP], rbias, ALU.add))
            link(V.memset(gp[:, :, :], -3.0e38))

            dve.wait_ge(logits_turned, 1)
            for t in range(TT):
                link(V.scalar_tensor_tensor(lg[:, t, :], ps[:, 1, t * 64:t * 64 + NG + EXP], rstd[:, t:t + 1], lbias,
                                            ALU.mult, ALU.add))
            link(V.tensor_copy(gp[:, :, 0:NG], lg[:, :, 0:NG]))
            for t in range(TT):
                link(V.max(top[:, t, :], gp[:, t, :]))
                link(V.max_index(topi[:, t, :], top[:, t, :], gp[:, t, :]))
            V.tensor_tensor(rt[:, :, 0:4], lg[:, :, 0:NG], top[:, :, 0:1].to_broadcast([P, TT, NG]),
                            ALU.subtract).then_inc(exp_in, 1)
            gi = rt[:, :, 4:5]
            link(V.tensor_copy(gi, topi[:, :, 0:1]))
            group_hot = comb[:, :, 0:NG]
            link(V.tensor_tensor(group_hot, iota[:, 0:NG].unsqueeze(1).to_broadcast([P, TT, NG]),
                                 gi.to_broadcast([P, TT, NG]), ALU.is_equal))
            masked = sel[:, :, 0, :].rearrange("p t (e g) -> p t e g", g=NG)
            link(V.tensor_tensor(masked, lg[:, :, NG:].rearrange("p t (g e) -> p t e g", g=NG),
                                 group_hot.unsqueeze(2).to_broadcast([P, TT, NE, NG]), ALU.mult))
            esel = rank[:, :, 0:NE]
            link(V.tensor_reduce(esel, masked, AX.X, ALU.add))
            for t in range(TT):
                link(V.max(etop[:, t, :], esel[:, t, :]))
                link(V.max_index(etopi[:, t, :], etop[:, t, :], esel[:, t, :]))
            V.tensor_tensor(rt[:, :, 5:6], etop[:, :, 1:2], etop[:, :, 0:1], ALU.subtract).then_inc(exp_in, 1)
            link(V.tensor_copy(rt[:, :, 8:10], etopi[:, :, 0:2]))
            link(V.scalar_tensor_tensor(rt[:, :, 8:10], gi.to_broadcast([P, TT, 2]), float(NE), rt[:, :, 8:10],
                                        ALU.mult, ALU.add))
            io = iota[:, 0:EXP].unsqueeze(1).to_broadcast([P, TT, EXP])
            for i in range(2):
                link(V.tensor_tensor(sel[:, :, i, :], io, rt[:, :, 8 + i:9 + i].to_broadcast([P, TT, EXP]), ALU.is_equal))
            V.tensor_tensor(sel[:, :, 2, :], sel[:, :, 0, :], sel[:, :, 1, :], ALU.add).then_inc(sel_ready, 1)
            dve.wait_ge(exp_done, 2)
            link(V.tensor_reduce(rt[:, :, 10:11], rt[:, :, 0:4], AX.X, ALU.add))
            link(V.tensor_scalar(rt[:, :, 11:12], rt[:, :, 6:7], 1.0, None, ALU.add))
            link(V.tensor_tensor(rt[:, :, 10:11], rt[:, :, 10:11], rt[:, :, 11:12], ALU.mult))
            link(V.reciprocal(rt[:, :, 12:13], rt[:, :, 10:11]))
            link(V.tensor_tensor(rt[:, :, 13:14], rt[:, :, 12:13], rt[:, :, 6:7], ALU.mult))
            dve.wait_ge(sel_ready, 1)
            for i in range(2):
                link(V.tensor_tensor(sel[:, :, i, :], sel[:, :, i, :], rt[:, :, 12 + i:13 + i].to_broadcast([P, TT, EXP]),
                                     ALU.mult))
            link(V.tensor_tensor(comb[:, :, :], sel[:, :, 0, :], sel[:, :, 1, :], ALU.add))
            dve.wait_ge(rank_done, 1)
            link(V.scalar_tensor_tensor(rank[:, :, :], ps[:, 2, 0:2 * EXP].rearrange("p (t e) -> p t e", t=TT), 1.0,
                                        sel[:, :, 2, :], ALU.add, ALU.mult))
            link(V.tensor_scalar(rank[:, :, :], rank[:, :, :], 1.0, None, ALU.subtract))
            V.tensor_copy(counts, ps[:, 2, 2 * EXP:3 * EXP]).then_inc(counts_ready, 1)
            dve.wait_ge(counts_ready, 1)

            JOB_STEPS = 4

            def job(j, e0, first_rank):
                c = [0]

                def step(ins):
                    c[0] += 1
                    ins.then_inc(job_order, 1)
                    dve.wait_ge(job_order, j * JOB_STEPS + c[0])

                ranks = rankc.rearrange("p t e -> p (t e)")
                if first_rank is None:
                    step(V.tensor_copy(rankc[:, :, :], rank[:, :, bass.ds(e0, BE)]))
                else:
                    step(V.tensor_scalar(rankc[:, :, :], rank[:, :, bass.ds(e0, BE)], first_rank, None, ALU.subtract))
                each = [P, TT * BE, SLOTS]
                step(V.tensor_tensor(onehot, iota[:, 0:SLOTS].unsqueeze(1).to_broadcast(each),
                                     ranks.unsqueeze(2).to_broadcast(each), ALU.is_equal))
                V.tensor_tensor(pick, onehot.rearrange("p (t e) s -> p t (e s)", t=TT),
                                rstd[:, 0:2].unsqueeze(2).to_broadcast([P, TT, BE * SLOTS]), ALU.mult).then_inc(picks_ready, 1)
                step(V.tensor_copy(rankc[:, :, :], comb[:, :, bass.ds(e0, BE)]))
                V.tensor_tensor(wpick.rearrange("p t (e s) -> p (t e) s", e=BE), onehot,
                                ranks.unsqueeze(2).to_broadcast(each), ALU.mult).then_inc(wpicks_ready, 1)
                for pr in range(2):
                    for k in range(0, KD, 2):
                        dve.wait_ge(gathered, j * 2 * KD + pr * KD + k + 1)
                        V.tensor_scalar(xT[:, k, pr * P:(pr + 1) * P], ps[:, 4, 0:P], mod[:, 4, k:k + 1],
                                        mod[:, 3, k:k + 1], ALU.mult, ALU.add).then_inc(tok_even, 1)
                    if pr == 0:
                        dve.wait_ge(picks_turned, j + 1)
                        step(V.tensor_copy(wpickT[:, 0, :], ps[:, 6, 0:T]))
                        V.tensor_copy(wpickT[:, 1, :], ps[:, 7, 0:T]).then_inc(scatter_ready, 1)
                    dve.wait_ge(up_done, j * 2 + pr + 1)
                    dve.wait_ge(gate_silu, j * 2 + pr + 1)
                    V.tensor_tensor(hid, silu, ps[:, 1, :], ALU.mult).then_inc(hidden_ready, 1)
                    for n in range(5):
                        if n < 4:
                            if n == 0 and pr == 0:
                                dve.wait_ge(gate2_landed, 16)
                                dve.wait_ge(acc_ready, TT)
                            dve.wait_ge(down_done, j * 8 + pr * 4 + n + 1)
                            V.tensor_tensor(yexp[:, n, :], ps[:, 2 + n % 2, :], gate2[:, n * N:(n + 1) * N],
                                            ALU.mult).then_inc(down_stored, 1)
                        if n:
                            for t in range(TT):
                                m = 2 * (n - 1) + t
                                cc = slice((n - 1) * N, n * N)
                                dve.wait_ge(combined, j * 16 + pr * 8 + m + 1)
                                V.tensor_tensor(acc[:, t, cc], acc[:, t, cc], ps[:, 6 + t, :], ALU.add).then_inc(added, 1)
                                dve.wait_ge(added, j * 16 + pr * 8 + m + 1)
                assert c[0] == JOB_STEPS

            with dve.Fori(0, NB) as j:
                job(j, j * BE, None)
            dve.wait_ge(jobs_ready, 1)
            n_jobs = dve.value_load(jobn[0:1, 0:1], min_val=NB, max_val=JOBS)
            with dve.If(n_jobs > NB):
                with dve.Fori(NB, n_jobs) as j:
                    e0 = dve.value_load(jobi[0:1, bass.ds(j, 1)], min_val=0, max_val=EXP - BE)
                    job(j, e0, jobtab[:, 1, bass.ds(j, 1)])
            dve.wait_ge(gain_landed, 16)
            dve.wait_ge(fin_sq, n_jobs * 8)
            link(V.tensor_reduce(rstd[:, 0:2], ss[:, :].rearrange("p (t c) -> p t c", t=TT), AX.X, ALU.add))
            V.tensor_scalar(rstd[:, 0:2], rstd[:, 0:2], 1.0 / D, EPS, ALU.mult, ALU.add).then_inc(fin_var, 1)
            dve.wait_ge(fin_root, 1)
            link(V.reciprocal(rstd[:, 0:2], rstd[:, 2:4]))
            for t in range(TT):
                for h in range(2):
                    cc = slice(h * D // 2, (h + 1) * D // 2)
                    V.scalar_tensor_tensor(acc[:, t, cc], acc[:, t, cc], rstd[:, t:t + 1], fgain[:, cc], ALU.mult,
                                           ALU.mult).then_inc(fin_out, 1)


NAMES = ["x", "c", "w_ada", "b_ada", "norm1_g", "w_in", "conv_w", "conv_b", "conv_ln_g", "conv_ln_b", "ssm_a_re",
         "ssm_a_im", "ssm_b_re", "ssm_b_im", "ssm_c_re", "ssm_c_im", "ssm_d", "ssm_log_dt", "out_norm_conv_g",
         "out_norm_ssm_g", "w_out", "norm2_g", "router_group_w", "router_group_b", "router_expert_w",
         "router_expert_b", "exp_w_gate", "exp_w_up", "exp_w_down", "final_norm_g"]


def kernel(**inputs):
    import numpy as np
    import concourse.bacc as bacc
    from concourse.bass_utils import run_bass_kernel_spmd

    nc = bacc.Bacc("TRN2", target_bir_lowering=False, num_devices=1, dynamic_dma_scratch_size=1024)
    arrays, aps = {}, {}
    for name in NAMES:
        arr = np.ascontiguousarray(inputs[name])
        arrays[f"in_{name}"] = arr
        aps[name] = nc.dram_tensor(f"in_{name}", arr.shape, mybir.dt.from_np(arr.dtype), kind="ExternalInput").ap()
    out = nc.dram_tensor("out_x", [1, T, D], F32, kind="ExternalOutput").ap()
    trunk(nc, aps, out)
    got = run_bass_kernel_spmd(nc, [arrays], core_ids=[0])
    return got.results[0]["out_x"]
```
